# Optimizing a Trainium2 kernel written in Bass

```python
import jax, jax.numpy as jnp
from jax import lax
import numpy as np

D_MODEL = 1024
BATCH = 1
SEQ = 2048
DEPTH = 1
DEC_BATCH = 8
DEC_SEQ = 8
PAST_LEN = 4096
PAGE_SIZE = 128

MIX_WIDTH = D_MODEL
ATT_HEADS = 8
ATT_KV_HEADS = 2
ATT_HEAD_DIM = 64
ATT_GROUP = ATT_HEADS // ATT_KV_HEADS
WINDOW = 128
ATT_BLOCK = WINDOW
ATT_SCALE = ATT_HEAD_DIM ** -0.5
ML_HEADS = 4
ML_V_DIM = 128
ML_QK_DIM = 64
ML_CHUNK = 64
ML_SCALE = ML_QK_DIM ** -0.5
D_FF = 2816
CONV_W = 3
EPS = 1e-6

ATT_Q_W = ATT_HEADS * ATT_HEAD_DIM
ATT_KV_W = ATT_KV_HEADS * ATT_HEAD_DIM
ML_QK_W = ML_HEADS * ML_QK_DIM
ML_V_W = ML_HEADS * ML_V_DIM
IN_WIDTH = ATT_Q_W + 2 * ATT_KV_W + 2 * ML_QK_W + 2 * ML_V_W + 2 * ML_HEADS

kernel_name = "hymba_swa_sink_mlstm_convffn_step"

def rms_norm(x, w):
    xf = x.astype(jnp.float32)
    y = xf * lax.rsqrt(jnp.mean(xf * xf, axis=-1, keepdims=True) + EPS)
    return (y * w.astype(jnp.float32)).astype(x.dtype)

def split_projection(z):
    sizes = (ATT_Q_W, ATT_KV_W, ATT_KV_W, ML_QK_W, ML_QK_W, ML_V_W, ML_V_W, 2 * ML_HEADS)
    offsets = [int(o) for o in np.cumsum(sizes)[:-1]]
    return jnp.split(z, offsets, axis=-1)

def sink_softmax(s, mask, sinks):
    sink = sinks.astype(jnp.float32).reshape(ATT_KV_HEADS, ATT_GROUP, 1, 1)
    s = jnp.where(mask, s, -jnp.inf)
    m = jnp.maximum(jnp.max(s, axis=-1, keepdims=True), sink)
    e = jnp.exp(s - m)
    return e / (jnp.sum(e, axis=-1, keepdims=True) + jnp.exp(sink - m))

def swa_prompt(q, k, v, sinks):
    B, S = q.shape[:2]
    nb = S // ATT_BLOCK
    qb = q.reshape(B, nb, ATT_BLOCK, ATT_KV_HEADS, ATT_GROUP, ATT_HEAD_DIM)
    kb = k.reshape(B, nb, ATT_BLOCK, ATT_KV_HEADS, ATT_HEAD_DIM)
    vb = v.reshape(B, nb, ATT_BLOCK, ATT_KV_HEADS, ATT_HEAD_DIM)
    pad = ((0, 0), (1, 0), (0, 0), (0, 0), (0, 0))
    kk = jnp.concatenate([jnp.pad(kb, pad)[:, :-1], kb], axis=2)
    vv = jnp.concatenate([jnp.pad(vb, pad)[:, :-1], vb], axis=2)
    s = jnp.einsum('bnqkgd,bnskd->bnkgqs', qb, kk).astype(jnp.float32) * ATT_SCALE
    qi = jnp.arange(ATT_BLOCK)[:, None]
    kj = jnp.arange(2 * ATT_BLOCK)[None, :]
    diff = qi + ATT_BLOCK - kj
    blk = jnp.arange(nb)[:, None, None]
    valid_key = (blk * ATT_BLOCK - ATT_BLOCK + kj[None]) >= 0
    mask = (diff >= 0)[None] & (diff < WINDOW)[None] & valid_key
    p = sink_softmax(s, mask[None, :, None, None], sinks)
    o = jnp.einsum('bnkgqs,bnskd->bnqkgd', p.astype(vv.dtype), vv)
    return o.reshape(B, S, ATT_Q_W)

def swa_sample(q, k, v, cache_k, cache_v, sinks):
    B, T = q.shape[:2]
    keys = jnp.concatenate([cache_k.astype(k.dtype), k], axis=1)
    vals = jnp.concatenate([cache_v.astype(v.dtype), v], axis=1)
    qg = q.reshape(B, T, ATT_KV_HEADS, ATT_GROUP, ATT_HEAD_DIM)
    s = jnp.einsum('btkgd,bskd->bkgts', qg, keys).astype(jnp.float32) * ATT_SCALE
    i = jnp.arange(T)[:, None]
    j = jnp.arange(WINDOW + T)[None, :]
    diff = i + WINDOW - j
    mask = (diff >= 0) & (diff < WINDOW)
    p = sink_softmax(s, mask, sinks)
    o = jnp.einsum('bkgts,bskd->btkgd', p.astype(vals.dtype), vals).reshape(B, T, ATT_Q_W)
    return o, keys[:, -WINDOW:], vals[:, -WINDOW:]

def mlstm_chunk(carry, inp):
    C, n, m = carry
    q, k, v, ig, lf = inp
    L = q.shape[2]
    b = jnp.cumsum(lf, axis=-1)
    tril = jnp.arange(L)[:, None] >= jnp.arange(L)[None, :]
    D = jnp.where(tril, b[..., :, None] - b[..., None, :] + ig[..., None, :], -jnp.inf)
    inter = b + m[..., None]
    m_row = jnp.maximum(inter, jnp.max(D, axis=-1))
    w_inter = jnp.exp(inter - m_row)
    qk = jnp.einsum('bhtd,bhsd->bhts', q, k) * jnp.exp(D - m_row[..., None])
    num = jnp.einsum('bhts,bhsv->bhtv', qk, v) + w_inter[..., None] * jnp.einsum('bhvd,bhtd->bhtv', C, q)
    den = jnp.sum(qk, axis=-1) + w_inter * jnp.einsum('bhd,bhtd->bht', n, q)
    h = num / jnp.maximum(jnp.abs(den), jnp.exp(-m_row))[..., None]
    bL = b[..., -1]
    a = bL[..., None] - b + ig
    m_new = jnp.maximum(bL + m, jnp.max(a, axis=-1))
    sc = jnp.exp(bL + m - m_new)
    ws = jnp.exp(a - m_new[..., None])
    C_new = sc[..., None, None] * C + jnp.einsum('bhs,bhsv,bhsd->bhvd', ws, v, k)
    n_new = sc[..., None] * n + jnp.einsum('bhs,bhsd->bhd', ws, k)
    return (C_new, n_new, m_new), h

def mlstm(q, k, v, ig, lf, C0, n0, m0, chunk):
    B, T = q.shape[:2]
    nc = T // chunk

    def to_chunks(a):
        a = a.astype(jnp.float32).reshape((B, nc, chunk) + a.shape[2:])
        return jnp.moveaxis(a, (1, 2), (0, 3))

    xs = (to_chunks(q), to_chunks(k), to_chunks(v), to_chunks(ig), to_chunks(lf))
    carry0 = (C0.astype(jnp.float32), n0.astype(jnp.float32), m0.astype(jnp.float32))
    (C, n, m), h = lax.scan(mlstm_chunk, carry0, xs)
    h = jnp.moveaxis(h, (0, 3), (1, 2)).reshape(B, T, ML_HEADS, ML_V_DIM)
    return h, C, n, m

def layer(x, cache_k, cache_v, C0, n0, m0, conv_buf,
          norm_mix_w, w_in, b_gates, q_norm_w, k_norm_w, sinks, ml_norm_w, w_out,
          norm_ffn_w, w_ffn_in, conv_w, conv_b, w_down):
    prompt = cache_k is None
    B, T, _ = x.shape
    h = rms_norm(x, norm_mix_w)
    q_a, k_a, v_a, q_m, k_m, v_m, o_m, gl = split_projection(h @ w_in)
    q_a = rms_norm(q_a.reshape(B, T, ATT_HEADS, ATT_HEAD_DIM), q_norm_w)
    k_a = rms_norm(k_a.reshape(B, T, ATT_KV_HEADS, ATT_HEAD_DIM), k_norm_w)
    v_a = v_a.reshape(B, T, ATT_KV_HEADS, ATT_HEAD_DIM)
    if prompt:
        o_att = swa_prompt(q_a, k_a, v_a, sinks)
        new_k, new_v = k_a[:, -WINDOW:], v_a[:, -WINDOW:]
    else:
        o_att, new_k, new_v = swa_sample(q_a, k_a, v_a, cache_k, cache_v, sinks)
    q_m = q_m.reshape(B, T, ML_HEADS, ML_QK_DIM) * ML_SCALE
    k_m = k_m.reshape(B, T, ML_HEADS, ML_QK_DIM)
    v_m = v_m.reshape(B, T, ML_HEADS, ML_V_DIM)
    gl = gl.astype(jnp.float32) + b_gates.astype(jnp.float32)
    ig = gl[..., :ML_HEADS]
    lf = jax.nn.log_sigmoid(gl[..., ML_HEADS:])
    if prompt:
        C0 = jnp.zeros((B, ML_HEADS, ML_V_DIM, ML_QK_DIM), jnp.float32)
        n0 = jnp.zeros((B, ML_HEADS, ML_QK_DIM), jnp.float32)
        m0 = jnp.zeros((B, ML_HEADS), jnp.float32)
        chunk = ML_CHUNK
    else:
        chunk = T
    h_m, C, n, m = mlstm(q_m, k_m, v_m, ig, lf, C0, n0, m0, chunk)
    h_m = rms_norm(h_m, ml_norm_w.reshape(ML_HEADS, ML_V_DIM)).reshape(B, T, ML_V_W)
    o_ml = (h_m * jax.nn.sigmoid(o_m.astype(jnp.float32))).astype(x.dtype)
    x = x + jnp.concatenate([o_att, o_ml], axis=-1) @ w_out
    h2 = rms_norm(x, norm_ffn_w)
    g, u = jnp.split(h2 @ w_ffn_in, 2, axis=-1)
    if prompt:
        conv_buf = jnp.zeros((B, CONV_W - 1, D_FF), x.dtype)
    gp = jnp.concatenate([conv_buf.astype(g.dtype), g], axis=1)
    gc = conv_b + gp[:, 0:T] * conv_w[0] + gp[:, 1:T + 1] * conv_w[1] + gp[:, 2:T + 2] * conv_w[2]
    x = x + (jax.nn.silu(gc) * u) @ w_down
    new_conv = gp[:, -(CONV_W - 1):]
    dt = x.dtype
    return x, new_k, new_v, C.astype(dt), n.astype(dt), m.astype(dt), new_conv

def setup_inputs(seed: int = 0) -> dict:
    key = jax.random.key(seed)
    ks = jax.random.split(key, 24)
    f32 = jnp.float32
    nrm = lambda k, shape, s: jax.random.normal(k, shape, f32) * s
    b_gates = jnp.concatenate([
        nrm(ks[11], (DEPTH, ML_HEADS), 0.1),
        3.0 + nrm(ks[12], (DEPTH, ML_HEADS), 0.5)], axis=-1)
    return {
        "x_prompt": nrm(ks[0], (BATCH, SEQ, D_MODEL), 1.0),
        "x_sample": nrm(ks[1], (DEC_BATCH, DEC_SEQ, D_MODEL), 1.0),
        "cache_attn_k": nrm(ks[2], (DEPTH, DEC_BATCH, WINDOW, ATT_KV_HEADS, ATT_HEAD_DIM), 1.0),
        "cache_attn_v": nrm(ks[3], (DEPTH, DEC_BATCH, WINDOW, ATT_KV_HEADS, ATT_HEAD_DIM), 1.0),
        "state_mlstm_C": nrm(ks[4], (DEPTH, DEC_BATCH, ML_HEADS, ML_V_DIM, ML_QK_DIM), 0.1),
        "state_mlstm_n": nrm(ks[5], (DEPTH, DEC_BATCH, ML_HEADS, ML_QK_DIM), 0.1),
        "state_mlstm_m": nrm(ks[6], (DEPTH, DEC_BATCH, ML_HEADS), 1.0),
        "cache_ffn_conv": nrm(ks[7], (DEPTH, DEC_BATCH, CONV_W - 1, D_FF), 1.0),
        "norm_mix_w": 1.0 + nrm(ks[8], (DEPTH, D_MODEL), 0.02),
        "w_in": nrm(ks[9], (DEPTH, D_MODEL, IN_WIDTH), D_MODEL ** -0.5),
        "b_gates": b_gates,
        "q_norm_w": 1.0 + nrm(ks[13], (DEPTH, ATT_HEAD_DIM), 0.02),
        "k_norm_w": 1.0 + nrm(ks[14], (DEPTH, ATT_HEAD_DIM), 0.02),
        "sinks": nrm(ks[15], (DEPTH, ATT_HEADS), 0.5),
        "ml_norm_w": 1.0 + nrm(ks[16], (DEPTH, ML_V_W), 0.02),
        "w_out": nrm(ks[17], (DEPTH, MIX_WIDTH, D_MODEL), MIX_WIDTH ** -0.5),
        "norm_ffn_w": 1.0 + nrm(ks[18], (DEPTH, D_MODEL), 0.02),
        "w_ffn_in": nrm(ks[19], (DEPTH, D_MODEL, 2 * D_FF), D_MODEL ** -0.5),
        "conv_w": nrm(ks[20], (DEPTH, CONV_W, D_FF), CONV_W ** -0.5),
        "conv_b": nrm(ks[21], (DEPTH, D_FF), 0.02),
        "w_down": nrm(ks[22], (DEPTH, D_FF, D_MODEL), D_FF ** -0.5),
    }

def reference(x_prompt, x_sample, cache_attn_k, cache_attn_v, state_mlstm_C, state_mlstm_n,
              state_mlstm_m, cache_ffn_conv, norm_mix_w, w_in, b_gates, q_norm_w, k_norm_w,
              sinks, ml_norm_w, w_out, norm_ffn_w, w_ffn_in, conv_w, conv_b, w_down):
    yp, ys = x_prompt, x_sample
    sp = [[] for _ in range(6)]
    ss = [[] for _ in range(6)]
    for l in range(DEPTH):
        wl = (norm_mix_w[l], w_in[l], b_gates[l], q_norm_w[l], k_norm_w[l], sinks[l], ml_norm_w[l],
              w_out[l], norm_ffn_w[l], w_ffn_in[l], conv_w[l], conv_b[l], w_down[l])
        yp, *st_p = layer(yp, None, None, None, None, None, None, *wl)
        ys, *st_s = layer(ys, cache_attn_k[l], cache_attn_v[l], state_mlstm_C[l], state_mlstm_n[l],
                          state_mlstm_m[l], cache_ffn_conv[l], *wl)
        for i in range(6):
            sp[i].append(st_p[i])
            ss[i].append(st_s[i])
    k_p, v_p, C_p, n_p, m_p, conv_p = [jnp.stack(a) for a in sp]
    k_s, v_s, C_s, n_s, m_s, conv_s = [jnp.stack(a) for a in ss]
    return (yp, ys, k_p, v_p, C_p, n_p, m_p, conv_p, k_s, v_s, C_s, n_s, m_s, conv_s)


_drawn_inputs = setup_inputs


def setup_inputs(seed=0):
    import zlib

    import numpy as np

    out = dict(_drawn_inputs(seed))
    spreads = {}
    factors = {'q_norm_w': 8.0,
     'k_norm_w': 2.9,
     'sinks': 64.0,
     'ml_norm_w': 6.984,
     'norm_ffn_w': 2.904,
     'conv_b': 5.636}
    for name, (base, spread) in spreads.items():
        noise = np.random.default_rng([zlib.crc32(name.encode()), seed]).standard_normal(out[name].shape)
        drawn = base * np.exp(spread * noise) if base else spread * noise
        out[name] = __import__('jax').numpy.asarray(drawn.astype(out[name].dtype))
    for name, factor in factors.items():
        out[name] = (out[name] * factor).astype(out[name].dtype)
    return out
```

```python
from contextlib import ExitStack

import concourse.bass as bass
from concourse import mybir

F32 = mybir.dt.float32
F32R = mybir.dt.float32r
ALU = mybir.AluOpType
ACT = mybir.ActivationFunctionType
AX = mybir.AxisListType.X

P = 128
D = 1024
KC = D // P
SEQ = 2048
NT = SEQ // P
SB, ST = 8, 8
NS = SB * ST
HQ, HKV, HD = 8, 2, 64
GQ = HQ // HKV
WIN = 128
MH, MQK, MV = 4, 64, 128
MVE = MV + 1
FF = 2816
FC = FF // P
CW = 3
EPS = 1e-6
ATT_SCALE = HD ** -0.5
ML_SCALE = MQK ** -0.5
NEG = -1.0e30
ATT_W = HQ * HD + 2 * HKV * HD
QW = HQ * HD
KVW = HKV * HD
MLQ = MH * MQK
MLV = MH * MV
ML_W = 2 * MH + 2 * MLQ + 2 * MLV
IN_W = ATT_W + ML_W


class Tile:

    def __init__(self, i, c):
        self.i, self.c, self.p = i, c, c % 2

    @property
    def n(self):
        return 2 * self.i + self.c

    @property
    def h(self):
        return self.i + self.c // 2

    def __add__(self, k):
        return Tile(self.i, self.c + k)

    def __sub__(self, k):
        return Tile(self.i, self.c - k)


def wait(eng, sem, value):
    if isinstance(value, int) and value <= 0:
        return
    eng.wait_ge(sem, value)


class Steps:

    def __init__(self, sem, per=1):
        self.sem, self.per = sem, per

    def mark(self, ins):
        ins.then_inc(self.sem, 1)

    def wait(self, eng, tile, step=None):
        step = self.per - 1 if step is None else step
        wait(eng, self.sem, self.per * tile.n + step + 1)


class Landed:

    def __init__(self, sems, per=1):
        self.sems, self.per = sems, per

    def mark(self, dma, tile):
        dma.then_inc(self.sems[tile.p], 16)

    def wait(self, eng, tile):
        wait(eng, self.sems[tile.p], 16 * self.per * (tile.h + 1))


def mm3(nc, out, a_hi, a_lo, b_hi, b_lo, first, last):
    nc.tensor.matmul(out, a_hi, b_hi, start=first, stop=False)
    nc.tensor.matmul(out, a_hi, b_lo, start=False, stop=False)
    return nc.tensor.matmul(out, a_lo, b_hi, start=False, stop=last)


class Stage:

    def __init__(self, nc, ctx, tag):
        self.nc, self.ctx, self.tag, self.sems = nc, ctx, tag, []
        ctx.callback(self.clear)

    def clear(self):
        self.nc.clear_and_free_semaphores(self.sems)
        self.nc.all_engine_barrier()

    def sb(self, name, shape, dt=F32):
        return self.ctx.enter_context(self.nc.sbuf_tensor(f"{self.tag}_{name}", shape, dt))

    def sem(self, name):
        self.sems.append(self.nc.alloc_semaphore(name=f"{self.tag}_{name}"))
        return self.sems[-1]

    def steps(self, name, per=1):
        return Steps(self.sem(name), per)

    def landed(self, name, per=1):
        return Landed([self.sem(f"{name}0"), self.sem(f"{name}1")], per)

    def banks(self):
        return [self.ctx.enter_context(self.nc.psum_tensor(f"{self.tag}_bank{b}", [P, 512], F32)) for b in range(8)]


def tiles_loop(eng, step, first, last):
    for t in range(first, 2):
        step(Tile(0, t))
    with eng.Fori(1, 7) as i:
        for c in range(2):
            step(Tile(i, c))
    for t in range(14, last):
        step(Tile(0, t))


def load_split_weight(k, nc, block_sems, spans, w_hi, w_lo, stage, width):
    landed, rounded, split = block_sems

    def sync(sp):
        for n, (src, _) in enumerate(spans):
            wait(sp, split, n - 1)
            sp.dma_start(stage[:, n % 2, 0:width[n]], src).then_inc(landed[n % 2], 16)

    def scalar(act):
        for n, (_, at) in enumerate(spans):
            act.wait_ge(landed[n % 2], 16 * (n // 2 + 1))
            nc.scalar.activation(w_hi[:, at:at + width[n]], stage[:, n % 2, 0:width[n]], ACT.Copy).then_inc(rounded, 1)

    def vector(dve):
        for n, (_, at) in enumerate(spans):
            dve.wait_ge(rounded, n + 1)
            nc.vector.tensor_tensor(w_lo[:, at:at + width[n]], stage[:, n % 2, 0:width[n]],
                                    w_hi[:, at:at + width[n]].bitcast(F32), ALU.subtract).then_inc(split, 1)

    return sync, scalar, vector


def constants(nc, C, ins):
    with ExitStack() as ctx:
        k = Stage(nc, ctx, "const")
        built, landed = k.sem("built"), k.sem("landed")
        block = ctx.enter_context(nc.Block())

        @block.sync
        def _(sp):
            n = 0
            for dst, src in (
                (C["norm_mix"], ins["norm_mix_w"][0:1, :].partition_broadcast(P)),
                (C["ml_norm"], ins["ml_norm_w"][0:1, :].partition_broadcast(P)),
                (C["q_norm"], ins["q_norm_w"][0:1, :].partition_broadcast(P)),
                (C["k_norm"], ins["k_norm_w"][0:1, :].partition_broadcast(P)),
                (C["sinks"], ins["sinks"][0:1, :].partition_broadcast(P)),
            ):
                sp.dma_start(dst[:, :], src).then_inc(landed, 16)
                n += 16
            with nc.allow_non_contiguous_dma(reason="a few gate biases and sinks"):
                for g, dst in enumerate((C["bias_i"], C["bias_f"])):
                    sp.dma_start(dst[0:MH, :], ins["b_gates"][0, g * MH:(g + 1) * MH].rearrange("(h a) -> h a", a=1)).then_inc(landed, 16)
                    n += 16
                sp.dma_start(C["sink_rows"][0:GQ, :], ins["sinks"][0, :].rearrange("(k j) -> j k", j=GQ)).then_inc(landed, 16)
                n += 16
            sp.wait_ge(landed, n)

        @block.gpsimd
        def _(pool):
            count = [0]

            def done(ins_):
                count[0] += 1
                ins_.then_inc(built, 1)

            def select(out, pattern, base, mult, fill, op=ALU.not_equal, in_=None):
                pool.wait_ge(built, count[0])
                done(nc.gpsimd.affine_select(out=out, in_=out if in_ is None else in_, compare_op=op, fill=fill,
                                             base=base, pattern=pattern, channel_multiplier=mult))

            zeroed = (C["ident"], C["mask"], C["cap"], C["sel_head"], C["sel_t"], C["sel_j"], C["mask_s8"], C["blk"])
            for buf in zeroed:
                done(nc.gpsimd.memset(buf[:], 0.0))
            done(nc.gpsimd.memset(C["ones"][:], 1.0))
            done(nc.gpsimd.memset(C["mhalf"][:], -0.5))
            done(nc.gpsimd.memset(C["cap64"][:], 0.0))
            select(C["ident"][:, :], [[-1, P]], 0, 1, 1.0)
            mask = C["mask"][:, :].rearrange("p (h b s) -> p h b s", h=2, b=2)
            for h in range(2):
                select(mask[:, h, 0, :], [[1, P]], 0, -1, NEG, op=ALU.is_gt)
                select(mask[:, h, 1, :], [[-1, P]], 0, 1, NEG, op=ALU.is_ge)
            select(C["cap"][:, :], [[1, P]], 0, -1, NEG, op=ALU.is_ge)
            cap64 = C["cap64"][:, :].rearrange("p (b t) -> p b t", t=ST)
            select(cap64, [[ST, SB], [1, ST]], 0, -1, NEG, op=ALU.is_ge)
            select(cap64, [[-ST, SB], [0, ST]], 0, 1, NEG, op=ALU.is_ge)
            select(C["sel_head"][:, :].rearrange("k (h p) -> k h p", h=MH), [[-1, MH], [0, P]], 0, 1, 1.0)
            select(C["sel_t"][:, :].rearrange("k (b t) -> k b t", t=ST), [[0, P // ST], [-1, ST]], 0, 1, 1.0)
            select(C["sel_j"][:, :].rearrange("k (a j t) -> k a j t", j=GQ, t=ST), [[0, P // 32], [-1, GQ], [0, ST]], 0, 1, 1.0)
            select(C["mask_s8"][:, :], [[1, WIN + ST]], 0, -1, NEG, op=ALU.is_gt)
            select(C["mask_s8"][:, :], [[-1, WIN + ST]], WIN, 1, NEG, op=ALU.is_ge)
            select(C["blk"][:, :], [[-ST, SB]], 0, 1, 0.0, op=ALU.is_ge, in_=C["ones"][0:NS, 0:SB])
            select(C["blk"][:, :], [[ST, SB]], ST - 1, -1, 0.0, op=ALU.is_ge)
            pool.wait_ge(built, count[0])


def attention(nc, C, ins, outs, h_dram, o_dram):
    with ExitStack() as ctx:
        k = Stage(nc, ctx, "att")
        w_hi = k.sb("w_hi", [P, KC * ATT_W], F32R)
        w_lo = k.sb("w_lo", [P, KC * ATT_W], F32R)
        stage = k.sb("stage", [P, 2, ATT_W])
        x = k.sb("x", [P, 2, D])
        square = k.sb("square", [P, D])
        hn = k.sb("hn", [P, D])
        h_hi = k.sb("h_hi", [P, 2, D], F32R)
        h_lo = k.sb("h_lo", [P, 2, D], F32R)
        z = k.sb("z", [P, 2, ATT_W])
        zz = k.sb("zz", [P, QW + KVW])
        xss = k.sb("xss", [P, 2])
        xvar = k.sb("xvar", [P, 1])
        xr = k.sb("xr", [P, 1])
        qss = k.sb("qss", [P, HQ + HKV])
        qvar = k.sb("qvar", [P, HQ + HKV])
        qr = k.sb("qr", [P, HQ + HKV])
        qu = k.sb("qu", [P, QW + KVW])
        qn = k.sb("qn", [P, QW])
        kn = k.sb("kn", [P, KVW])
        v = k.sb("v", [P, 2, KVW])
        qT = k.sb("qT", [P, QW])
        kT = k.sb("kT", [P, 2, P])
        s = k.sb("s", [P, HQ * 2 * P])
        pT = k.sb("pT", [P, HQ * 2 * P])
        smax = k.sb("smax", [P, HQ])
        m = k.sb("m", [P, HQ])
        neg_m = k.sb("neg_m", [P, HQ])
        sink_m = k.sb("sink_m", [P, HQ])
        esink = k.sb("esink", [P, HQ])
        ssum = k.sb("ssum", [P, HQ])
        den = k.sb("den", [P, HQ])
        rden = k.sb("rden", [P, HQ])
        o = k.sb("o", [P, 2, QW])
        ck = k.sb("ck", [P, SB, KVW])
        cv = k.sb("cv", [P, SB, KVW])
        ckT = k.sb("ckT", [P, SB, WIN + ST])
        vnew = k.sb("vnew", [ST, SB, KVW])
        qTs = k.sb("qTs", [P, SB, GQ * ST])
        mask_s = k.sb("mask_s", [P, WIN + ST])
        sink_s = k.sb("sink_s", [P, HKV])
        ss = k.sb("ss", [P, 4, WIN + ST])
        stat = k.sb("stat", [P, 8, 4])
        psT = k.sb("psT", [P, 4, P])
        psnT = k.sb("psnT", [ST, 4, P])
        os_ = k.sb("os", [P, 4, HD])
        bank = k.banks()

        wl = [k.sem("w_landed0"), k.sem("w_landed1")]
        w_rounded, w_split = k.sem("w_rounded"), k.sem("w_split")
        x_in = k.landed("x_in")
        x_square = k.steps("x_square")
        x_var = k.steps("x_var")
        x_rstd = k.steps("x_rstd")
        x_normed = k.steps("x_normed")
        h_turned = k.steps("h_turned", 2)
        h_rounded = k.steps("h_rounded", 2)
        h_split = k.steps("h_split", 2)
        h_out = k.landed("h_out", 2)
        proj = k.steps("proj", 2)
        z_ready = k.steps("z_ready", 2)
        z_square = k.steps("z_square")
        z_sum = k.steps("z_sum")
        z_var = k.steps("z_var")
        z_rstd = k.steps("z_rstd")
        z_scaled = k.steps("z_scaled")
        qk_normed = k.steps("qk_normed", 2)
        v_kept = k.steps("v_kept")
        qk_turned = k.steps("qk_turned", 2)
        q_kept = k.steps("q_kept")
        k_kept = k.steps("k_kept")
        scored = k.steps("scored", 4)
        masked = k.steps("masked", 4)
        s_stats = k.steps("s_stats", 4)
        s_exp = k.steps("s_exp", 2)
        s_den = k.steps("s_den", 2)
        p_turned = k.steps("p_turned", 4)
        p_kept_a = k.steps("p_kept_a", 2)
        p_kept_v = k.steps("p_kept_v", 2)
        pv = k.steps("pv")
        o_ready = k.steps("o_ready")
        o_out = k.landed("o_out")
        k_out, v_out = k.sem("k_out"), k.sem("v_out")

        spans, widths = [], []
        w_in = ins["w_in"][0]
        for c in range(KC):
            spans.append((w_in[c * P:(c + 1) * P, 0:ATT_W], c * ATT_W))
            widths.append(ATT_W)
        w_sync, w_scalar, w_vector = load_split_weight(k, nc, (wl, w_rounded, w_split), spans, w_hi, w_lo, stage, widths)
        whi = w_hi[:, :].rearrange("p (c n) -> p c n", c=KC)
        wlo = w_lo[:, :].rearrange("p (c n) -> p c n", c=KC)

        def rows(t):
            return NS if t.c == NT else P

        samp = Tile(0, NT)
        s_in, sT_done, s_mask, s_keep, s_score, s_dve, s_act, s_turn, s_pv, s_os = (
            k.sem(n) for n in ("s_in", "s_turned", "s_mask", "s_keep", "s_score", "s_dve", "s_act", "s_turn", "s_pv", "s_os"))
        s_vnew, s_out = k.sem("s_vnew"), k.sem("s_out")

        block = ctx.enter_context(nc.Block())

        @block.sync
        def _(sp):
            def load_x(t):
                x_normed.wait(sp, t - 2)
                if t.c == NT:
                    x_in.mark(sp.dma_start(x[0:NS, t.p, :], ins["x_sample"].rearrange("b t d -> (b t) d")), t)
                else:
                    x_in.mark(sp.dma_start(x[:, t.p, :], ins["x_prompt"][0, bass.ds(t.n * P, P), :]), t)

            def store_h(t):
                h_split.wait(sp, t)
                cols = slice(0, D)
                if t.c == NT:
                    for part, src in ((0, h_hi), (1, h_lo)):
                        h_out.mark(sp.dma_start(h_dram[NT, :, part, :].rearrange("p (c r) -> p c r", c=KC)[:, :, 0:NS],
                                                src[:, t.p, :].bitcast(F32).rearrange("p (c r) -> p c r", c=KC)[:, :, 0:NS]), t)
                    return
                h_out.mark(sp.dma_start(h_dram[bass.ds(t.n, 1), :, 0, :].rearrange("a p n -> (a p) n"), h_hi[:, t.p, cols].bitcast(F32)), t)
                h_out.mark(sp.dma_start(h_dram[bass.ds(t.n, 1), :, 1, :].rearrange("a p n -> (a p) n"), h_lo[:, t.p, cols].bitcast(F32)), t)

            def store_o(t):
                o_ready.wait(sp, t)
                o_out.mark(sp.dma_start(o_dram[bass.ds(t.n * P, P), 0:QW], o[:, t.p, :]), t)

            load_x(Tile(0, 0))
            load_x(Tile(0, 1))
            w_sync(sp)
            sp.dma_start(ck[:, :, :], ins["cache_attn_k"][0].rearrange("b s k d -> s b (k d)")).then_inc(s_in, 16)
            sp.dma_start(cv[:, :, :], ins["cache_attn_v"][0].rearrange("b s k d -> s b (k d)")).then_inc(s_in, 16)
            for b_ in range(SB):
                for cache, out in ((ins["cache_attn_k"], outs["k_sample"]), (ins["cache_attn_v"], outs["v_sample"])):
                    sp.dma_start(out[0, b_, 0:WIN - ST].rearrange("s k d -> s (k d)"),
                                 cache[0, b_, ST:WIN].rearrange("s k d -> s (k d)")).then_inc(s_out, 16)
            store_h(Tile(0, 0))

            def period(t):
                load_x(t + 2) if not (isinstance(t.c, int) and isinstance(t.i, int) and t.c + 2 > NT) else None
                store_h(t + 1)
                if not (isinstance(t.i, int) and t.c < 2):
                    store_o(t - 2)

            tiles_loop(sp, period, 0, NT)
            store_o(Tile(0, NT - 2))
            store_o(Tile(0, NT - 1))
            last = Tile(0, NT - 1)
            v_kept.wait(sp, last)
            sp.dma_start(outs["v_prompt"][0, 0].rearrange("s k d -> s (k d)"), v[:, last.p, :]).then_inc(v_out, 16)
            z_ready.wait(sp, samp)
            vs = z[0:NS, samp.p, QW + KVW:ATT_W]
            for b_ in range(SB):
                rows_b = z[b_ * ST:(b_ + 1) * ST, samp.p, QW + KVW:ATT_W]
                sp.dma_start(vnew[:, b_, :], rows_b).then_inc(s_vnew, 16)
                sp.dma_start(outs["v_sample"][0, b_, WIN - ST:WIN].rearrange("s k d -> s (k d)"), rows_b).then_inc(s_out, 16)
            qk_normed.wait(sp, samp)
            for b_ in range(SB):
                sp.dma_start(outs["k_sample"][0, b_, WIN - ST:WIN].rearrange("s k d -> s (k d)"),
                             kn[b_ * ST:(b_ + 1) * ST, :]).then_inc(s_out, 16)
            sp.wait_ge(s_os, 1)
            for g in range(4):
                kv, bq = g // 2, g % 2
                for b4 in range(4):
                    tok = SEQ + (bq * 4 + b4) * ST
                    for j in range(GQ):
                        sp.dma_start(o_dram[tok:tok + ST, (kv * GQ + j) * HD:(kv * GQ + j + 1) * HD],
                                     os_[b4 * 32 + j * ST:b4 * 32 + (j + 1) * ST, g, :]).then_inc(s_out, 16)
            sp.wait_ge(s_out, 16 * (2 * SB + 2 * SB + 4 * 4 * GQ))
            sp.wait_ge(k_out, 16)
            sp.wait_ge(v_out, 16)
            h_out.wait(sp, samp)
            h_out.wait(sp, samp - 1)
            o_out.wait(sp, last)
            o_out.wait(sp, last - 1)

        @block.tensor
        def _(pe):
            def turn_h(t):
                r = rows(t)
                x_normed.wait(pe, t)
                for b in range(2):
                    if b == 0:
                        q_kept.wait(pe, t - 2)
                    else:
                        k_kept.wait(pe, t - 2)
                        o_ready.wait(pe, t - 3)
                    h_split.wait(pe, t - 1, b)
                    for c in range(4):
                        ins_ = nc.tensor.transpose(bank[2 + b][:, c * P:c * P + r],
                                                   hn[0:r, (b * 4 + c) * P:(b * 4 + c + 1) * P], C["ident"][0:r, 0:r])
                    h_turned.mark(ins_)

            def project(t, g):
                r = rows(t)
                lo, hi = ((0, QW), (QW, ATT_W))[g]
                if g == 0:
                    h_split.wait(pe, t)
                z_ready.wait(pe, t - 1, g)
                for c in range(KC):
                    a = slice(c * P, c * P + r)
                    ins_ = mm3(nc, bank[g][0:r, 0:hi - lo], h_hi[:, t.p, a], h_lo[:, t.p, a],
                               whi[:, c, lo:hi], wlo[:, c, lo:hi], c == 0, c == KC - 1)
                proj.mark(ins_)

            def turn_p(t, first=False):
                for b in range(4):
                    s_exp.wait(pe, t, b // 2)
                    for hh in range(2):
                        h = 2 * b + hh
                        for part in ((1,) if first else (0, 1)):
                            at = hh * 256 + part * P
                            ins_ = nc.tensor.transpose(bank[4 + b][:, at:at + P],
                                                       s[:, h * 256 + part * P:h * 256 + (part + 1) * P], C["ident"][:, :])
                    p_turned.mark(ins_)

            def turn_qk(t):
                r = rows(t)
                qk_normed.wait(pe, t)
                h_split.wait(pe, t + 1, 1)
                for j in range(GQ):
                    ins_ = nc.tensor.transpose(bank[2][:, j * P:j * P + r], qn[0:r, j * P:(j + 1) * P], C["ident"][0:r, 0:r])
                qk_turned.mark(ins_)
                qk_turned.mark(nc.tensor.transpose(bank[3][:, 0:r], kn[0:r, :], C["ident"][0:r, 0:r]))

            def values(t, first=False):
                p_kept_a.wait(pe, t)
                p_kept_v.wait(pe, t)
                v_kept.wait(pe, t)
                k_kept.wait(pe, t + 1)
                for h in range(HQ):
                    kv = h // GQ
                    if not first:
                        nc.tensor.matmul(bank[3][:, h * HD:(h + 1) * HD], pT[:, h * 256:h * 256 + P],
                                         v[:, 1 - t.p, kv * HD:(kv + 1) * HD], start=True, stop=False)
                    ins_ = nc.tensor.matmul(bank[3][:, h * HD:(h + 1) * HD], pT[:, h * 256 + P:(h + 1) * 256],
                                            v[:, t.p, kv * HD:(kv + 1) * HD], start=first, stop=True)
                pv.mark(ins_)

            def scores(t, first=False):
                q_kept.wait(pe, t)
                k_kept.wait(pe, t)
                for b in range(4):
                    if b < 2:
                        p_kept_a.wait(pe, t - 1, b)
                    else:
                        p_kept_v.wait(pe, t - 1, b - 2)
                    for hh in range(2):
                        h = 2 * b + hh
                        half, j = h // GQ, h % GQ
                        part = slice(half * HD, (half + 1) * HD)
                        for pr in ((1,) if first else (0, 1)):
                            keys = kT[part, t.p if pr else 1 - t.p, :]
                            ins_ = nc.tensor.matmul(bank[4 + b][:, hh * 256 + pr * P:hh * 256 + (pr + 1) * P],
                                                    qT[part, j * P:(j + 1) * P], keys, start=True, stop=True)
                    scored.mark(ins_)

            turn_h(Tile(0, 0))
            turn_h(Tile(0, 1))
            pe.wait_ge(w_split, KC)
            project(Tile(0, 0), 0)
            project(Tile(0, 0), 1)

            def period(t):
                static = isinstance(t.i, int)
                project(t + 1, 0)
                if not (static and t.c == 0):
                    turn_p(t - 1, first=static and t.c == 1)
                turn_qk(t)
                project(t + 1, 1)
                if not (static and t.c == 0):
                    values(t - 1, first=static and t.c == 1)
                scores(t, first=static and t.c == 0)
                if not (static and t.c + 2 > NT):
                    turn_h(t + 2)

            tiles_loop(pe, period, 0, NT)
            last = Tile(0, NT - 1)
            turn_p(last)
            qk_normed.wait(pe, samp)
            o_ready.wait(pe, last - 1)
            for j in range(GQ):
                ins_ = nc.tensor.transpose(bank[2][:, j * P:j * P + NS], qn[0:NS, j * P:(j + 1) * P], C["ident"][0:NS, 0:NS])
            qk_turned.mark(ins_)
            qk_turned.mark(nc.tensor.transpose(bank[3][:, 0:NS], kn[0:NS, :], C["ident"][0:NS, 0:NS]))
            values(last)
            pe.wait_ge(s_in, 32)
            for b in range(2):
                z_ready.wait(pe, samp, b)
                for c in range(4):
                    ins_ = nc.tensor.transpose(bank[b][:, c * P:(c + 1) * P], ck[:, b * 4 + c, :], C["ident"][:, :])
                ins_.then_inc(sT_done, 1)
            p_kept_v.wait(pe, last)
            nc.tensor.matmul(bank[7][:, 0:WIN + ST], C["sel_t"][:, :], C["mask_s8"][:, :], start=True, stop=True)
            nc.tensor.matmul(bank[7][:, 256:256 + HKV], C["sel_j"][:, :], C["sink_rows"][:, :], start=True, stop=True).then_inc(s_mask, 1)
            pe.wait_ge(s_keep, 5)
            p_kept_a.wait(pe, last)
            for g in range(4):
                kv, bq = g // 2, g % 2
                part = slice(kv * HD, (kv + 1) * HD)
                for b4 in range(4):
                    ins_ = nc.tensor.matmul(bank[4 + kv][b4 * 32:(b4 + 1) * 32, bq * 256:bq * 256 + WIN + ST],
                                            qTs[part, bq * 4 + b4, :], ckT[part, bq * 4 + b4, :], start=True, stop=True)
            ins_.then_inc(s_score, 1)
            pe.wait_ge(s_act, 6)
            pe.wait_ge(s_keep, 7)
            for g in range(4):
                nc.tensor.transpose(bank[6][:, g * P:(g + 1) * P], ss[:, g, 0:WIN], C["ident"][:, :])
                ins_ = nc.tensor.transpose(bank[7][0:ST, g * P:(g + 1) * P], ss[:, g, WIN:WIN + ST], C["ident"][:, :])
            ins_.then_inc(s_turn, 1)
            pe.wait_ge(s_dve, 9)
            pe.wait_ge(s_vnew, 16 * SB)
            o_ready.wait(pe, last)
            for g in range(4):
                kv, bq = g // 2, g % 2
                for b4 in range(4):
                    b_ = bq * 4 + b4
                    out = bank[3][b4 * 32:(b4 + 1) * 32, g * HD:(g + 1) * HD]
                    nc.tensor.matmul(out, psT[:, g, b4 * 32:(b4 + 1) * 32], cv[:, b_, kv * HD:(kv + 1) * HD], start=True, stop=False)
                    ins_ = nc.tensor.matmul(out, psnT[:, g, b4 * 32:(b4 + 1) * 32], vnew[:, b_, kv * HD:(kv + 1) * HD],
                                            start=False, stop=True)
            ins_.then_inc(s_pv, 1)

        @block.scalar
        def _(act):
            def square_x(t):
                r = rows(t)
                x_in.wait(act, t)
                x_var.wait(act, t - 2)
                x_square.wait(act, t - 1)
                x_square.mark(nc.scalar.activation(square[0:r, :], x[0:r, t.p, :], ACT.Square, accum_out=xss[0:r, t.p:t.p + 1]))

            def round_h(t):
                r = rows(t)
                h_out.wait(act, t - 2)
                proj.wait(act, t - 2)
                for b in range(2):
                    h_turned.wait(act, t, b)
                    src = bank[2 + b][:, :].rearrange("p (c r) -> p c r", c=4)[:, :, 0:r]
                    dst = h_hi[:, t.p, b * 512:(b + 1) * 512].rearrange("p (c r) -> p c r", c=4)[:, :, 0:r]
                    h_rounded.mark(nc.scalar.activation(dst, src, ACT.Copy))

            def keep_z(t, g):
                r = rows(t)
                lo, hi = ((0, QW), (QW, ATT_W))[g]
                proj.wait(act, t, g)
                if g == 0:
                    z_scaled.wait(act, t - 2)
                else:
                    v_kept.wait(act, t - 2)
                z_ready.mark(nc.scalar.activation(z[0:r, t.p, lo:hi], bank[g][0:r, 0:hi - lo], ACT.Copy))

            def keep_q(t):
                qk_turned.wait(act, t, 0)
                scored.wait(act, t - 1)
                q_kept.mark(nc.scalar.activation(qT[:, :], bank[2][:, :], ACT.Copy))

            def exps(t):
                s_stats.wait(act, t)
                s_den.wait(act, t - 1)
                for h in range(HQ):
                    ins_ = nc.scalar.activation(s[:, h * 256:(h + 1) * 256], s[:, h * 256:(h + 1) * 256], ACT.Exp,
                                                bias=neg_m[:, h:h + 1], accum_out=ssum[:, h:h + 1])
                    if h == 3:
                        nc.scalar.activation(esink[:, :], sink_m[:, :], ACT.Exp)
                    if h % 4 == 3:
                        s_exp.mark(ins_)

            def keep_p(t, first=False):
                for b in range(2):
                    p_turned.wait(act, t, b)
                    pv.wait(act, t - 1)
                    parts = slice(1, 2) if first else slice(0, 2)
                    dst = pT[:, b * 512:(b + 1) * 512].rearrange("p (h a r) -> p h a r", h=2, a=2)[:, :, parts, :]
                    src = bank[4 + b][:, :].rearrange("p (h a r) -> p h a r", h=2, a=2)[:, :, parts, :]
                    p_kept_a.mark(nc.scalar.activation(dst, src, ACT.Copy))

            square_x(Tile(0, 0))
            square_x(Tile(0, 1))
            round_h(Tile(0, 0))
            round_h(Tile(0, 1))
            w_scalar(act)
            keep_z(Tile(0, 0), 0)
            keep_z(Tile(0, 0), 1)

            def period(t):
                static = isinstance(t.i, int)
                ahead = not (static and t.c + 2 > NT)
                if ahead:
                    square_x(t + 2)
                keep_z(t + 1, 0)
                if not (static and t.c == 0):
                    keep_p(t - 1, first=static and t.c == 1)
                keep_q(t)
                keep_z(t + 1, 1)
                if ahead:
                    round_h(t + 2)
                exps(t)

            tiles_loop(act, period, 0, NT)
            last = Tile(0, NT - 1)
            keep_p(last)
            qk_turned.wait(act, samp, 0)
            src = bank[2][:, :].rearrange("p (j r) -> p j r", j=GQ)[:, :, 0:NS].rearrange("p j (b t) -> p b j t", t=ST)
            for b_ in range(SB):
                ins_ = nc.scalar.activation(qTs[:, b_, :].rearrange("p (j t) -> p j t", j=GQ), src[:, b_], ACT.Copy)
            ins_.then_inc(s_act, 1)
            act.wait_ge(s_dve, 5)
            for g in range(4):
                nc.scalar.activation(ss[:, g, :], ss[:, g, :], ACT.Exp, bias=stat[:, 2, g:g + 1],
                                     accum_out=stat[:, 4, g:g + 1]).then_inc(s_act, 1)
            nc.scalar.activation(stat[:, 5, :], stat[:, 3, :], ACT.Exp).then_inc(s_act, 1)

        @block.vector
        def _(dve):
            def var_x(t):
                r = rows(t)
                x_square.wait(dve, t)
                x_rstd.wait(dve, t - 1)
                x_var.mark(nc.vector.tensor_scalar(xvar[0:r, :], xss[0:r, t.p:t.p + 1], 1.0 / D, EPS, ALU.mult, ALU.add))

            def norm_x(t):
                r = rows(t)
                x_rstd.wait(dve, t)
                h_turned.wait(dve, t - 1)
                x_normed.mark(nc.vector.scalar_tensor_tensor(hn[0:r, :], x[0:r, t.p, :], xr[0:r, 0:1], C["norm_mix"][0:r, :],
                                                             ALU.mult, ALU.mult))

            def split_h(t):
                r = rows(t)
                for b in range(2):
                    h_rounded.wait(dve, t, b)
                    src = bank[2 + b][:, :].rearrange("p (c r) -> p c r", c=4)[:, :, 0:r]
                    hi = h_hi[:, t.p, b * 512:(b + 1) * 512].rearrange("p (c r) -> p c r", c=4)[:, :, 0:r]
                    dst = h_lo[:, t.p, b * 512:(b + 1) * 512].rearrange("p (c r) -> p c r", c=4)[:, :, 0:r]
                    h_split.mark(nc.vector.tensor_tensor(dst, src, hi.bitcast(F32), ALU.subtract))

            def sum_z(t):
                r = rows(t)
                z_square.wait(dve, t)
                z_sum.mark(nc.vector.reduce_sum(qss[0:r, :], zz[0:r, :].rearrange("p (h d) -> p h d", d=HD), axis=AX))

            def var_z(t):
                r = rows(t)
                z_sum.wait(dve, t)
                z_rstd.wait(dve, t - 1)
                z_var.mark(nc.vector.tensor_scalar(qvar[0:r, :], qss[0:r, :], 1.0 / HD, EPS, ALU.mult, ALU.add))

            def scale_z(t):
                r = rows(t)
                z_rstd.wait(dve, t)
                qk_normed.wait(dve, t - 1)
                z_scaled.mark(nc.vector.tensor_tensor(
                    qu[0:r, :].rearrange("p (h d) -> p h d", d=HD),
                    z[0:r, t.p, 0:QW + KVW].rearrange("p (h d) -> p h d", d=HD),
                    qr[0:r, :].unsqueeze(2).broadcast_to([r, HQ + HKV, HD]), ALU.mult))

            def keep_k(t):
                qk_turned.wait(dve, t, 1)
                k_kept.mark(nc.vector.tensor_copy(kT[:, t.p, :], bank[3][:, 0:P]))

            def keep_p(t, first=False):
                for b in range(2, 4):
                    p_turned.wait(dve, t, b)
                    pv.wait(dve, t - 1)
                    parts = slice(1, 2) if first else slice(0, 2)
                    dst = pT[:, b * 512:(b + 1) * 512].rearrange("p (h a r) -> p h a r", h=2, a=2)[:, :, parts, :]
                    src = bank[4 + b][:, :].rearrange("p (h a r) -> p h a r", h=2, a=2)[:, :, parts, :]
                    p_kept_v.mark(nc.vector.tensor_copy(dst, src))

            def keep_o(t):
                pv.wait(dve, t)
                o_out.wait(dve, t - 2)
                s_den.wait(dve, t)
                o_ready.mark(nc.vector.tensor_tensor(
                    o[:, t.p, :].rearrange("p (h d) -> p h d", d=HD), bank[3][:, :].rearrange("p (h d) -> p h d", d=HD),
                    rden[:, :].unsqueeze(2).broadcast_to([P, HQ, HD]), ALU.mult))

            def softmax_stats(t, first=False):
                p_turned.wait(dve, t - 1)
                for b in range(4):
                    scored.wait(dve, t, b)
                    dst, src, msk = s[:, b * 512:(b + 1) * 512], bank[4 + b][:, :], C["mask"][:, :]
                    if first:
                        dst, src, msk = (a.rearrange("p (h a r) -> p h a r", h=2, a=2)[:, :, 1, :] for a in (dst, src, msk))
                    masked.mark(nc.vector.scalar_tensor_tensor(dst, src, ATT_SCALE, msk, ALU.mult, ALU.add))
                masked.wait(dve, t)
                s_stats.mark(nc.vector.reduce_max(smax[:, :], s[:, :].rearrange("p (h r) -> p h r", h=HQ), axis=AX))
                s_stats.wait(dve, t, 0)
                s_stats.mark(nc.vector.tensor_tensor(m[:, :], smax[:, :], C["sinks"][:, :], ALU.max))
                s_stats.wait(dve, t, 1)
                s_stats.mark(nc.vector.tensor_tensor(sink_m[:, :], C["sinks"][:, :], m[:, :], ALU.subtract))
                s_stats.mark(nc.vector.tensor_scalar(neg_m[:, :], m[:, :], -1.0, None, ALU.mult))

            def denominators(t):
                s_exp.wait(dve, t)
                s_den.mark(nc.vector.tensor_tensor(den[:, :], ssum[:, :], esink[:, :], ALU.add))
                s_den.wait(dve, t, 0)
                s_den.mark(nc.vector.reciprocal(rden[:, :], den[:, :]))

            for t0 in range(2):
                var_x(Tile(0, t0))
                norm_x(Tile(0, t0))
            split_h(Tile(0, 0))
            split_h(Tile(0, 1))
            w_vector(dve)
            nc.vector.memset(s[:, :], NEG)
            sum_z(Tile(0, 0))
            var_z(Tile(0, 0))
            scale_z(Tile(0, 0))

            def period(t):
                static = isinstance(t.i, int)
                ahead = not (static and t.c + 2 > NT)
                if ahead:
                    var_x(t + 2)
                if not (static and t.c == 0):
                    keep_p(t - 1, first=static and t.c == 1)
                if ahead:
                    norm_x(t + 2)
                keep_k(t)
                if not (static and t.c == 0):
                    keep_o(t - 1)
                softmax_stats(t, first=static and t.c == 0)
                if ahead:
                    split_h(t + 2)
                sum_z(t + 1)
                var_z(t + 1)
                denominators(t)
                scale_z(t + 1)

            tiles_loop(dve, period, 0, NT)
            last = Tile(0, NT - 1)
            keep_p(last)
            qk_turned.wait(dve, samp, 1)
            k_kept.mark(nc.vector.tensor_copy(ckT[:, :, WIN:WIN + ST], bank[3][:, 0:NS].rearrange("p (b t) -> p b t", t=ST)))
            keep_o(last)
            k_kept.wait(dve, samp)
            dve.wait_ge(s_act, 1)
            nc.vector.memset(stat[:, 0, :], 0.0).then_inc(s_keep, 1)
            nc.vector.memset(stat[:, 1, :], 0.0).then_inc(s_keep, 1)
            nc.vector.memset(stat[:, 6, :], 0.0).then_inc(s_keep, 1)
            for b in range(2):
                dve.wait_ge(sT_done, b + 1)
                nc.vector.tensor_copy(ckT[:, b * 4:(b + 1) * 4, 0:WIN], bank[b][:, :].rearrange("p (b s) -> p b s", b=4)).then_inc(s_keep, 1)
            dve.wait_ge(s_mask, 1)
            nc.vector.tensor_copy(mask_s[:, :], bank[7][:, 0:WIN + ST]).then_inc(s_keep, 1)
            nc.vector.tensor_copy(sink_s[:, :], bank[7][:, 256:256 + HKV]).then_inc(s_keep, 1)
            dve.wait_ge(s_score, 1)
            dve.wait_ge(s_keep, 7)
            for g in range(4):
                src = bank[4 + g // 2][:, (g % 2) * 256:(g % 2) * 256 + WIN + ST]
                ins_ = nc.vector.scalar_tensor_tensor(ss[:, g, :], src, ATT_SCALE, mask_s[:, :], ALU.mult, ALU.add)
            ins_.then_inc(s_dve, 1)
            dve.wait_ge(s_dve, 1)
            nc.vector.reduce_max(stat[:, 0, :], ss[:, :, :], axis=AX).then_inc(s_dve, 1)
            dve.wait_ge(s_dve, 2)
            sink_g = sink_s[:, :].unsqueeze(2).broadcast_to([P, HKV, 2])
            four = lambda a: a.rearrange("p (k b) -> p k b", k=HKV)
            nc.vector.tensor_tensor(four(stat[:, 1, :]), four(stat[:, 0, :]), sink_g, ALU.max).then_inc(s_dve, 1)
            dve.wait_ge(s_dve, 3)
            nc.vector.tensor_scalar(stat[:, 2, :], stat[:, 1, :], -1.0, None, ALU.mult).then_inc(s_dve, 1)
            nc.vector.tensor_tensor(four(stat[:, 3, :]), sink_g, four(stat[:, 1, :]), ALU.subtract).then_inc(s_dve, 1)
            dve.wait_ge(s_act, 6)
            nc.vector.tensor_tensor(stat[:, 6, :], stat[:, 4, :], stat[:, 5, :], ALU.add).then_inc(s_dve, 1)
            dve.wait_ge(s_dve, 6)
            nc.vector.reciprocal(stat[:, 7, :], stat[:, 6, :]).then_inc(s_dve, 1)
            dve.wait_ge(s_turn, 1)
            nc.vector.tensor_copy(psT[:, :, :], bank[6][:, :].rearrange("p (g r) -> p g r", g=4)).then_inc(s_dve, 1)
            nc.vector.tensor_copy(psnT[:, :, :], bank[7][0:ST, :].rearrange("p (g r) -> p g r", g=4)).then_inc(s_dve, 1)
            dve.wait_ge(s_pv, 1)
            dve.wait_ge(s_dve, 9)
            nc.vector.tensor_tensor(os_[:, :, :], bank[3][:, 0:4 * HD].rearrange("p (g d) -> p g d", g=4),
                                    stat[:, 7, :].unsqueeze(2).broadcast_to([P, 4, HD]), ALU.mult).then_inc(s_os, 1)

        @block.gpsimd
        def _(pool):
            def rstd_x(t):
                r = rows(t)
                x_normed.wait(pool, t - 1)
                x_var.wait(pool, t)
                x_rstd.mark(nc.gpsimd.tensor_tensor(xr[0:r, :], xvar[0:r, :], C["mhalf"][0:r, 0:1], ALU.pow))

            def keep_v(t):
                r = rows(t)
                z_ready.wait(pool, t, 1)
                pv.wait(pool, t - 1)
                v_kept.mark(nc.gpsimd.tensor_tensor(v[0:r, t.p, :], z[0:r, t.p, QW + KVW:ATT_W], C["ones"][0:r, 0:KVW], ALU.mult))

            def square_z(t):
                r = rows(t)
                z_ready.wait(pool, t, 1)
                z_sum.wait(pool, t - 1)
                zt = z[0:r, t.p, 0:QW + KVW]
                z_square.mark(nc.gpsimd.tensor_tensor(zz[0:r, :], zt, zt, ALU.mult))

            def rstd_z(t):
                r = rows(t)
                z_scaled.wait(pool, t - 1)
                z_var.wait(pool, t)
                z_rstd.mark(nc.gpsimd.tensor_tensor(qr[0:r, :], qvar[0:r, :], C["mhalf"][0:r, :], ALU.pow))

            def weigh_qk(t):
                r = rows(t)
                z_scaled.wait(pool, t)
                qk_turned.wait(pool, t - 1)
                qk_normed.mark(nc.gpsimd.tensor_tensor(
                    qn[0:r, :].rearrange("p (j k d) -> p k j d", k=HKV, d=HD),
                    qu[0:r, 0:QW].rearrange("p (k j d) -> p k j d", k=HKV, d=HD),
                    C["q_norm"][0:r, :].unsqueeze(1).unsqueeze(1).broadcast_to([r, HKV, GQ, HD]), ALU.mult))
                qk_normed.mark(nc.gpsimd.tensor_tensor(
                    kn[0:r, :].rearrange("p (h d) -> p h d", d=HD), qu[0:r, QW:QW + KVW].rearrange("p (h d) -> p h d", d=HD),
                    C["k_norm"][0:r, :].unsqueeze(1).broadcast_to([r, HKV, HD]), ALU.mult))

            rstd_x(Tile(0, 0))
            rstd_x(Tile(0, 1))
            square_z(Tile(0, 0))
            rstd_z(Tile(0, 0))
            weigh_qk(Tile(0, 0))

            def period(t):
                static = isinstance(t.i, int)
                if not (static and t.c + 2 > NT):
                    rstd_x(t + 2)
                keep_v(t)
                square_z(t + 1)
                rstd_z(t + 1)
                if static and t.c == NT - 1:
                    qk_turned.wait(pool, t)
                    pool.dma_start(outs["k_prompt"][0, 0].rearrange("s k d -> s (k d)"), kn[:, :]).then_inc(k_out, 16)
                    pool.wait_ge(k_out, 16)
                weigh_qk(t + 1)

            tiles_loop(pool, period, 0, NT)


def mlstm(nc, C, ins, outs, h_dram, o_dram):
    QM, KM, VM, OM = 2 * MH, 2 * MH + MLQ, 2 * MH + 2 * MLQ, 2 * MH + 2 * MLQ + MLV
    G = 4
    GW = ML_W // G
    slot = [(h % 2) * 2 + h // 2 for h in range(MH)]
    with ExitStack() as ctx:
        k = Stage(nc, ctx, "ml")
        w_hi = k.sb("w_hi", [P, KC * ML_W], F32R)
        w_lo = k.sb("w_lo", [P, KC * ML_W], F32R)
        whi = w_hi[:, :].rearrange("p (c n) -> p c n", c=KC)
        wlo = w_lo[:, :].rearrange("p (c n) -> p c n", c=KC)
        hh = k.sb("hh", [P, 2, 2, D], F32R)
        z = k.sb("z", [P, 2, ML_W])
        q_T = k.sb("q_T", [P, 2 * P])
        k_T = k.sb("k_T", [P, 2 * P])
        ig = k.sb("ig", [MH, P])
        fg = k.sb("fg", [MH, P])
        nab = k.sb("nab", [MH, P])
        ef = k.sb("ef", [MH, P])
        sp_ = k.sb("softplus", [MH, P])
        lf = k.sb("lf", [MH, P])
        b = k.sb("b", [MH, P])
        m = k.sb("m", [MH, 2, P])
        neg_M = k.sb("neg_M", [MH, P])
        R = k.sb("rows", [MH, 4, P])
        dsc = k.sb("dsc", [MH, MH])
        cols = k.sb("cols", [P, 20])
        e = k.sb("e", [P, MH * P])
        a = k.sb("a", [P, MH * P])
        vx = k.sb("vx", [P, MH, MVE])
        kw = k.sb("kw", [P, MLQ])
        num = k.sb("num", [P, MH * MVE])
        CT = k.sb("CT", [P, 2, 2 * MVE])
        dn = k.sb("dn", [P, MH])
        dn2 = k.sb("dn2", [P, MH])
        rd = k.sb("rd", [P, MH])
        h = k.sb("h", [P, MLV])
        hq = k.sb("hq", [P, MLV])
        hss = k.sb("hss", [P, MH])
        hvar = k.sb("hvar", [P, MH])
        hr = k.sb("hr", [P, MH])
        h1 = k.sb("h1", [P, MLV])
        eo = k.sb("eo", [P, MLV])
        sg = k.sb("sg", [P, MLV])
        o = k.sb("o", [P, 2, MLV])
        bank = k.banks()

        wl = [k.sem("w_landed0"), k.sem("w_landed1")]
        w_rounded, w_split = k.sem("w_rounded"), k.sem("w_split")
        h_in = k.landed("h_in")
        proj = k.steps("proj", G)
        z_ready = k.steps("z_ready", G)
        turned = k.steps("turned", 2)
        qk_kept = k.steps("qk_kept", 2)
        rows_v = k.steps("rows_v", 9)
        rows_a = k.steps("rows_a", 5)
        mid = k.steps("mid", 3)
        cols_kept = k.steps("cols_kept")
        capped = k.steps("capped")
        e_done = k.steps("e_done")
        a_done = k.steps("a_done", 2)
        vx_kept = k.steps("vx_kept")
        kw_done = k.steps("kw_done")
        summed = k.steps("summed", 3)
        num_kept = k.steps("num_kept", 2)
        joined = k.steps("joined")
        state = k.steps("state")
        den_v = k.steps("den_v", 3)
        h_done = k.steps("h_done")
        h_square = k.steps("h_square")
        h_sum = k.steps("h_sum", 2)
        h_rstd = k.steps("h_rstd")
        h_scaled = k.steps("h_scaled")
        h_weighed = k.steps("h_weighed")
        o_exp = k.steps("o_exp")
        o_sig = k.steps("o_sig", 2)
        o_ready = k.steps("o_ready")
        o_out = k.landed("o_out")
        state_zero = k.sem("state_zero")
        prompt_turned, prompt_kept, prompt_out = k.sem("prompt_turned"), k.sem("prompt_kept"), k.sem("prompt_out")

        def rows(t):
            return NS if t.c == NT else P

        samp = Tile(0, NT)
        last = Tile(0, NT - 1)

        with ExitStack() as stage_ctx:
            stage = stage_ctx.enter_context(nc.sbuf_tensor("ml_stage", [P, 2, ML_W], F32))
            block = stage_ctx.enter_context(nc.Block())
            w_in = ins["w_in"][0]

            @block.sync
            def _(sp):
                for c in range(KC):
                    wait(sp, w_split, c - 1)
                    src = w_in[c * P:(c + 1) * P, :]
                    sp.dma_start(stage[:, c % 2, 0:QM], src[:, IN_W - QM:IN_W]).then_inc(wl[c % 2], 16)
                    sp.dma_start(stage[:, c % 2, QM:ML_W], src[:, ATT_W:IN_W - QM]).then_inc(wl[c % 2], 16)

            @block.scalar
            def _(act):
                for c in range(KC):
                    act.wait_ge(wl[c % 2], 32 * (c // 2 + 1))
                    nc.scalar.activation(whi[:, c, :], stage[:, c % 2, :], ACT.Copy).then_inc(w_rounded, 1)

            @block.vector
            def _(dve):
                for c in range(KC):
                    dve.wait_ge(w_rounded, c + 1)
                    nc.vector.tensor_tensor(wlo[:, c, :], stage[:, c % 2, :], whi[:, c, :].bitcast(F32), ALU.subtract).then_inc(w_split, 1)

        C0 = k.sb("C0", [P, SB * MH, MQK])
        n0 = k.sb("n0", [SB, MLQ])
        m0 = k.sb("m0", [MH, SB])
        C0T = k.sb("C0T", [P, SB, 2, MV])
        nT = k.sb("nT", [P, 2, SB])
        first_of = k.sb("first_of", [MH, NS])
        cols_s = k.sb("cols_s", [P, 16 + MH * SB + MH])
        iT = k.sb("iT", [P, MH, NS])
        tm = k.sb("tm", [MH, 2, NS])
        nq = k.sb("nq", [NS, MH, SB])
        nqs = k.sb("nqs", [NS, MH])
        kwx = k.sb("kwx", [NS, MH, SB, MQK])
        Cn = z[:, :, :].rearrange("p a n -> p (a n)")[:, 0:MH * SB * MQK].rearrange("p (h b d) -> p h b d", h=MH, b=SB)
        nn = k.sb("nn", [SB, MLQ])
        Cp = k.sb("Cp", [P, 2 * P])
        ev = {n: k.sem("ev_" + n) for n in (
            "state_in", "C0_turned", "C0_kept", "nT_turned", "nT_kept", "pattern", "bscan", "mscan", "tm", "tm_exp", "mid", "cols_kept",
            "qk", "interT", "iT", "inter", "nq_mult", "nq", "kwx", "delta", "Cscaled", "Cn", "n_delta", "nn", "joined", "out")}

        def sig(ins_, name):
            ins_.then_inc(ev[name], 1)

        def need(eng, name, n=1):
            eng.wait_ge(ev[name], n)

        block = ctx.enter_context(nc.Block())

        @block.sync
        def _(sp):
            def load_h(t):
                proj.wait(sp, t - 2)
                dst = hh[:, t.p, :, :].bitcast(F32)
                if t.c == NT:
                    cut = lambda x_: x_.rearrange("p a (c r) -> p (a c) r", r=P)[:, :, 0:NS]
                    h_in.mark(sp.dma_start(cut(dst), cut(h_dram[NT])), t)
                else:
                    h_in.mark(sp.dma_start(dst, h_dram[bass.ds(t.n, 1)].rearrange("a p b n -> (a p) b n")), t)

            def store_o(t):
                o_ready.wait(sp, t)
                r = rows(t)
                o_out.mark(sp.dma_start(o_dram[bass.ds(t.n * P, r), QW:QW + MLV], o[0:r, t.p, :]), t)

            load_h(Tile(0, 0))
            load_h(Tile(0, 1))
            sp.dma_start(C0[:, :, :], ins["state_mlstm_C"][0].rearrange("b h v d -> v (b h) d")).then_inc(ev["state_in"], 16)
            sp.dma_start(n0[:, :], ins["state_mlstm_n"][0].rearrange("b h d -> b (h d)")).then_inc(ev["state_in"], 16)
            with nc.allow_non_contiguous_dma(reason="32 stabilisers"):
                sp.dma_start(m0[:, :], ins["state_mlstm_m"][0].rearrange("b h -> h b")).then_inc(ev["state_in"], 16)

            def period(t):
                if not (isinstance(t.i, int) and t.c + 2 > NT):
                    load_h(t + 2)
                if not (isinstance(t.i, int) and t.c < 1):
                    store_o(t - 1)

            tiles_loop(sp, period, 0, NT)
            store_o(last)
            sp.wait_ge(prompt_kept, 1)
            state.wait(sp, last)
            for j in range(2):
                for hd in range(2):
                    sp.dma_start(outs["C_prompt"][0, 0, 2 * j + hd], Cp[:, j * P + hd * MQK:j * P + (hd + 1) * MQK]).then_inc(prompt_out, 16)
                    with nc.allow_non_contiguous_dma(reason="a normaliser of 64"):
                        sp.dma_start(outs["n_prompt"][0, 0, 2 * j + hd, :].rearrange("(d a) -> d a", a=1),
                                     CT[hd * MQK:(hd + 1) * MQK, j, hd * MVE + MV:hd * MVE + MVE]).then_inc(prompt_out, 16)
            with nc.allow_non_contiguous_dma(reason="four stabilisers"):
                sp.dma_start(outs["m_prompt"][0, 0, :].rearrange("(h a) -> h a", a=1), m[:, last.p, P - 1:P]).then_inc(prompt_out, 16)
            need(sp, "joined")
            o_ready.wait(sp, samp)
            sp.dma_start(o_dram[SEQ:SEQ + NS, QW:QW + MLV], o[0:NS, 0, :]).then_inc(ev["out"], 16)
            need(sp, "mscan", SB)
            with nc.allow_non_contiguous_dma(reason="32 stabilisers"):
                sp.dma_start(outs["m_sample"][0].rearrange("b h -> h b"),
                             m[:, 0, 0:NS].rearrange("h (b t) -> h b t", t=ST)[:, :, ST - 1]).then_inc(ev["out"], 16)
            need(sp, "nn", 2)
            sp.dma_start(outs["n_sample"][0].rearrange("b h d -> b (h d)"), nn[:, :]).then_inc(ev["out"], 16)
            for hd in range(MH):
                need(sp, "Cn", hd + 1)
                sp.dma_start(outs["C_sample"][0, :, hd].rearrange("b v d -> v b d"), Cn[:, hd]).then_inc(ev["out"], 16)
            sp.wait_ge(prompt_out, 16 * 9)
            need(sp, "out", 16 * 7)
            o_out.wait(sp, last)
            o_out.wait(sp, last - 1)

        @block.tensor
        def _(pe):
            def project(t, g):
                r = rows(t)
                if g == 0:
                    h_in.wait(pe, t)
                z_ready.wait(pe, t - 1 if g < 2 else t, (g - 2) % G)
                for c in range(KC):
                    at = slice(c * P, c * P + r)
                    ins_ = mm3(nc, bank[g % 2][0:r, 0:GW], hh[:, t.p, 0, at], hh[:, t.p, 1, at],
                               whi[:, c, g * GW:(g + 1) * GW], wlo[:, c, g * GW:(g + 1) * GW], c == 0, c == KC - 1)
                proj.mark(ins_)

            def turn(t):
                r = rows(t)
                z_ready.wait(pe, t, 1)
                joined.wait(pe, t - 1)
                for n in range(4):
                    ins_ = nc.tensor.transpose(bank[2][:, n * P:n * P + r], z[0:r, t.p, QM + n * P:QM + (n + 1) * P], C["ident"][0:r, 0:r])
                turned.mark(ins_)
                for n in range(2):
                    ins_ = nc.tensor.transpose(bank[3][0:MH, n * P:n * P + r], z[0:r, t.p, n * MH:(n + 1) * MH], C["ident"][0:r, 0:r])
                turned.mark(ins_)

            def middle(t):
                qk_kept.wait(pe, t)
                rows_v.wait(pe, t, 1)
                for hd in range(MH):
                    part = slice((hd % 2) * MQK, (hd % 2 + 1) * MQK)
                    at = slice((hd // 2) * P, (hd // 2 + 1) * P)
                    ins_ = nc.tensor.matmul(bank[2 + hd % 2][:, at], k_T[part, at], q_T[part, at], start=True, stop=True)
                mid.mark(ins_)
                rows_v.wait(pe, t, 7)
                state.wait(pe, t - 1)
                for hd in range(MH):
                    ins_ = nc.tensor.matmul(bank[4][:, slot[hd] * P:(slot[hd] + 1) * P], C["sel_head"][:, hd * P:(hd + 1) * P],
                                            neg_M[:, :], start=True, stop=True)
                mid.mark(ins_)
                rows_a.wait(pe, t)
                rows_v.wait(pe, t)
                nc.tensor.matmul(bank[7][:, 16:20], C["ones"][0:MH, :], dsc[:, :], start=True, stop=True)
                for n in range(4):
                    ins_ = nc.tensor.transpose(bank[7][:, n * MH:(n + 1) * MH], R[:, n, :], C["ident"][0:MH, 0:MH])
                mid.mark(ins_)

            def sums(t):
                a_done.wait(pe, t)
                vx_kept.wait(pe, t)
                num_kept.wait(pe, t - 1)
                for hd in range(MH):
                    ins_ = nc.tensor.matmul(bank[5 + hd // 2][:, (hd % 2) * MVE:(hd % 2 + 1) * MVE],
                                            a[:, slot[hd] * P:(slot[hd] + 1) * P], vx[:, hd, :], start=True, stop=True)
                summed.mark(ins_)
                state.wait(pe, t - 1)
                pe.wait_ge(state_zero, 1)
                for j in range(2):
                    ins_ = nc.tensor.matmul(bank[2 + j][:, 0:2 * MVE], q_T[:, j * P:(j + 1) * P], CT[:, j, :], start=True, stop=True)
                summed.mark(ins_)
                kw_done.wait(pe, t)
                capped.wait(pe, t)
                for j in range(2):
                    ins_ = nc.tensor.matmul(bank[(4, 7)[j]][:, 0:2 * MVE], kw[:, j * P:(j + 1) * P],
                                            vx[:, 2 * j:2 * j + 2, :].rearrange("s h v -> s (h v)"), start=True, stop=True)
                summed.mark(ins_)

            for g in range(G):
                project(Tile(0, 0), g)

            def period(t):
                project(t + 1, 0)
                turn(t)
                project(t + 1, 1)
                project(t + 1, 2)
                middle(t)
                project(t + 1, 3)
                sums(t)

            tiles_loop(pe, period, 0, NT)
            state.wait(pe, last)
            for j in range(2):
                for hd in range(2):
                    nc.tensor.transpose(bank[4][:, (2 * j + hd) * P:(2 * j + hd + 1) * P], CT[:, j, hd * MVE:hd * MVE + MV], C["ident"][:, :])\
                        .then_inc(prompt_turned, 1)
            turn(samp)
            need(pe, "state_in", 48)
            z_ready.wait(pe, samp)
            for q in range(4):
                num_kept.wait(pe, last)
                for n in range(4):
                    b_, j = (4 * q + n) // 2, (4 * q + n) % 2
                    ins_ = nc.tensor.transpose(bank[(0, 1, 5, 6)[q]][:, n * P:(n + 1) * P],
                                               C0[:, b_ * MH + 2 * j:b_ * MH + 2 * j + 2, :].rearrange("v h d -> v (h d)"), C["ident"][:, :])
                sig(ins_, "C0_turned")
            for j in range(2):
                ins_ = nc.tensor.transpose(bank[7][:, j * SB:(j + 1) * SB], n0[:, j * P:(j + 1) * P], C["ident"][0:SB, 0:SB])
            sig(ins_, "nT_turned")
            qk_kept.wait(pe, samp)
            need(pe, "bscan")
            for hd in range(MH):
                part = slice((hd % 2) * MQK, (hd % 2 + 1) * MQK)
                at = (hd // 2) * P
                ins_ = nc.tensor.matmul(bank[2 + hd % 2][0:NS, at:at + NS], k_T[part, at:at + NS], q_T[part, at:at + NS], start=True, stop=True)
            sig(ins_, "qk")
            rows_v.wait(pe, samp, 7)
            pe.wait_ge(prompt_kept, 1)
            for hd in range(MH):
                nc.tensor.matmul(bank[4][0:NS, slot[hd] * NS:(slot[hd] + 1) * NS], C["sel_head"][:, hd * P:hd * P + NS],
                                 neg_M[:, 0:NS], start=True, stop=True)
            rows_a.wait(pe, samp)
            need(pe, "nT_kept")
            for n in range(4):
                nc.tensor.transpose(bank[7][0:NS, n * MH:(n + 1) * MH], R[:, n, 0:NS], C["ident"][0:MH, 0:MH])
            sc = R[:, 1, 0:NS].rearrange("h (b t) -> h b t", t=ST)[:, :, ST - 1]
            for hd in range(MH):
                nc.tensor.matmul(bank[7][:, 16 + hd * SB:16 + (hd + 1) * SB], C["sel_head"][:, hd * P:(hd + 1) * P], sc, start=True, stop=True)
            sig(nc.tensor.transpose(bank[7][0:SB, 16 + MH * SB:16 + MH * SB + MH], sc, C["ident"][0:MH, 0:MH]), "mid")
            need(pe, "C0_kept", 4)
            for hd in range(MH):
                part = slice((hd % 2) * MQK, (hd % 2 + 1) * MQK)
                for b_ in range(SB):
                    at = (hd // 2) * P + b_ * ST
                    ins_ = nc.tensor.matmul(bank[5 + hd % 2][:, (hd // 2) * NS + b_ * ST:(hd // 2) * NS + (b_ + 1) * ST],
                                            C0T[part, b_, hd // 2, :], q_T[part, at:at + ST], start=True, stop=True)
            for hd in range(MH):
                part = slice((hd % 2) * MQK, (hd % 2 + 1) * MQK)
                at = (hd // 2) * P
                ins_ = nc.tensor.matmul(bank[hd % 2][0:NS, (hd // 2) * SB:(hd // 2 + 1) * SB], q_T[part, at:at + NS],
                                        nT[part, hd // 2, :], start=True, stop=True)
            sig(ins_, "interT")
            a_done.wait(pe, samp)
            vx_kept.wait(pe, samp)
            for hd in range(MH):
                ins_ = nc.tensor.matmul(bank[2 + hd // 2][0:NS, (hd % 2) * MVE:(hd % 2 + 1) * MVE],
                                        a[0:NS, slot[hd] * NS:(slot[hd] + 1) * NS], vx[0:NS, hd, :], start=True, stop=True)
            summed.mark(ins_)
            need(pe, "iT", 2)
            for hd in range(MH):
                ins_ = nc.tensor.transpose(bank[5][0:NS, hd * P:(hd + 1) * P], iT[:, hd, :], C["ident"][:, :])
            sig(ins_, "inter")
            need(pe, "kwx")
            need(pe, "nq_mult", 4)
            capped.wait(pe, samp)
            for hd in range(MH):
                sig(nc.tensor.matmul(bank[(0, 1, 4, 6)[hd]][:, :], vx[0:NS, hd, 0:MV],
                                     kwx[:, hd, :, :].rearrange("s b d -> s (b d)"), start=True, stop=True), "delta")
            sig(nc.tensor.matmul(bank[7][0:SB, 0:MLQ], C["blk"][:, :], kw[0:NS, :], start=True, stop=True), "n_delta")

        @block.scalar
        def _(act):
            def keep_z(t, g):
                r = rows(t)
                proj.wait(act, t, g)
                if g == 0:
                    turned.wait(act, t - 2)
                    vx_kept.wait(act, t - 2)
                    kw_done.wait(act, t - 2)
                    o_exp.wait(act, t - 2)
                z_ready.mark(nc.scalar.activation(z[0:r, t.p, g * GW:(g + 1) * GW], bank[g % 2][0:r, 0:GW], ACT.Copy))

            def keep_qk(t):
                r = rows(t)
                turned.wait(act, t, 0)
                summed.wait(act, t - 1, 1)
                src = bank[2][:, :].rearrange("p (n r) -> p n r", r=P)
                cut = lambda x_: x_[:, :].rearrange("p (n r) -> p n r", r=P)[:, :, 0:r]
                qk_kept.mark(nc.scalar.activation(cut(q_T), src[:, 0:2, 0:r], ACT.Copy, scale=ML_SCALE))
                qk_kept.mark(nc.scalar.activation(cut(k_T), src[:, 2:4, 0:r], ACT.Copy))

            def forget(t):
                r = rows(t)
                rows_v.wait(act, t, 2)
                rows_a.mark(nc.scalar.activation(ef[:, 0:r], nab[:, 0:r], ACT.Exp))
                rows_a.wait(act, t, 0)
                rows_a.mark(nc.scalar.activation(sp_[:, 0:r], ef[:, 0:r], ACT.Ln, bias=1.0))

            def weights(t):
                rows_v.wait(act, t, 7)
                mid.wait(act, t - 1)
                rows_a.mark(nc.scalar.activation(R[:, 1, :], neg_M[:, :], ACT.Exp, bias=m[:, 1 - t.p, P - 1:P]))
                rows_a.mark(nc.scalar.activation(R[:, 2, :], m[:, t.p, :], ACT.Exp, scale=-1.0))
                rows_a.mark(nc.scalar.activation(R[:, 3, :], R[:, 0, :], ACT.Exp, bias=neg_M[:, P - 1:P]))

            def exp_e(t):
                capped.wait(act, t)
                r, w = (NS, MH * NS) if t.c == NT else (P, MH * P)
                e_done.mark(nc.scalar.activation(e[0:r, 0:w], e[0:r, 0:w], ACT.Exp))

            def exp_o(t):
                r = rows(t)
                z_ready.wait(act, t)
                o_sig.wait(act, t - 1, 0)
                o_exp.mark(nc.scalar.activation(eo[0:r, :], z[0:r, t.p, OM:ML_W], ACT.Exp, scale=-1.0))

            def keep_num(t):
                summed.wait(act, t, 0)
                h_done.wait(act, t - 1)
                for j in range(2):
                    num_kept.mark(nc.scalar.activation(num[:, j * 2 * MVE:(j + 1) * 2 * MVE], bank[5 + j][:, 0:2 * MVE], ACT.Copy))

            for g in range(G):
                keep_z(Tile(0, 0), g)

            def period(t):
                keep_z(t + 1, 0)
                keep_qk(t)
                forget(t)
                keep_z(t + 1, 1)
                weights(t)
                exp_o(t)
                keep_z(t + 1, 2)
                exp_e(t)
                keep_z(t + 1, 3)
                keep_num(t)

            act.wait_ge(state_zero, 1)
            tiles_loop(act, period, 0, NT)
            act.wait_ge(prompt_turned, 4)
            src = bank[4][:, :].rearrange("p (n r) -> p n r", r=P)
            for j in range(2):
                nc.scalar.activation(Cp[:, j * P:j * P + MQK], src[:, 2 * j, 0:MQK], ACT.Copy)
                ins_ = nc.scalar.activation(Cp[:, j * P + MQK:(j + 1) * P], src[:, 2 * j + 1, MQK:2 * MQK], ACT.Copy)
            ins_.then_inc(prompt_kept, 1)
            keep_qk(samp)
            forget(samp)
            exp_o(samp)
            for q in range(4):
                need(act, "C0_turned", q + 1)
                sig(nc.scalar.activation(C0T[:, 2 * q:2 * q + 2, :, :].rearrange("p b j v -> p (b j v)"),
                                         bank[(0, 1, 5, 6)[q]][:, :], ACT.Copy), "C0_kept")
            need(act, "tm", 2)
            mid.wait(act, last)
            rows_a.mark(nc.scalar.activation(R[:, 1, 0:NS], tm[:, 0, :], ACT.Exp))
            rows_a.mark(nc.scalar.activation(R[:, 2, 0:NS], m[:, 0, 0:NS], ACT.Exp, scale=-1.0))
            rows_a.mark(nc.scalar.activation(R[:, 3, 0:NS], tm[:, 1, :], ACT.Exp))
            exp_e(samp)
            need(act, "interT")
            for n in range(2):
                sig(nc.scalar.activation(iT[:, n:MH:2, :], bank[5 + n][:, 0:2 * NS].rearrange("p (a r) -> p a r", a=2), ACT.Copy), "iT")
            h_done.wait(act, last)
            summed.wait(act, samp, 0)
            for j in range(2):
                num_kept.mark(nc.scalar.activation(num[0:NS, j * 2 * MVE:(j + 1) * 2 * MVE], bank[2 + j][0:NS, 0:2 * MVE], ACT.Copy))

        @block.vector
        def _(dve):
            def gates(t):
                r = rows(t)
                turned.wait(dve, t)
                rows_a.wait(dve, t - 1)
                rows_v.mark(nc.vector.tensor_scalar(ig[:, 0:r], bank[3][0:MH, 0:r], C["bias_i"][:, 0:1], None, ALU.add))
                rows_v.mark(nc.vector.tensor_scalar(fg[:, 0:r], bank[3][0:MH, P:P + r], C["bias_f"][:, 0:1], None, ALU.add))
                rows_v.wait(dve, t, 1)
                rows_v.mark(nc.vector.scalar_tensor_tensor(nab[:, 0:r], fg[:, 0:r], -1.0, fg[:, 0:r], ALU.mult, ALU.min))

            def log_forget(t):
                r = rows(t)
                rows_a.wait(dve, t, 1)
                rows_v.mark(nc.vector.scalar_tensor_tensor(lf[:, 0:r], fg[:, 0:r], 0.0, sp_[:, 0:r], ALU.min, ALU.subtract))
                rows_v.wait(dve, t, 3)

            def scans(t):
                log_forget(t)
                mid.wait(dve, t - 1)
                rows_v.mark(nc.vector.tensor_tensor_scan(b[:, :], C["ones"][0:MH, :], lf[:, :], 0.0, ALU.mult, ALU.add))
                rows_v.mark(nc.vector.tensor_tensor_scan(m[:, t.p, :], lf[:, :], ig[:, :], m[:, 1 - t.p, P - 1:P], ALU.add, ALU.max))
                rows_v.wait(dve, t, 5)
                rows_v.mark(nc.vector.tensor_tensor(R[:, 0, :], ig[:, :], b[:, :], ALU.subtract))
                rows_v.mark(nc.vector.tensor_tensor(neg_M[:, :], b[:, :], m[:, t.p, :], ALU.subtract))
                rows_a.wait(dve, t, 2)
                rows_v.mark(nc.vector.tensor_scalar(dsc[:, :], C["ident"][0:MH, 0:MH], R[:, 1, P - 1:P], None, ALU.mult))

            def cap_e(t):
                mid.wait(dve, t)
                joined.wait(dve, t - 1)
                state.wait(dve, t - 1)
                cols_kept.mark(nc.vector.tensor_copy(cols[:, :], bank[7][:, 0:20]))
                cols_kept.wait(dve, t)
                a_done.wait(dve, t - 1)
                for hd in range(MH):
                    at = slice(slot[hd] * P, (slot[hd] + 1) * P)
                    ins_ = nc.vector.scalar_tensor_tensor(e[:, at], bank[4][:, at], cols[:, hd:hd + 1], C["cap"][:, :], ALU.add, ALU.min)
                capped.mark(ins_)

            def make_a(t):
                e_done.wait(dve, t)
                summed.wait(dve, t - 1, 0)
                for n in range(2):
                    a_done.mark(nc.vector.tensor_tensor(a[:, n * 2 * P:(n + 1) * 2 * P], bank[2 + n][:, 0:2 * P],
                                                        e[:, n * 2 * P:(n + 1) * 2 * P], ALU.mult))

            def join(t):
                num_kept.wait(dve, t)
                summed.wait(dve, t, 1)
                for hd in range(MH):
                    at = slice(hd * MVE, (hd + 1) * MVE)
                    ins_ = nc.vector.scalar_tensor_tensor(num[:, at], bank[2 + hd // 2][:, (hd % 2) * MVE:(hd % 2 + 1) * MVE],
                                                          cols[:, MH + hd:MH + hd + 1], num[:, at], ALU.mult, ALU.add)
                joined.mark(ins_)

            def update_state(t):
                summed.wait(dve, t)
                for hd in range(MH):
                    part = slice((hd % 2) * MQK, (hd % 2 + 1) * MQK)
                    blk = CT[part, hd // 2, (hd % 2) * MVE:(hd % 2 + 1) * MVE]
                    ins_ = nc.vector.scalar_tensor_tensor(blk, blk, cols[part, 16 + hd:17 + hd],
                                                          bank[(4, 7)[hd // 2]][part, (hd % 2) * MVE:(hd % 2 + 1) * MVE], ALU.mult, ALU.add)
                state.mark(ins_)

            def divide(t):
                r = rows(t)
                joined.wait(dve, t)
                nv = num[0:r, :].rearrange("p (h v) -> p h v", h=MH)
                cc = cols_s if t.c == NT else cols
                den_v.mark(nc.vector.scalar_tensor_tensor(dn[0:r, :], nv[:, :, MV], -1.0, nv[:, :, MV], ALU.mult, ALU.max))
                den_v.wait(dve, t, 0)
                den_v.mark(nc.vector.tensor_tensor(dn2[0:r, :], dn[0:r, :], cc[0:r, 8:12], ALU.max))
                den_v.wait(dve, t, 1)
                den_v.mark(nc.vector.reciprocal(rd[0:r, :], dn2[0:r, :]))
                den_v.wait(dve, t, 2)
                h_square.wait(dve, t - 1)
                h_done.mark(nc.vector.tensor_tensor(h[0:r, :].rearrange("p (h v) -> p h v", h=MH), nv[:, :, 0:MV],
                                                    rd[0:r, :].unsqueeze(2).broadcast_to([r, MH, MV]), ALU.mult))

            def gate_out(t):
                r = rows(t)
                o_exp.wait(dve, t)
                o_sig.mark(nc.vector.tensor_scalar(sg[0:r, :], eo[0:r, :], 1.0, None, ALU.add))
                o_sig.wait(dve, t, 0)
                o_sig.mark(nc.vector.reciprocal(sg[0:r, :], sg[0:r, :]))

            def norm_out(t):
                r = rows(t)
                h_square.wait(dve, t)
                h_sum.mark(nc.vector.reduce_sum(hss[0:r, :], hq[0:r, :].rearrange("p (h v) -> p h v", h=MH), axis=AX))
                h_sum.wait(dve, t, 0)
                h_rstd.wait(dve, t - 1)
                h_sum.mark(nc.vector.tensor_scalar(hvar[0:r, :], hss[0:r, :], 1.0 / MV, EPS, ALU.mult, ALU.add))
                h_rstd.wait(dve, t)
                h_weighed.wait(dve, t - 1)
                h_scaled.mark(nc.vector.tensor_tensor(h1[0:r, :].rearrange("p (h v) -> p h v", h=MH),
                                                      h[0:r, :].rearrange("p (h v) -> p h v", h=MH),
                                                      hr[0:r, :].unsqueeze(2).broadcast_to([r, MH, MV]), ALU.mult))

            def finish_out(t):
                r = rows(t)
                h_weighed.wait(dve, t)
                o_sig.wait(dve, t)
                o_out.wait(dve, t - 2)
                o_ready.mark(nc.vector.tensor_tensor(o[0:r, t.p, :], hq[0:r, :], sg[0:r, :], ALU.mult))

            nc.vector.memset(CT[:, :, :], 0.0)
            nc.vector.memset(m[:, :, :], 0.0)
            nc.vector.memset(vx[:, :, MV:MVE], 1.0).then_inc(state_zero, 1)
            dve.wait_ge(state_zero, 1)

            def period(t):
                gates(t)
                scans(t)
                gate_out(t)
                cap_e(t)
                make_a(t)
                join(t)
                update_state(t)
                divide(t)
                norm_out(t)
                finish_out(t)

            tiles_loop(dve, period, 0, NT)
            nc.vector.memset(first_of[:, :], 1.0).then_inc(ev["pattern"], 1)
            need(dve, "pattern")
            nc.vector.memset(first_of[:, :].rearrange("h (b t) -> h b t", t=ST)[:, :, 0], 0.0).then_inc(ev["pattern"], 1)
            gates(samp)
            need(dve, "nT_turned")
            sig(nc.vector.tensor_copy(nT[:, :, :], bank[7][:, 0:2 * SB].rearrange("p (j b) -> p j b", j=2)), "nT_kept")
            log_forget(samp)
            need(dve, "pattern", 2)
            mid.wait(dve, last)
            rows_v.mark(nc.vector.tensor_tensor_scan(b[:, 0:NS], first_of[:, :], lf[:, 0:NS], 0.0, ALU.mult, ALU.add))
            sig(nc.vector.memset(dsc[:, :], 0.0), "bscan")
            need(dve, "state_in", 48)
            sp_done = None
            for b_ in range(SB):
                at = slice(b_ * ST, (b_ + 1) * ST)
                sig(nc.vector.tensor_tensor_scan(m[:, 0, at], lf[:, at], ig[:, at], m0[:, b_:b_ + 1], ALU.add, ALU.max), "mscan")
            rows_v.wait(dve, samp, 4)
            need(dve, "mscan", SB)
            rows_v.mark(nc.vector.tensor_tensor(R[:, 0, 0:NS], ig[:, 0:NS], b[:, 0:NS], ALU.subtract))
            rows_v.mark(nc.vector.tensor_tensor(neg_M[:, 0:NS], b[:, 0:NS], m[:, 0, 0:NS], ALU.subtract))
            rows_v.mark(nc.vector.memset(tm[:, :, :], 0.0))
            rows_v.wait(dve, samp, 7)
            bt = lambda x_: x_.rearrange("h (b t) -> h b t", t=ST)
            sig(nc.vector.tensor_tensor(bt(tm[:, 0, :]), bt(neg_M[:, 0:NS]), m0[:, :].unsqueeze(2).broadcast_to([MH, SB, ST]), ALU.add), "tm")
            sig(nc.vector.tensor_tensor(bt(tm[:, 1, :]), bt(R[:, 0, 0:NS]),
                                        bt(neg_M[:, 0:NS])[:, :, ST - 1:ST].broadcast_to([MH, SB, ST]), ALU.add), "tm")
            need(dve, "mid")
            nc.vector.tensor_copy(cols_s[0:NS, 0:16], bank[7][0:NS, 0:16])
            nc.vector.tensor_copy(cols_s[:, 16:16 + MH * SB], bank[7][:, 16:16 + MH * SB])
            cols_kept.mark(nc.vector.tensor_copy(cols_s[0:SB, 16 + MH * SB:16 + MH * SB + MH], bank[7][0:SB, 16 + MH * SB:16 + MH * SB + MH]))
            cols_kept.wait(dve, samp)
            for hd in range(MH):
                at = slice(slot[hd] * NS, (slot[hd] + 1) * NS)
                ins_ = nc.vector.scalar_tensor_tensor(e[0:NS, at], bank[4][0:NS, at], cols_s[0:NS, hd:hd + 1], C["cap64"][:, :], ALU.add, ALU.min)
            capped.mark(ins_)
            e_done.wait(dve, samp)
            for n in range(2):
                a_done.mark(nc.vector.tensor_tensor(
                    a[0:NS, n * 2 * NS:(n + 1) * 2 * NS].rearrange("p (a r) -> p a r", a=2),
                    bank[2 + n][0:NS, 0:2 * P].rearrange("p (a r) -> p a r", a=2)[:, :, 0:NS],
                    e[0:NS, n * 2 * NS:(n + 1) * 2 * NS].rearrange("p (a r) -> p a r", a=2), ALU.mult))
            need(dve, "interT")
            for hd in range(MH):
                sig(nc.vector.tensor_tensor(nq[:, hd, :], bank[hd % 2][0:NS, (hd // 2) * SB:(hd // 2 + 1) * SB], C["blk"][:, :], ALU.mult), "nq_mult")
            need(dve, "nq_mult", 4)
            sig(nc.vector.reduce_sum(nqs[:, :], nq[:, :, :], axis=AX), "nq")
            kw_done.wait(dve, samp)
            for hd in range(MH):
                ins_ = nc.vector.tensor_tensor(kwx[:, hd, :, :], kw[0:NS, hd * MQK:(hd + 1) * MQK].unsqueeze(1).broadcast_to([NS, SB, MQK]),
                                               C["blk"][:, :].unsqueeze(2).broadcast_to([NS, SB, MQK]), ALU.mult)
            sig(ins_, "kwx")
            need(dve, "inter")
            need(dve, "nq")
            num_kept.wait(dve, samp)
            for hd in range(MH):
                at = slice(hd * MVE, hd * MVE + MV)
                nc.vector.scalar_tensor_tensor(num[0:NS, at], bank[5][0:NS, hd * P:(hd + 1) * P], cols_s[0:NS, MH + hd:MH + hd + 1],
                                               num[0:NS, at], ALU.mult, ALU.add)
                d_ = num[0:NS, hd * MVE + MV:(hd + 1) * MVE]
                ins_ = nc.vector.scalar_tensor_tensor(d_, nqs[:, hd:hd + 1], cols_s[0:NS, MH + hd:MH + hd + 1], d_, ALU.mult, ALU.add)
            joined.mark(ins_)
            gate_out(samp)
            divide(samp)
            norm_out(samp)
            finish_out(samp)
            sig(nc.vector.memset(dsc[:, :], 0.0), "joined")
            o_ready.wait(dve, samp)
            c0 = C0[:, :, :].rearrange("v (b h) d -> v b h d", h=MH)
            for hd in range(MH):
                sig(nc.vector.tensor_tensor(Cn[:, hd], c0[:, :, hd, :],
                                            cols_s[:, 16 + hd * SB:16 + (hd + 1) * SB].unsqueeze(2).broadcast_to([P, SB, MQK]), ALU.mult), "Cscaled")
            for hd in range(MH):
                need(dve, "delta", hd + 1)
                need(dve, "Cscaled", hd + 1)
                sig(nc.vector.tensor_tensor(Cn[:, hd], Cn[:, hd], bank[(0, 1, 4, 6)[hd]][:, :].rearrange("p (b d) -> p b d", b=SB), ALU.add), "Cn")
            need(dve, "n_delta")
            hv = lambda x_: x_.rearrange("b (h d) -> b h d", h=MH)
            sig(nc.vector.tensor_tensor(hv(nn[:, :]), hv(n0[:, :]),
                                        cols_s[0:SB, 16 + MH * SB:16 + MH * SB + MH].unsqueeze(2).broadcast_to([SB, MH, MQK]), ALU.mult), "nn")
            need(dve, "nn")
            sig(nc.vector.tensor_tensor(nn[:, :], nn[:, :], bank[7][0:SB, 0:MLQ], ALU.add), "nn")

        @block.gpsimd
        def _(pool):
            def keep_v(t):
                r = rows(t)
                z_ready.wait(pool, t, 3)
                summed.wait(pool, t - 1)
                vx_kept.mark(nc.gpsimd.tensor_tensor(vx[0:r, :, 0:MV], z[0:r, t.p, VM:VM + MLV].rearrange("p (h v) -> p h v", h=MH),
                                                     C["ones"][0:r, :].unsqueeze(1).broadcast_to([r, MH, MV]), ALU.mult))

            def weigh_k(t):
                r = rows(t)
                cols_kept.wait(pool, t)
                cc = cols_s if t.c == NT else cols
                kw_done.mark(nc.gpsimd.tensor_tensor(kw[0:r, :].rearrange("p (h d) -> p h d", h=MH),
                                                     z[0:r, t.p, KM:KM + MLQ].rearrange("p (h d) -> p h d", h=MH),
                                                     cc[0:r, 12:16].unsqueeze(2).broadcast_to([r, MH, MQK]), ALU.mult))

            def square_h(t):
                r = rows(t)
                o_ready.wait(pool, t - 1)
                h_done.wait(pool, t)
                h_square.mark(nc.gpsimd.tensor_tensor(hq[0:r, :], h[0:r, :], h[0:r, :], ALU.mult))

            def rstd_h(t):
                r = rows(t)
                h_scaled.wait(pool, t - 1)
                h_sum.wait(pool, t)
                h_rstd.mark(nc.gpsimd.tensor_tensor(hr[0:r, :], hvar[0:r, :], C["mhalf"][0:r, 0:MH], ALU.pow))

            def weigh_h(t):
                r = rows(t)
                h_scaled.wait(pool, t)
                h_weighed.mark(nc.gpsimd.tensor_tensor(hq[0:r, :], h1[0:r, :], C["ml_norm"][0:r, :], ALU.mult))

            def period(t):
                keep_v(t)
                weigh_k(t)
                square_h(t)
                rstd_h(t)
                weigh_h(t)

            pool.wait_ge(state_zero, 1)
            tiles_loop(pool, period, 0, NT)
            period(samp)


def output(nc, ident, mhalf, ins, o_dram, x1_dram, h2_dram, conv_cols):
    with ExitStack() as ctx:
        k = Stage(nc, ctx, "out")
        w_hi = k.sb("w_hi", [P, KC * D], F32R)
        w_lo = k.sb("w_lo", [P, KC * D], F32R)
        whi = w_hi[:, :].rearrange("p (c n) -> p c n", c=KC)
        wlo = w_lo[:, :].rearrange("p (c n) -> p c n", c=KC)
        stage = k.sb("stage", [P, 2, D])
        norm_w = k.sb("norm_w", [P, D])
        conv_rows = k.sb("conv_rows", [SB * (CW - 1) + CW + 1, FF])
        o = k.sb("o", [P, 2, D])
        o_hi = k.sb("o_hi", [P, 2, D], F32R)
        o_lo = k.sb("o_lo", [P, 2, D], F32R)
        x = k.sb("x", [P, 2, D])
        x1 = k.sb("x1", [P, 2, D])
        square = k.sb("square", [P, D])
        xss = k.sb("xss", [P, 1])
        xvar = k.sb("xvar", [P, 1])
        xr = k.sb("xr", [P, 1])
        hn = k.sb("hn", [P, D])
        h_hi = k.sb("h_hi", [P, 2, D], F32R)
        h_lo = k.sb("h_lo", [P, 2, D], F32R)
        bank = k.banks()

        wl = [k.sem("w_landed0"), k.sem("w_landed1")]
        w_rounded, w_split = k.sem("w_rounded"), k.sem("w_split")
        rows_in, rows_turned, rows_kept = k.sem("rows_in"), k.sem("rows_turned"), k.sem("rows_kept")
        norm_in = k.sem("norm_in")
        o_in, x_in = k.landed("o_in"), k.landed("x_in")
        o_turned = k.steps("o_turned", 2)
        o_rounded = k.steps("o_rounded", 2)
        o_split = k.steps("o_split", 2)
        proj = k.steps("proj", 2)
        added = k.steps("added", 2)
        x_square = k.steps("x_square")
        x_var = k.steps("x_var")
        x_rstd = k.steps("x_rstd")
        x_normed = k.steps("x_normed")
        h_turned = k.steps("h_turned", 2)
        h_rounded = k.steps("h_rounded", 2)
        h_split = k.steps("h_split", 2)
        x1_out, h_out = k.landed("x1_out"), k.landed("h_out", 2)

        spans = [(ins["w_out"][0][c * P:(c + 1) * P, :], c * D) for c in range(KC)]
        w_sync, w_scalar, w_vector = load_split_weight(k, nc, (wl, w_rounded, w_split), spans, w_hi, w_lo, stage, [D] * KC)
        samp = Tile(0, NT)

        def rows(t):
            return NS if t.c == NT else P

        def cut(a, r):
            return a.rearrange("p (c r) -> p c r", r=P)[:, :, 0:r]

        block = ctx.enter_context(nc.Block())

        @block.sync
        def _(sp):
            def load(t):
                r = rows(t)
                o_turned.wait(sp, t - 2)
                o_in.mark(sp.dma_start(o[0:r, t.p, :], o_dram[bass.ds(t.n * P, r), :]), t)
                added.wait(sp, t - 2)
                src = ins["x_sample"].rearrange("b t d -> (b t) d") if t.c == NT else ins["x_prompt"][0, bass.ds(t.n * P, P), :]
                x_in.mark(sp.dma_start(x[0:r, t.p, :], src), t)

            def store(t):
                r = rows(t)
                added.wait(sp, t)
                x1_out.mark(sp.dma_start(x1_dram[bass.ds(t.n, 1), 0:r].rearrange("a p n -> (a p) n"), x1[0:r, t.p, :]), t)
                h_split.wait(sp, t)
                for part, src in ((0, h_hi), (1, h_lo)):
                    h_out.mark(sp.dma_start(h2_dram[:, part, :, bass.ds(t.n * P, r)], cut(src[:, t.p, :].bitcast(F32), r)), t)

            load(Tile(0, 0))
            w_sync(sp)
            sp.dma_start(norm_w[:, :], ins["norm_ffn_w"][0:1, :].partition_broadcast(P)).then_inc(norm_in, 16)
            rows_of = conv_rows[:, :]
            sp.dma_start(rows_of[0:SB * (CW - 1), :], ins["cache_ffn_conv"][0].rearrange("b c f -> (b c) f")).then_inc(rows_in, 16)
            sp.dma_start(rows_of[SB * (CW - 1):SB * (CW - 1) + CW, :], ins["conv_w"][0]).then_inc(rows_in, 16)
            sp.dma_start(rows_of[SB * (CW - 1) + CW:SB * (CW - 1) + CW + 1, :], ins["conv_b"][0:1, :]).then_inc(rows_in, 16)
            load(Tile(0, 1))

            def period(t):
                if not (isinstance(t.i, int) and t.c < 2):
                    store(t - 2)
                if not (isinstance(t.i, int) and t.c + 2 > NT):
                    load(t + 2)

            tiles_loop(sp, period, 0, NT + 1)
            store(samp - 1)
            store(samp)
            for t in (samp - 1, samp):
                x1_out.wait(sp, t)
                h_out.wait(sp, t)

        @block.tensor
        def _(pe):
            def turn(t, src, ready, turned, free, at):
                r = rows(t)
                ready.wait(pe, t)
                for b in range(2):
                    free.wait(pe, t - 1, b)
                    for c in range(4):
                        ins_ = nc.tensor.transpose(bank[at + b][:, c * P:c * P + r], src(t)[0:r, (b * 4 + c) * P:(b * 4 + c + 1) * P], ident[0:r, 0:r])
                    turned.mark(ins_)

            def turn_o(t):
                turn(t, lambda t: o[:, t.p, :], o_in, o_turned, o_split, 2)

            def turn_h(t):
                turn(t, lambda t: hn[:, :], x_normed, h_turned, h_split, 4)

            def project(t, g):
                r = rows(t)
                o_split.wait(pe, t)
                added.wait(pe, t - 1, g)
                for c in range(KC):
                    at = slice(c * P, c * P + r)
                    ins_ = mm3(nc, bank[g][0:r, :], o_hi[:, t.p, at], o_lo[:, t.p, at],
                               whi[:, c, g * 512:(g + 1) * 512], wlo[:, c, g * 512:(g + 1) * 512], c == 0, c == KC - 1)
                proj.mark(ins_)

            turn_o(Tile(0, 0))
            pe.wait_ge(rows_in, 48)
            n = SB * (CW - 1) + CW + 1
            for f in range(FC):
                ins_ = nc.tensor.transpose(bank[6][:, f * n:(f + 1) * n], conv_rows[:, f * P:(f + 1) * P], ident[0:n, 0:n])
            ins_.then_inc(rows_turned, 1)
            pe.wait_ge(w_split, KC)

            def period(t):
                project(t, 0)
                if not (isinstance(t.i, int) and t.c + 1 > NT):
                    turn_o(t + 1)
                project(t, 1)
                if not (isinstance(t.i, int) and t.c < 1):
                    turn_h(t - 1)

            tiles_loop(pe, period, 0, NT + 1)
            turn_h(samp)

        def round_(act, t, dst, turned, rounded, free, at):
            r = rows(t)
            free(t - 2)
            for b in range(2):
                turned.wait(act, t, b)
                rounded.mark(nc.scalar.activation(cut(dst[:, t.p, b * 512:(b + 1) * 512], r), cut(bank[at + b][:, :], r), ACT.Copy))

        def split_(dve, t, hi, lo, rounded, split, at):
            r = rows(t)
            for b in range(2):
                rounded.wait(dve, t, b)
                sl = slice(b * 512, (b + 1) * 512)
                split.mark(nc.vector.tensor_tensor(cut(lo[:, t.p, sl], r), cut(bank[at + b][:, :], r), cut(hi[:, t.p, sl], r).bitcast(F32), ALU.subtract))

        @block.scalar
        def _(act):
            def round_o(t):
                round_(act, t, o_hi, o_turned, o_rounded, lambda u: proj.wait(act, u), 2)

            def round_h(t):
                round_(act, t, h_hi, h_turned, h_rounded, lambda u: h_out.wait(act, u), 4)

            def square_x(t):
                r = rows(t)
                added.wait(act, t)
                x_var.wait(act, t - 1)
                x_square.wait(act, t - 1)
                x_square.mark(nc.scalar.activation(square[0:r, :], x1[0:r, t.p, :], ACT.Square, accum_out=xss[0:r, :]))

            round_o(Tile(0, 0))
            w_scalar(act)

            def period(t):
                if not (isinstance(t.i, int) and t.c + 1 > NT):
                    round_o(t + 1)
                if not (isinstance(t.i, int) and t.c < 1):
                    round_h(t - 1)
                square_x(t)

            tiles_loop(act, period, 0, NT + 1)
            round_h(samp)

        @block.vector
        def _(dve):
            def split_o(t):
                split_(dve, t, o_hi, o_lo, o_rounded, o_split, 2)

            def split_h(t):
                split_(dve, t, h_hi, h_lo, h_rounded, h_split, 4)

            def add_x(t, g):
                r = rows(t)
                proj.wait(dve, t, g)
                if g == 0:
                    x_in.wait(dve, t)
                    x1_out.wait(dve, t - 2)
                at = slice(g * 512, (g + 1) * 512)
                added.mark(nc.vector.tensor_tensor(x1[0:r, t.p, at], bank[g][0:r, :], x[0:r, t.p, at], ALU.add))

            def norm_x(t):
                r = rows(t)
                x_square.wait(dve, t)
                x_rstd.wait(dve, t - 1)
                x_var.mark(nc.vector.tensor_scalar(xvar[0:r, :], xss[0:r, :], 1.0 / D, EPS, ALU.mult, ALU.add))
                x_rstd.wait(dve, t)
                h_turned.wait(dve, t - 1)
                x_normed.mark(nc.vector.scalar_tensor_tensor(hn[0:r, :], x1[0:r, t.p, :], xr[0:r, 0:1], norm_w[0:r, :],
                                                             ALU.mult, ALU.mult))

            split_o(Tile(0, 0))
            w_vector(dve)
            dve.wait_ge(norm_in, 16)
            dve.wait_ge(rows_turned, 1)
            nc.vector.tensor_copy(conv_cols[:, :], bank[6][:, 0:FC * (SB * (CW - 1) + CW + 1)]).then_inc(rows_kept, 1)

            def period(t):
                add_x(t, 0)
                if not (isinstance(t.i, int) and t.c + 1 > NT):
                    split_o(t + 1)
                add_x(t, 1)
                if not (isinstance(t.i, int) and t.c < 1):
                    split_h(t - 1)
                norm_x(t)

            tiles_loop(dve, period, 0, NT + 1)
            split_h(samp)

        @block.gpsimd
        def _(pool):
            def period(t):
                r = rows(t)
                x_normed.wait(pool, t - 1)
                x_var.wait(pool, t)
                x_rstd.mark(nc.gpsimd.tensor_tensor(xr[0:r, :], xvar[0:r, :], mhalf[0:r, 0:1], ALU.pow))

            tiles_loop(pool, period, 0, NT + 1)


def ffn(nc, ident, ins, outs, x1_dram, h2_dram, conv_cols, halo, conv_out, group):
    NP = FC // 2
    CC = SB * (CW - 1) + CW + 1
    base = group * (SEQ // 2)
    half = SEQ // 2
    blocks = [(0, 512), (512, 512)] if group == 0 else [(0, 384), (384, 384), (768, 320)]
    nb = len(blocks)
    TG = blocks[-1][0] + blocks[-1][1]
    sample = group == 1
    ntile = (TG + P - 1) // P
    items = [(j, g) for j in range(ntile) for g in range(2)]
    NI = len(items)
    ring = 4 if NI % 4 == 0 else 3
    with ExitStack() as ctx:
        k = Stage(nc, ctx, f"ffn{group}")
        h2 = k.sb("h2", [P, 2, KC, TG], F32R)
        acc = k.sb("acc", [P, ntile, D])
        act_hi = k.sb("act_hi", [P, 2, TG], F32R)
        act_lo = k.sb("act_lo", [P, 2, TG], F32R)
        raw = k.sb("raw", [P, TG])
        w_hi = k.sb("w_hi", [P, 2, 2, KC * P], F32R)
        w_lo = k.sb("w_lo", [P, 2, 2, KC * P], F32R)
        d_hi = k.sb("d_hi", [P, 2, D], F32R)
        d_lo = k.sb("d_lo", [P, 2, D], F32R)
        stage = k.sb("stage", [P, 2, D])
        gp = k.sb("gp", [P, half + CW - 1])
        gs = k.sb("gs", [P, SB, ST + CW - 1])
        t = k.sb("t", [P, 2, 512])
        cc = k.sb("cc", [P, 2, CC])
        bank = k.banks()

        h_in, acc_in, y_out = k.sem("h_in"), k.sem("acc_in"), k.sem("y_out")
        st_in = [k.sem("stage_in0"), k.sem("stage_in1")]
        w_rounded, w_split = k.sem("w_rounded"), k.sem("w_split")
        up = k.sem("up")
        down = k.sem("down")
        g_kept, t_made, silu = k.sem("g_kept"), k.sem("t_made"), k.sem("silu")
        taps, prod = k.sem("taps"), k.sem("prod")
        a_rounded, a_split = k.sem("a_rounded"), k.sem("a_split")
        added, cols_kept, kept_tail = k.sem("added"), k.sem("cols_kept"), k.sem("kept_tail")
        head_kept = k.sem("head_kept")
        rows_turned, rows_kept, rows_out = k.sem("rows_turned"), k.sem("rows_kept"), k.sem("rows_out")

        def at(sem, per):
            return lambda eng, i, s: wait(eng, sem, per * i + s + 1)

        B2 = 2 * nb
        w_up = at(up, 2 * B2)
        w_down = at(down, NI)
        w_g, w_t, w_silu, w_prod, w_aspl, w_arnd = (at(s, B2) for s in (g_kept, t_made, silu, prod, a_split, a_rounded))
        w_taps = at(taps, 2 * B2)
        w_added = at(added, NI)
        w_cols = at(cols_kept, 2)
        w_tail = at(kept_tail, 2)

        PIECES = 6

        def pieces(i, last):
            out = [(0, "w", 1, 0), (1, "w", 1, 1)]
            if not last:
                out += [(2, "w", 0, 0), (3, "w", 0, 1)]
            n = len(out)
            return out + [(n, "d", 0, 0), (n + 1, "d", 1, 0)]

        def rounds(eng, step):
            step(0)
            step(1)
            with eng.Fori(2, NP - 1) as i:
                step(i)
            step(NP - 1)

        block = ctx.enter_context(nc.Block())

        @block.sync
        def _(sp):
            def piece(i, pos, kind, x, part):
                n = PIECES * i + pos + 2
                wait(sp, w_split, n - 1)
                if kind == "w":
                    chunk = 2 * (i + (1 - x)) + x
                    src = ins["w_ffn_in"][0].rearrange("(c p) n -> p c n", p=P)[:, :, bass.ds(chunk * P + part * FF, P)]
                    dst = stage[:, pos % 2, :].rearrange("p (c n) -> p c n", c=KC)
                else:
                    src = ins["w_down"][0][bass.ds((2 * i + x) * P, P), :]
                    dst = stage[:, pos % 2, :]
                sp.dma_start(dst, src).then_inc(st_in[pos % 2], 16)

            piece(-1, 4, "w", 0, 0)
            piece(-1, 5, "w", 0, 1)
            for c in range(KC):
                for part in range(2):
                    sp.dma_start(h2[:, part, c, :].bitcast(F32), h2_dram[:, part, c, base:base + TG]).then_inc(h_in, 16)
            for j in range(ntile):
                r = min(P, TG - j * P)
                sp.dma_start(acc[0:r, j, :], x1_dram[base // P + j, 0:r, :]).then_inc(acc_in, 16)

            def step(i):
                for p_ in pieces(i, isinstance(i, int) and i == NP - 1):
                    piece(i, *p_)

            rounds(sp, step)
            for n, (j, g) in enumerate(items):
                if g == 0:
                    continue
                w_added(sp, NP - 1, n)
                if j * P < half:
                    dst = outs["y_prompt"][0, base + j * P:base + (j + 1) * P, :]
                    sp.dma_start(dst, acc[:, j, :]).then_inc(y_out, 16)
                else:
                    sp.dma_start(outs["y_sample"].rearrange("b t d -> (b t) d"), acc[0:NS, j, :]).then_inc(y_out, 16)
            if sample:
                for q in range(3):
                    sp.wait_ge(rows_kept, q + 1)
                    w_ = min(8, FC - 8 * q) * P
                    sl = slice(8 * q * P, 8 * q * P + w_)
                    sp.dma_start(outs["conv_prompt"][0, 0, :, sl], stage[0:CW - 1, q % 2, 0:w_]).then_inc(rows_out, 16)
                    sp.dma_start(outs["conv_sample"][0].rearrange("b c f -> (b c) f")[:, sl], stage[CW - 1:CC - 2, q % 2, 0:w_]).then_inc(rows_out, 16)
                    if q == 0:
                        sp.wait_ge(rows_out, 32)
                sp.wait_ge(rows_out, 96)
            sp.wait_ge(y_out, 16 * ntile)

        @block.tensor
        def _(pe):
            def gate_up(i, x):
                for b, (off, n) in enumerate(blocks):
                    kk = x * nb + b
                    for part in range(2):
                        if part == 0:
                            w_t(pe, i - (kk < 2), (kk - 2) % B2)
                        else:
                            w_prod(pe, i - (kk < 2), (kk - 2) % B2)
                        out = bank[2 * part + kk % 2][:, 0:n]
                        for c in range(KC):
                            sl = slice(c * P, (c + 1) * P)
                            ins_ = mm3(nc, out, w_hi[:, x, part, sl], w_lo[:, x, part, sl],
                                       h2[:, 0, c, off:off + n], h2[:, 1, c, off:off + n], c == 0, c == KC - 1)
                        ins_.then_inc(up, 1)

            def project_down(i):
                w_aspl(pe, i, B2 - 1)
                for n, (j, g) in enumerate(items):
                    r = min(P, TG - j * P)
                    bk = bank[4 + n % ring]
                    w_added(pe, i - (n < ring), (n - ring) % NI)
                    for x in range(2):
                        cs = slice(g * 512, (g + 1) * 512)
                        ins_ = mm3(nc, bk[0:r, :], act_hi[:, x, j * P:j * P + r], act_lo[:, x, j * P:j * P + r],
                                   d_hi[:, x, cs], d_lo[:, x, cs], x == 0, x == 1)
                    ins_.then_inc(down, 1)

            pe.wait_ge(h_in, 16 * 2 * KC)

            def step(i):
                wait(pe, w_split, PIECES * i + 2 if isinstance(i, int) and i == 0 else PIECES * i)
                gate_up(i, 0)
                if not (isinstance(i, int) and i == 0):
                    wait(pe, w_split, PIECES * i + 2)
                    project_down(i - 1)
                wait(pe, w_split, PIECES * i + 4)
                gate_up(i, 1)

            rounds(pe, step)
            wait(pe, w_split, PIECES * NP)
            project_down(NP - 1)
            if sample:
                pe.wait_ge(kept_tail, 2 * NP)
                for f in range(FC):
                    q = f // 8
                    bk = bank[(f % 8) // 4]
                    if f % 8 == 0:
                        wait(pe, rows_kept, q)
                    ins_ = nc.tensor.transpose(bk[0:CC - 2, (f % 4) * P:(f % 4 + 1) * P], conv_out[:, f * (CC - 2):(f + 1) * (CC - 2)], ident[:, :])
                    if f % 8 == 7 or f == FC - 1:
                        ins_.then_inc(rows_turned, 1)

        @block.scalar
        def _(act):
            def round_piece(i, pos, kind, x, part):
                n = PIECES * i + pos + 2
                act.wait_ge(st_in[pos % 2], 16 * (3 * i + 1 + pos // 2 + 1))
                if kind == "w" and x == 1:
                    w_up(act, i - 1, 2 * B2 - 1)
                elif kind == "w":
                    w_up(act, i, B2 - 1)
                else:
                    w_down(act, i - 1, NI - 1)
                dst = w_hi[:, x, part, :] if kind == "w" else d_hi[:, x, :]
                nc.scalar.activation(dst, stage[:, pos % 2, :], ACT.Copy).then_inc(w_rounded, 1)

            def post(i, x, b):
                off, n = blocks[b]
                kk = x * nb + b
                w_up(act, i, 2 * kk)
                w_cols(act, i, x)
                if b == 0:
                    w_taps(act, i - (x == 0), (2 * (kk - 1) + 1) % (2 * B2))
                    w_tail(act, i - (x == 0), (x - 1) % 2)
                src = bank[kk % 2]
                pn = min(n, half - off)
                ins_ = nc.scalar.activation(gp[:, CW - 1 + off:CW - 1 + off + pn], src[:, 0:pn], ACT.Copy)
                if pn < n:
                    ins_ = nc.scalar.activation(gs[:, :, CW - 1:], src[:, pn:n].rearrange("p (b t) -> p b t", t=ST), ACT.Copy)
                ins_.then_inc(g_kept, 1)
                w_prod(act, i - (kk < 2), (kk - 2) % B2)
                w_aspl_if(act, i, kk)
                nc.scalar.activation(t[:, kk % 2, 0:n], src[:, 0:n], ACT.Identity, scale=cc[:, x, CC - 2:CC - 1],
                                     bias=cc[:, x, CC - 1:CC]).then_inc(t_made, 1)
                w_taps(act, i, 2 * kk + 1)
                nc.scalar.activation(t[:, kk % 2, 0:n], t[:, kk % 2, 0:n], ACT.Silu).then_inc(silu, 1)

            def w_aspl_if(eng, i, kk):
                prev, step = i - (kk < 2), (kk - 2) % B2
                if step >= nb:
                    w_aspl(eng, prev, step)

            def round_a(i, x, b):
                off, n = blocks[b]
                w_prod(act, i, x * nb + b)
                w_down(act, i - 1, NI - 1)
                src = raw[:, off:off + n] if x == 0 else t[:, (nb + b) % 2, 0:n]
                nc.scalar.activation(act_hi[:, x, off:off + n], src, ACT.Copy).then_inc(a_rounded, 1)

            def first(pos, part):
                act.wait_ge(st_in[pos % 2], 16)
                nc.scalar.activation(w_hi[:, 0, part, :], stage[:, pos % 2, :], ACT.Copy).then_inc(w_rounded, 1)

            first(0, 0)
            first(1, 1)

            def step(i):
                ps = pieces(i, isinstance(i, int) and i == NP - 1)
                for b in range(nb):
                    post(i, 0, b)
                    if b < 2:
                        round_piece(i, *ps[b])
                if len(ps) == PIECES:
                    round_piece(i, *ps[2])
                    round_piece(i, *ps[3])
                for b in range(nb):
                    round_a(i, 0, b)
                round_piece(i, *ps[-2])
                post(i, 1, 0)
                round_a(i, 1, 0)
                round_piece(i, *ps[-1])
                for b in range(1, nb):
                    post(i, 1, b)
                    round_a(i, 1, b)

            rounds(act, step)

        @block.vector
        def _(dve):
            def split_piece(i, pos, kind, x, part):
                n = PIECES * i + pos + 2
                dve.wait_ge(w_rounded, n + 1)
                hi, lo = (w_hi[:, x, part, :], w_lo[:, x, part, :]) if kind == "w" else (d_hi[:, x, :], d_lo[:, x, :])
                nc.vector.tensor_tensor(lo, stage[:, pos % 2, :], hi.bitcast(F32), ALU.subtract).then_inc(w_split, 1)

            def columns(i, x):
                w_t(dve, i - 1, x * nb + nb - 1)
                w_taps(dve, i - 1, 2 * (x * nb + nb - 1) + 1)
                nc.vector.tensor_copy(cc[:, x, :], conv_cols[:, bass.ds((2 * i + x) * CC, CC)]).then_inc(cols_kept, 1)

            def heads(i, x):
                if sample:
                    w_cols(dve, i, x)
                    nc.vector.tensor_copy(gp[:, 0:CW - 1], halo[:, bass.ds((2 * i + x) * (CW - 1), CW - 1)])
                    ins_ = nc.vector.tensor_copy(gs[:, :, 0:CW - 1], cc[:, x, 0:SB * (CW - 1)].rearrange("p (b c) -> p b c", b=SB))
                    ins_.then_inc(head_kept, 1)
                    wait(dve, head_kept, 2 * i + x + 1)

            def tails(i, x):
                w_g(dve, i, x * nb + nb - 1)
                f = 2 * i + x
                if sample:
                    nc.vector.tensor_copy(conv_out[:, bass.ds(f * (CC - 2), CW - 1)], gp[:, half:half + CW - 1])
                    nc.vector.tensor_copy(conv_out[:, bass.ds(f * (CC - 2) + CW - 1, SB * (CW - 1))].rearrange("p (b c) -> p b c", b=SB),
                                          gs[:, :, ST:ST + CW - 1]).then_inc(kept_tail, 1)
                else:
                    nc.vector.tensor_copy(halo[:, bass.ds(f * (CW - 1), CW - 1)], gp[:, half:half + CW - 1]).then_inc(kept_tail, 1)

            def post(i, x, b):
                off, n = blocks[b]
                kk = x * nb + b
                if b == 0:
                    heads(i, x)
                pn = min(n, half - off)
                tb = t[:, kk % 2, 0:n]
                w_t(dve, i, kk)
                for s in (1, 2):
                    col = cc[:, x, CC - 2 - s:CC - 1 - s]
                    ins_ = nc.vector.scalar_tensor_tensor(tb[:, 0:pn], gp[:, CW - 1 + off - s:CW - 1 + off - s + pn], col, tb[:, 0:pn], ALU.mult, ALU.add)
                    if pn < n:
                        ts = tb[:, pn:n].rearrange("p (b t) -> p b t", t=ST)
                        ins_ = nc.vector.scalar_tensor_tensor(ts, gs[:, :, CW - 1 - s:CW - 1 - s + ST], col, ts, ALU.mult, ALU.add)
                    ins_.then_inc(taps, 1)
                    w_taps(dve, i, 2 * kk + s - 1)
                if b == nb - 1:
                    tails(i, x)
                w_silu(dve, i, kk)
                w_up(dve, i, 2 * kk + 1)
                dst = raw[:, off:off + n] if x == 0 else tb
                nc.vector.tensor_tensor(dst, tb, bank[2 + kk % 2][:, 0:n], ALU.mult).then_inc(prod, 1)

            def split_a(i, x, b):
                off, n = blocks[b]
                w_arnd(dve, i, x * nb + b)
                src = raw[:, off:off + n] if x == 0 else t[:, (nb + b) % 2, 0:n]
                nc.vector.tensor_tensor(act_lo[:, x, off:off + n], src, act_hi[:, x, off:off + n].bitcast(F32), ALU.subtract).then_inc(a_split, 1)

            def add(i, n):
                j, g = items[n]
                r = min(P, TG - j * P)
                w_down(dve, i, n)
                sl = acc[0:r, j, g * 512:(g + 1) * 512]
                nc.vector.tensor_tensor(sl, bank[4 + n % ring][0:r, :], sl, ALU.add).then_inc(added, 1)

            if not sample:
                nc.vector.memset(gp[:, 0:CW - 1], 0.0).then_inc(head_kept, 1)
                dve.wait_ge(head_kept, 1)

            def first(pos, part):
                dve.wait_ge(w_rounded, pos + 1)
                nc.vector.tensor_tensor(w_lo[:, 0, part, :], stage[:, pos % 2, :], w_hi[:, 0, part, :].bitcast(F32), ALU.subtract).then_inc(w_split, 1)

            first(0, 0)
            first(1, 1)
            dve.wait_ge(acc_in, 16 * ntile)

            def step(i):
                ps = pieces(i, isinstance(i, int) and i == NP - 1)
                columns(i, 0)
                columns(i, 1)
                for b in range(nb):
                    post(i, 0, b)
                    if b < 2:
                        split_piece(i, *ps[b])
                if not (isinstance(i, int) and i == 0):
                    for n in range(NI):
                        if n in (6, 12) and len(ps) == PIECES:
                            split_piece(i, *ps[n // 6 + 1])
                        add(i - 1, n)
                elif len(ps) == PIECES:
                    split_piece(i, *ps[2])
                    split_piece(i, *ps[3])
                for b in range(nb):
                    split_a(i, 0, b)
                split_piece(i, *ps[-2])
                post(i, 1, 0)
                split_a(i, 1, 0)
                split_piece(i, *ps[-1])
                for b in range(1, nb):
                    post(i, 1, b)
                    split_a(i, 1, b)

            rounds(dve, step)
            for n in range(NI):
                add(NP - 1, n)
            if sample:
                for q in range(3):
                    dve.wait_ge(rows_turned, q + 1)
                    if q == 2:
                        dve.wait_ge(rows_out, 32)
                    left = min(8, FC - 8 * q) * P
                    for bk in range((left + 511) // 512):
                        w_ = min(512, left - bk * 512)
                        ins_ = nc.vector.tensor_copy(stage[0:CC - 2, q % 2, bk * 512:bk * 512 + w_], bank[bk][0:CC - 2, 0:w_])
                    ins_.then_inc(rows_kept, 1)


def constant_buffers(nc, ctx):
    def sb(name, shape):
        return ctx.enter_context(nc.sbuf_tensor(name, shape, F32))

    names = {
        "mask": [P, 4 * P], "cap": [P, P], "cap64": [NS, NS], "sel_head": [MH, MH * P], "sel_t": [ST, P],
        "sel_j": [GQ, P], "mask_s8": [ST, WIN + ST], "blk": [NS, SB], "ones": [P, P],
        "norm_mix": [P, D], "ml_norm": [P, MLV], "q_norm": [P, HD], "k_norm": [P, HD],
        "sinks": [P, HQ], "bias_i": [MH, 1], "bias_f": [MH, 1], "sink_rows": [GQ, HKV],
    }
    return {n: sb(n, shape) for n, shape in names.items()}


def trunk_step(nc, ins, outs, h_dram, o_dram, x1_dram, h2_dram):
    rows = SB * (CW - 1)
    with ExitStack() as outer:
        def kept(name, shape):
            return outer.enter_context(nc.sbuf_tensor(name, shape, F32))

        ident = kept("ident", [P, P])
        mhalf = kept("mhalf", [P, HQ + HKV])
        with ExitStack() as inner:
            C = constant_buffers(nc, inner)
            C["ident"], C["mhalf"] = ident, mhalf
            constants(nc, C, ins)
            attention(nc, C, ins, outs, h_dram, o_dram)
            mlstm(nc, C, ins, outs, h_dram, o_dram)
        conv_cols = kept("conv_cols", [P, FC * (rows + CW + 1)])
        halo = kept("halo", [P, FC * (CW - 1)])
        conv_out = kept("conv_out", [P, FC * (CW - 1 + rows)])
        output(nc, ident, mhalf, ins, o_dram, x1_dram, h2_dram, conv_cols)
        for group in range(2):
            ffn(nc, ident, ins, outs, x1_dram, h2_dram, conv_cols, halo, conv_out, group)


_INS = ["x_prompt", "x_sample", "cache_attn_k", "cache_attn_v", "state_mlstm_C", "state_mlstm_n", "state_mlstm_m",
        "cache_ffn_conv", "norm_mix_w", "w_in", "b_gates", "q_norm_w", "k_norm_w", "sinks", "ml_norm_w", "w_out",
        "norm_ffn_w", "w_ffn_in", "conv_w", "conv_b", "w_down"]
_OUTS = [("y_prompt", (1, SEQ, D)), ("y_sample", (SB, ST, D)),
         ("k_prompt", (1, 1, WIN, HKV, HD)), ("v_prompt", (1, 1, WIN, HKV, HD)),
         ("C_prompt", (1, 1, MH, MV, MQK)), ("n_prompt", (1, 1, MH, MQK)), ("m_prompt", (1, 1, MH)),
         ("conv_prompt", (1, 1, CW - 1, FF)),
         ("k_sample", (1, SB, WIN, HKV, HD)), ("v_sample", (1, SB, WIN, HKV, HD)),
         ("C_sample", (1, SB, MH, MV, MQK)), ("n_sample", (1, SB, MH, MQK)), ("m_sample", (1, SB, MH)),
         ("conv_sample", (1, SB, CW - 1, FF))]


def kernel(**inputs):
    import numpy as _np
    import concourse.bacc as _bacc
    from concourse import mybir as _mybir
    from concourse.bass_utils import run_bass_kernel_spmd as _run

    nc = _bacc.Bacc("TRN2", target_bir_lowering=False, num_devices=1)
    arrays, args, results = {}, [], []
    for name in _INS:
        a = _np.ascontiguousarray(inputs[name])
        arrays[f"in_{name}_dram"] = a
        args.append(nc.dram_tensor(f"in_{name}_dram", a.shape, _mybir.dt.from_np(a.dtype), kind="ExternalInput").ap())
    for name, shape in _OUTS:
        results.append(nc.dram_tensor(f"out_{name}_dram", shape, F32, kind="ExternalOutput").ap())
    h_dram = nc.dram_tensor("h_parts", (NT + 1, P, 2, D), F32, kind="Internal").ap()
    o_dram = nc.dram_tensor("mixed", (SEQ + NS, D), F32, kind="Internal").ap()
    x1_dram = nc.dram_tensor("x1", (NT + 1, P, D), F32, kind="Internal").ap()
    h2_dram = nc.dram_tensor("h2_parts", (P, 2, KC, SEQ + NS), F32, kind="Internal").ap()
    trunk_step(nc, dict(zip(_INS, args)), {n: r for (n, _), r in zip(_OUTS, results)}, h_dram, o_dram, x1_dram, h2_dram)
    r = _run(nc, [arrays], core_ids=[0])
    return tuple(r.results[0][f"out_{name}_dram"] for name, _ in _OUTS)
```

```python
from contextlib import ExitStack

import concourse.bass as bass
from concourse import mybir

F32 = mybir.dt.float32
F32R = mybir.dt.float32r
ALU = mybir.AluOpType
ACT = mybir.ActivationFunctionType
AX = mybir.AxisListType.X

P = 128
D = 1024
KC = D // P
SEQ = 2048
NT = SEQ // P
SB, ST = 8, 8
NS = SB * ST
HQ, HKV, HD = 8, 2, 64
GQ = HQ // HKV
WIN = 128
MH, MQK, MV = 4, 64, 128
MVE = MV + 1
FF = 2816
FC = FF // P
CW = 3
EPS = 1e-6
ATT_SCALE = HD ** -0.5
ML_SCALE = MQK ** -0.5
NEG = -1.0e30
ATT_W = HQ * HD + 2 * HKV * HD
QW = HQ * HD
KVW = HKV * HD
MLQ = MH * MQK
MLV = MH * MV
ML_W = 2 * MH + 2 * MLQ + 2 * MLV
IN_W = ATT_W + ML_W


class Tile:

    def __init__(self, i, c):
        self.i, self.c, self.p = i, c, c % 2

    @property
    def n(self):
        return 2 * self.i + self.c

    @property
    def h(self):
        return self.i + self.c // 2

    def __add__(self, k):
        return Tile(self.i, self.c + k)

    def __sub__(self, k):
        return Tile(self.i, self.c - k)


def wait(eng, sem, value):
    if isinstance(value, int) and value <= 0:
        return
    eng.wait_ge(sem, value)


class Steps:

    def __init__(self, sem, per=1):
        self.sem, self.per = sem, per

    def mark(self, ins):
        ins.then_inc(self.sem, 1)

    def wait(self, eng, tile, step=None):
        step = self.per - 1 if step is None else step
        wait(eng, self.sem, self.per * tile.n + step + 1)


class Landed:

    def __init__(self, sems, per=1):
        self.sems, self.per = sems, per

    def mark(self, dma, tile):
        dma.then_inc(self.sems[tile.p], 16)

    def wait(self, eng, tile):
        wait(eng, self.sems[tile.p], 16 * self.per * (tile.h + 1))


def mm3(nc, out, a_hi, a_lo, b_hi, b_lo, first, last):
    nc.tensor.matmul(out, a_hi, b_hi, start=first, stop=False)
    nc.tensor.matmul(out, a_hi, b_lo, start=False, stop=False)
    return nc.tensor.matmul(out, a_lo, b_hi, start=False, stop=last)


class Stage:

    def __init__(self, nc, ctx, tag):
        self.nc, self.ctx, self.tag, self.sems = nc, ctx, tag, []
        ctx.callback(self.clear)

    def clear(self):
        self.nc.clear_and_free_semaphores(self.sems)
        self.nc.all_engine_barrier()

    def sb(self, name, shape, dt=F32):
        return self.ctx.enter_context(self.nc.sbuf_tensor(f"{self.tag}_{name}", shape, dt))

    def sem(self, name):
        self.sems.append(self.nc.alloc_semaphore(name=f"{self.tag}_{name}"))
        return self.sems[-1]

    def steps(self, name, per=1):
        return Steps(self.sem(name), per)

    def landed(self, name, per=1):
        return Landed([self.sem(f"{name}0"), self.sem(f"{name}1")], per)

    def banks(self):
        return [self.ctx.enter_context(self.nc.psum_tensor(f"{self.tag}_bank{b}", [P, 512], F32)) for b in range(8)]


def tiles_loop(eng, step, first, last, peel=14):
    for t in range(first, 2):
        step(Tile(0, t))
    with eng.Fori(1, peel // 2) as i:
        for c in range(2):
            step(Tile(i, c))
    for t in range(peel, last):
        step(Tile(0, t))


class Weight:

    def __init__(self, keep, name, width):
        self.width, self.at = width, 0
        at = (keep.nc.sbuf_base + 31) // 32 * 32
        raw = keep.sb(f"{name}_raw", [P, KC * width])
        self.raw = raw[:, :].rearrange("p (c n) -> p c n", c=KC)
        self.lo_buf = keep.nc.alloc_sbuf_tensor_at(f"{keep.tag}_{name}_lo", [P, KC * width], F32R, offset=at)
        self.lo = self.lo_buf[:, :].rearrange("p (c n) -> p c n", c=KC)
        self.landed = [keep.sem(f"{name}_landed{n}") for n in range(KC // 2)]

    def load(self, sp, columns):
        self.loads = 2 * 16 * len(columns)
        for c in range(KC):
            at = 0
            for src in columns:
                n = src.shape[-1]
                sp.dma_start(self.raw[:, c, at:at + n], src[c * P:(c + 1) * P, :]).then_inc(self.landed[c // 2], 16)
                at += n

    def use(self, k, name):
        self.hi_buf = k.sb(f"{name}_hi", [P, KC * self.width], F32R)
        self.hi = self.hi_buf[:, :].rearrange("p (c n) -> p c n", c=KC)
        self.rounded, self.split = k.sem(f"{name}_rounded"), k.sem(f"{name}_split")

    def round(self, nc, act):
        for c in range(KC):
            act.wait_ge(self.landed[c // 2], self.loads)
            nc.scalar.activation(self.hi[:, c, :], self.raw[:, c, :], ACT.Copy).then_inc(self.rounded, 1)

    def subtract(self, nc, dve):
        for c in range(KC):
            dve.wait_ge(self.rounded, c + 1)
            nc.vector.tensor_tensor(self.lo[:, c, :], self.raw[:, c, :], self.hi[:, c, :].bitcast(F32),
                                    ALU.subtract).then_inc(self.split, 1)


def constants(nc, C, ins, load_ahead):
    with ExitStack() as ctx:
        k = Stage(nc, ctx, "const")
        built, landed = k.sem("built"), k.sem("landed")
        block = ctx.enter_context(nc.Block())

        @block.sync
        def _(sp):
            n = 0
            for dst, src in (
                (C["norm_mix"], ins["norm_mix_w"][0:1, :].partition_broadcast(P)),
                (C["ml_norm"], ins["ml_norm_w"][0:1, :].partition_broadcast(P)),
                (C["q_norm"], ins["q_norm_w"][0:1, :].partition_broadcast(P)),
                (C["k_norm"], ins["k_norm_w"][0:1, :].partition_broadcast(P)),
                (C["sinks"], ins["sinks"][0:1, :].partition_broadcast(P)),
            ):
                sp.dma_start(dst[:, :], src).then_inc(landed, 16)
                n += 16
            with nc.allow_non_contiguous_dma(reason="a few gate biases and sinks"):
                for g, dst in enumerate((C["bias_i"], C["bias_f"])):
                    sp.dma_start(dst[0:MH, :], ins["b_gates"][0, g * MH:(g + 1) * MH].rearrange("(h a) -> h a", a=1)).then_inc(landed, 16)
                    n += 16
                sp.dma_start(C["sink_rows"][0:GQ, :], ins["sinks"][0, :].rearrange("(k j) -> j k", j=GQ)).then_inc(landed, 16)
                n += 16
            load_ahead(sp)
            sp.wait_ge(landed, n)

        @block.gpsimd
        def _(pool):
            count = [0]

            def done(ins_):
                count[0] += 1
                ins_.then_inc(built, 1)

            def select(out, pattern, base, mult, fill, op=ALU.not_equal, in_=None):
                pool.wait_ge(built, count[0])
                done(nc.gpsimd.affine_select(out=out, in_=out if in_ is None else in_, compare_op=op, fill=fill,
                                             base=base, pattern=pattern, channel_multiplier=mult))

            zeroed = (C["ident"], C["mask"], C["cap"], C["sel_head"], C["sel_t"], C["sel_j"], C["mask_s8"], C["blk"])
            for buf in zeroed:
                done(nc.gpsimd.memset(buf[:], 0.0))
            done(nc.gpsimd.memset(C["ones"][:], 1.0))
            done(nc.gpsimd.memset(C["mhalf"][:], -0.5))
            done(nc.gpsimd.memset(C["cap64"][:], 0.0))
            select(C["ident"][:, :], [[-1, P]], 0, 1, 1.0)
            mask = C["mask"][:, :].rearrange("p (h b s) -> p h b s", h=2, b=2)
            for h in range(2):
                select(mask[:, h, 0, :], [[1, P]], 0, -1, NEG, op=ALU.is_gt)
                select(mask[:, h, 1, :], [[-1, P]], 0, 1, NEG, op=ALU.is_ge)
            select(C["cap"][:, :], [[1, P]], 0, -1, NEG, op=ALU.is_ge)
            cap64 = C["cap64"][:, :].rearrange("p (b t) -> p b t", t=ST)
            select(cap64, [[ST, SB], [1, ST]], 0, -1, NEG, op=ALU.is_ge)
            select(cap64, [[-ST, SB], [0, ST]], 0, 1, NEG, op=ALU.is_ge)
            select(C["sel_head"][:, :].rearrange("k (h p) -> k h p", h=MH), [[-1, MH], [0, P]], 0, 1, 1.0)
            select(C["sel_t"][:, :].rearrange("k (b t) -> k b t", t=ST), [[0, P // ST], [-1, ST]], 0, 1, 1.0)
            select(C["sel_j"][:, :].rearrange("k (a j t) -> k a j t", j=GQ, t=ST), [[0, P // 32], [-1, GQ], [0, ST]], 0, 1, 1.0)
            select(C["mask_s8"][:, :], [[1, WIN + ST]], 0, -1, NEG, op=ALU.is_gt)
            select(C["mask_s8"][:, :], [[-1, WIN + ST]], WIN, 1, NEG, op=ALU.is_ge)
            select(C["blk"][:, :], [[-ST, SB]], 0, 1, 0.0, op=ALU.is_ge, in_=C["ones"][0:NS, 0:SB])
            select(C["blk"][:, :], [[ST, SB]], ST - 1, -1, 0.0, op=ALU.is_ge)
            pool.wait_ge(built, count[0])


def attention(nc, C, ins, outs, h_dram, o_dram, w, load_ahead):
    with ExitStack() as ctx:
        k = Stage(nc, ctx, "att")
        w.use(k, "w")
        x = k.sb("x", [P, 2, D])
        square = k.sb("square", [P, D])
        hn = k.sb("hn", [P, D])
        h_hi = k.sb("h_hi", [P, 2, D], F32R)
        h_lo = k.sb("h_lo", [P, 2, D], F32R)
        z = k.sb("z", [P, 2, ATT_W])
        zz = k.sb("zz", [P, QW + KVW])
        xss = k.sb("xss", [P, 2])
        xvar = k.sb("xvar", [P, 1])
        xr = k.sb("xr", [P, 1])
        qss = k.sb("qss", [P, HQ + HKV])
        qvar = k.sb("qvar", [P, HQ + HKV])
        qr = k.sb("qr", [P, HQ + HKV])
        qu = k.sb("qu", [P, QW + KVW])
        qn = k.sb("qn", [P, QW])
        kn = k.sb("kn", [P, KVW])
        v = k.sb("v", [P, 2, KVW])
        qT = k.sb("qT", [P, QW])
        kT = k.sb("kT", [P, 2, P])
        s = k.sb("s", [P, HQ * 2 * P])
        pT = k.sb("pT", [P, HQ * 2 * P])
        smax = k.sb("smax", [P, HQ])
        m = k.sb("m", [P, HQ])
        neg_m = k.sb("neg_m", [P, HQ])
        sink_m = k.sb("sink_m", [P, HQ])
        esink = k.sb("esink", [P, HQ])
        ssum = k.sb("ssum", [P, HQ])
        den = k.sb("den", [P, HQ])
        rden = k.sb("rden", [P, HQ])
        o = k.sb("o", [P, 2, QW])
        ck = k.sb("ck", [P, SB, KVW])
        cv = k.sb("cv", [P, SB, KVW])
        ckT = k.sb("ckT", [P, SB, WIN + ST])
        vnew = k.sb("vnew", [ST, SB, KVW])
        qTs = k.sb("qTs", [P, SB, GQ * ST])
        mask_s = k.sb("mask_s", [P, WIN + ST])
        sink_s = k.sb("sink_s", [P, HKV])
        ss = k.sb("ss", [P, 4, WIN + ST])
        stat = k.sb("stat", [P, 8, 4])
        psT = k.sb("psT", [P, 4, P])
        psnT = k.sb("psnT", [ST, 4, P])
        os_ = k.sb("os", [P, 4, HD])
        bank = k.banks()
        h_bank = (bank[2], bank[0])

        x_in = k.landed("x_in")
        x_square = k.steps("x_square")
        x_var = k.steps("x_var")
        x_rstd = k.steps("x_rstd")
        x_normed = k.steps("x_normed")
        h_turned = k.steps("h_turned", 2)
        h_rounded = k.steps("h_rounded", 2)
        h_split = k.steps("h_split", 2)
        h_out = k.landed("h_out", 2)
        proj = k.steps("proj", 2)
        z_ready = k.steps("z_ready", 2)
        z_square = k.steps("z_square")
        z_sum = k.steps("z_sum")
        z_var = k.steps("z_var")
        z_rstd = k.steps("z_rstd")
        z_scaled = k.steps("z_scaled")
        qk_normed = k.steps("qk_normed", 2)
        v_kept = k.steps("v_kept")
        qk_turned = k.steps("qk_turned", 2)
        q_kept = k.steps("q_kept")
        k_kept = k.steps("k_kept")
        scored = k.steps("scored", 4)
        masked = k.steps("masked", 4)
        s_stats = k.steps("s_stats", 8)
        s_exp = k.steps("s_exp", 2)
        s_den = k.steps("s_den", 2)
        p_turned = k.steps("p_turned", 4)
        p_kept_a = k.steps("p_kept_a", 2)
        p_kept_v = k.steps("p_kept_v", 2)
        pv = k.steps("pv")
        o_ready = k.steps("o_ready")
        o_out = k.landed("o_out")
        k_out, v_out = k.sem("k_out"), k.sem("v_out")

        def rows(t):
            return NS if t.c == NT else P

        samp = Tile(0, NT)
        s_in, sT_done, s_mask, s_keep, s_score, s_dve, s_act, s_turn, s_pv, s_os = (
            k.sem(n) for n in ("s_in", "s_turned", "s_mask", "s_keep", "s_score", "s_dve", "s_act", "s_turn", "s_pv", "s_os"))
        s_vnew, s_out = k.sem("s_vnew"), k.sem("s_out")

        def store_os(eng, kv):
            for bq in range(2):
                for b4 in range(4):
                    tok = SEQ + (bq * 4 + b4) * ST
                    eng.dma_start(o_dram[tok:tok + ST, kv * GQ * HD:(kv + 1) * GQ * HD].rearrange("t (j d) -> j t d", j=GQ),
                                  os_[b4 * 32:(b4 + 1) * 32, 2 * kv + bq, :]).then_inc(s_out, 16)

        block = ctx.enter_context(nc.Block())

        @block.sync
        def _(sp):
            def load_x(t):
                x_normed.wait(sp, t - 2)
                if t.c == NT:
                    x_in.mark(sp.dma_start(x[0:NS, t.p, :], ins["x_sample"].rearrange("b t d -> (b t) d")), t)
                else:
                    x_in.mark(sp.dma_start(x[:, t.p, :], ins["x_prompt"][0, bass.ds(t.n * P, P), :]), t)

            def store_h(t):
                h_split.wait(sp, t)
                if t.c == NT:
                    for part, src in ((0, h_hi), (1, h_lo)):
                        h_out.mark(sp.dma_start(h_dram[NT, :, part, :].rearrange("p (c r) -> p c r", c=KC)[:, :, 0:NS],
                                                src[:, t.p, :].bitcast(F32).rearrange("p (c r) -> p c r", c=KC)[:, :, 0:NS]), t)
                    return
                h_out.mark(sp.dma_start(h_dram[bass.ds(t.n, 1), :, 0, :].rearrange("a p n -> (a p) n"), h_hi[:, t.p, :].bitcast(F32)), t)
                h_out.mark(sp.dma_start(h_dram[bass.ds(t.n, 1), :, 1, :].rearrange("a p n -> (a p) n"), h_lo[:, t.p, :].bitcast(F32)), t)

            def store_o(t):
                o_ready.wait(sp, t)
                o_out.mark(sp.dma_start(o_dram[bass.ds(t.n * P, P), 0:QW], o[:, t.p, :]), t)

            load_x(Tile(0, 0))
            load_x(Tile(0, 1))
            sp.dma_start(ck[:, :, :], ins["cache_attn_k"][0].rearrange("b s k d -> s b (k d)")).then_inc(s_in, 16)
            sp.dma_start(cv[:, :, :], ins["cache_attn_v"][0].rearrange("b s k d -> s b (k d)")).then_inc(s_in, 16)
            for b_ in range(SB):
                for cache, out in ((ins["cache_attn_k"], outs["k_sample"]), (ins["cache_attn_v"], outs["v_sample"])):
                    sp.dma_start(out[0, b_, 0:WIN - ST].rearrange("s k d -> s (k d)"),
                                 cache[0, b_, ST:WIN].rearrange("s k d -> s (k d)")).then_inc(s_out, 16)
            store_h(Tile(0, 0))
            load_ahead(sp)

            def period(t):
                if not (isinstance(t.i, int) and t.c + 2 > NT):
                    load_x(t + 2)
                store_h(t + 1)
                if not (isinstance(t.i, int) and t.c < 2):
                    store_o(t - 2)

            tiles_loop(sp, period, 0, NT)
            store_o(Tile(0, NT - 2))
            store_o(Tile(0, NT - 1))
            last = Tile(0, NT - 1)
            v_kept.wait(sp, last)
            sp.dma_start(outs["v_prompt"][0, 0].rearrange("s k d -> s (k d)"), v[:, last.p, :]).then_inc(v_out, 16)
            z_ready.wait(sp, samp)
            for b_ in range(SB):
                rows_b = z[b_ * ST:(b_ + 1) * ST, samp.p, QW + KVW:ATT_W]
                sp.dma_start(vnew[:, b_, :], rows_b).then_inc(s_vnew, 16)
                sp.dma_start(outs["v_sample"][0, b_, WIN - ST:WIN].rearrange("s k d -> s (k d)"), rows_b).then_inc(s_out, 16)
            qk_normed.wait(sp, samp)
            for b_ in range(SB):
                sp.dma_start(outs["k_sample"][0, b_, WIN - ST:WIN].rearrange("s k d -> s (k d)"),
                             kn[b_ * ST:(b_ + 1) * ST, :]).then_inc(s_out, 16)
            sp.wait_ge(s_os, 1)
            store_os(sp, 0)
            sp.wait_ge(s_out, 16 * (2 * SB + 2 * SB + 4 * 4))
            sp.wait_ge(k_out, 16)
            sp.wait_ge(v_out, 16)
            h_out.wait(sp, samp)
            h_out.wait(sp, samp - 1)
            o_out.wait(sp, last)
            o_out.wait(sp, last - 1)

        @block.tensor
        def _(pe):
            def turn_h(t):
                r = rows(t)
                x_normed.wait(pe, t)
                for b in range(2):
                    if b == 0:
                        q_kept.wait(pe, t - 2)
                    elif not (isinstance(t.i, int) and t.c < 2):
                        z_ready.wait(pe, t - 1, 0)
                    h_split.wait(pe, t - 1, b)
                    for c in range(4):
                        ins_ = nc.tensor.transpose(h_bank[b][:, c * P:c * P + r],
                                                   hn[0:r, (b * 4 + c) * P:(b * 4 + c + 1) * P], C["ident"][0:r, 0:r])
                    h_turned.mark(ins_)

            def project(t, g):
                r = rows(t)
                lo, hi = ((0, QW), (QW, ATT_W))[g]
                if g == 0:
                    h_split.wait(pe, t)
                z_ready.wait(pe, t - 1, g)
                for c in range(KC):
                    if isinstance(t.i, int) and t.c == 0 and g == 0:
                        pe.wait_ge(w.split, c + 1)
                    a = slice(c * P, c * P + r)
                    ins_ = mm3(nc, bank[g][0:r, 0:hi - lo], h_hi[:, t.p, a], h_lo[:, t.p, a],
                               w.hi[:, c, lo:hi], w.lo[:, c, lo:hi], c == 0, c == KC - 1)
                proj.mark(ins_)

            def turn_p(t, first=False):
                for b in range(4):
                    s_exp.wait(pe, t, b // 2)
                    for hh in range(2):
                        h = 2 * b + hh
                        for part in ((1,) if first else (0, 1)):
                            at = hh * 256 + part * P
                            ins_ = nc.tensor.transpose(bank[4 + b][:, at:at + P],
                                                       s[:, h * 256 + part * P:h * 256 + (part + 1) * P], C["ident"][:, :])
                    p_turned.mark(ins_)

            def turn_qk(t):
                r = rows(t)
                qk_normed.wait(pe, t)
                h_split.wait(pe, t + 1, 1)
                for j in range(GQ):
                    ins_ = nc.tensor.transpose(bank[2][:, j * P:j * P + r], qn[0:r, j * P:(j + 1) * P], C["ident"][0:r, 0:r])
                qk_turned.mark(ins_)
                o_ready.wait(pe, t - 2)
                qk_turned.mark(nc.tensor.transpose(bank[3][:, 0:r], kn[0:r, :], C["ident"][0:r, 0:r]))

            def values(t, first=False):
                p_kept_a.wait(pe, t)
                p_kept_v.wait(pe, t)
                v_kept.wait(pe, t)
                k_kept.wait(pe, t + 1)
                for h in range(HQ):
                    kv = h // GQ
                    if not first:
                        nc.tensor.matmul(bank[3][:, h * HD:(h + 1) * HD], pT[:, h * 256:h * 256 + P],
                                         v[:, 1 - t.p, kv * HD:(kv + 1) * HD], start=True, stop=False)
                    ins_ = nc.tensor.matmul(bank[3][:, h * HD:(h + 1) * HD], pT[:, h * 256 + P:(h + 1) * 256],
                                            v[:, t.p, kv * HD:(kv + 1) * HD], start=first, stop=True)
                pv.mark(ins_)

            def scores(t, first=False):
                q_kept.wait(pe, t)
                k_kept.wait(pe, t)
                for b in range(4):
                    if b < 2:
                        p_kept_a.wait(pe, t - 1, b)
                    else:
                        p_kept_v.wait(pe, t - 1, b - 2)
                    for hh in range(2):
                        h = 2 * b + hh
                        half, j = h // GQ, h % GQ
                        part = slice(half * HD, (half + 1) * HD)
                        for pr in ((1,) if first else (0, 1)):
                            keys = kT[part, t.p if pr else 1 - t.p, :]
                            ins_ = nc.tensor.matmul(bank[4 + b][:, hh * 256 + pr * P:hh * 256 + (pr + 1) * P],
                                                    qT[part, j * P:(j + 1) * P], keys, start=True, stop=True)
                    scored.mark(ins_)

            turn_h(Tile(0, 0))
            turn_h(Tile(0, 1))
            h_split.wait(pe, Tile(0, 1))
            project(Tile(0, 0), 0)
            project(Tile(0, 0), 1)

            def period(t):
                static = isinstance(t.i, int)
                project(t + 1, 0)
                turn_qk(t)
                if not (static and t.c == 0):
                    turn_p(t - 1, first=static and t.c == 1)
                project(t + 1, 1)
                if not (static and t.c + 2 > NT):
                    turn_h(t + 2)
                if not (static and t.c == 0):
                    values(t - 1, first=static and t.c == 1)
                scores(t, first=static and t.c == 0)

            tiles_loop(pe, period, 0, NT)
            last = Tile(0, NT - 1)
            turn_p(last)
            qk_normed.wait(pe, samp)
            o_ready.wait(pe, last - 1)
            for j in range(GQ):
                ins_ = nc.tensor.transpose(bank[2][:, j * P:j * P + NS], qn[0:NS, j * P:(j + 1) * P], C["ident"][0:NS, 0:NS])
            qk_turned.mark(ins_)
            qk_turned.mark(nc.tensor.transpose(bank[3][:, 0:NS], kn[0:NS, :], C["ident"][0:NS, 0:NS]))
            values(last)
            pe.wait_ge(s_in, 32)
            for b in range(2):
                z_ready.wait(pe, samp, b)
                for c in range(4):
                    ins_ = nc.tensor.transpose(bank[b][:, c * P:(c + 1) * P], ck[:, b * 4 + c, :], C["ident"][:, :])
                ins_.then_inc(sT_done, 1)
            p_kept_v.wait(pe, last)
            nc.tensor.matmul(bank[7][:, 0:WIN + ST], C["sel_t"][:, :], C["mask_s8"][:, :], start=True, stop=True)
            nc.tensor.matmul(bank[7][:, 256:256 + HKV], C["sel_j"][:, :], C["sink_rows"][:, :], start=True, stop=True).then_inc(s_mask, 1)
            pe.wait_ge(s_keep, 5)
            p_kept_a.wait(pe, last)
            for g in range(4):
                kv, bq = g // 2, g % 2
                part = slice(kv * HD, (kv + 1) * HD)
                for b4 in range(4):
                    ins_ = nc.tensor.matmul(bank[4 + kv][b4 * 32:(b4 + 1) * 32, bq * 256:bq * 256 + WIN + ST],
                                            qTs[part, bq * 4 + b4, :], ckT[part, bq * 4 + b4, :], start=True, stop=True)
            ins_.then_inc(s_score, 1)
            pe.wait_ge(s_act, 6)
            pe.wait_ge(s_keep, 7)
            for g in range(4):
                nc.tensor.transpose(bank[6][:, g * P:(g + 1) * P], ss[:, g, 0:WIN], C["ident"][:, :])
                ins_ = nc.tensor.transpose(bank[7][0:ST, g * P:(g + 1) * P], ss[:, g, WIN:WIN + ST], C["ident"][:, :])
            ins_.then_inc(s_turn, 1)
            pe.wait_ge(s_dve, 9)
            pe.wait_ge(s_vnew, 16 * SB)
            o_ready.wait(pe, last)
            for g in range(4):
                kv, bq = g // 2, g % 2
                for b4 in range(4):
                    b_ = bq * 4 + b4
                    out = bank[3][b4 * 32:(b4 + 1) * 32, g * HD:(g + 1) * HD]
                    nc.tensor.matmul(out, psT[:, g, b4 * 32:(b4 + 1) * 32], cv[:, b_, kv * HD:(kv + 1) * HD], start=True, stop=False)
                    ins_ = nc.tensor.matmul(out, psnT[:, g, b4 * 32:(b4 + 1) * 32], vnew[:, b_, kv * HD:(kv + 1) * HD],
                                            start=False, stop=True)
            ins_.then_inc(s_pv, 1)

        @block.scalar
        def _(act):
            def square_x(t):
                r = rows(t)
                x_in.wait(act, t)
                x_var.wait(act, t - 2)
                x_square.wait(act, t - 1)
                x_square.mark(nc.scalar.activation(square[0:r, :], x[0:r, t.p, :], ACT.Square, accum_out=xss[0:r, t.p:t.p + 1]))

            def round_h(t):
                r = rows(t)
                h_out.wait(act, t - 2)
                proj.wait(act, t - 2)
                for b in range(2):
                    h_turned.wait(act, t, b)
                    src = h_bank[b][:, :].rearrange("p (c r) -> p c r", c=4)[:, :, 0:r]
                    dst = h_hi[:, t.p, b * 512:(b + 1) * 512].rearrange("p (c r) -> p c r", c=4)[:, :, 0:r]
                    h_rounded.mark(nc.scalar.activation(dst, src, ACT.Copy))

            def keep_z(t, g):
                r = rows(t)
                lo, hi = ((0, QW), (QW, ATT_W))[g]
                proj.wait(act, t, g)
                if g == 0:
                    z_scaled.wait(act, t - 2)
                else:
                    v_kept.wait(act, t - 2)
                z_ready.mark(nc.scalar.activation(z[0:r, t.p, lo:hi], bank[g][0:r, 0:hi - lo], ACT.Copy))

            def keep_q(t):
                qk_turned.wait(act, t, 0)
                scored.wait(act, t - 1)
                q_kept.mark(nc.scalar.activation(qT[:, :], bank[2][:, :], ACT.Copy))

            def exps(t):
                s_den.wait(act, t - 1)
                for h in range(HQ):
                    if h % 4 == 0:
                        s_stats.wait(act, t, h + 3)
                    ins_ = nc.scalar.activation(s[:, h * 256:(h + 1) * 256], s[:, h * 256:(h + 1) * 256], ACT.Exp,
                                                bias=neg_m[:, h:h + 1], accum_out=ssum[:, h:h + 1])
                    if h == 6:
                        nc.scalar.activation(esink[:, :], sink_m[:, :], ACT.Exp)
                    if h % 4 == 3:
                        s_exp.mark(ins_)

            def keep_p(t, first=False):
                for b in range(2):
                    p_turned.wait(act, t, b)
                    pv.wait(act, t - 1)
                    parts = slice(1, 2) if first else slice(0, 2)
                    dst = pT[:, b * 512:(b + 1) * 512].rearrange("p (h a r) -> p h a r", h=2, a=2)[:, :, parts, :]
                    src = bank[4 + b][:, :].rearrange("p (h a r) -> p h a r", h=2, a=2)[:, :, parts, :]
                    p_kept_a.mark(nc.scalar.activation(dst, src, ACT.Copy))

            w.round(nc, act)
            square_x(Tile(0, 0))
            square_x(Tile(0, 1))
            round_h(Tile(0, 0))
            round_h(Tile(0, 1))
            keep_z(Tile(0, 0), 0)
            keep_z(Tile(0, 0), 1)

            def period(t):
                static = isinstance(t.i, int)
                ahead = not (static and t.c + 2 > NT)
                if ahead:
                    square_x(t + 2)
                keep_z(t + 1, 0)
                keep_q(t)
                if not (static and t.c == 0):
                    keep_p(t - 1, first=static and t.c == 1)
                keep_z(t + 1, 1)
                if ahead:
                    round_h(t + 2)
                exps(t)

            tiles_loop(act, period, 0, NT)
            last = Tile(0, NT - 1)
            keep_p(last)
            qk_turned.wait(act, samp, 0)
            src = bank[2][:, :].rearrange("p (j r) -> p j r", j=GQ)[:, :, 0:NS].rearrange("p j (b t) -> p b j t", t=ST)
            for b_ in range(SB):
                ins_ = nc.scalar.activation(qTs[:, b_, :].rearrange("p (j t) -> p j t", j=GQ), src[:, b_], ACT.Copy)
            ins_.then_inc(s_act, 1)
            act.wait_ge(s_dve, 5)
            for g in range(4):
                nc.scalar.activation(ss[:, g, :], ss[:, g, :], ACT.Exp, bias=stat[:, 2, g:g + 1],
                                     accum_out=stat[:, 4, g:g + 1]).then_inc(s_act, 1)
            nc.scalar.activation(stat[:, 5, :], stat[:, 3, :], ACT.Exp).then_inc(s_act, 1)
            act.wait_ge(s_os, 1)
            store_os(act, 1)

        @block.vector
        def _(dve):
            def var_x(t):
                r = rows(t)
                x_square.wait(dve, t)
                x_rstd.wait(dve, t - 1)
                x_var.mark(nc.vector.tensor_scalar(xvar[0:r, :], xss[0:r, t.p:t.p + 1], 1.0 / D, EPS, ALU.mult, ALU.add))

            def norm_x(t):
                r = rows(t)
                x_rstd.wait(dve, t)
                h_turned.wait(dve, t - 1)
                x_normed.mark(nc.vector.scalar_tensor_tensor(hn[0:r, :], x[0:r, t.p, :], xr[0:r, 0:1], C["norm_mix"][0:r, :],
                                                             ALU.mult, ALU.mult))

            def split_h(t):
                r = rows(t)
                for b in range(2):
                    h_rounded.wait(dve, t, b)
                    src = h_bank[b][:, :].rearrange("p (c r) -> p c r", c=4)[:, :, 0:r]
                    hi = h_hi[:, t.p, b * 512:(b + 1) * 512].rearrange("p (c r) -> p c r", c=4)[:, :, 0:r]
                    dst = h_lo[:, t.p, b * 512:(b + 1) * 512].rearrange("p (c r) -> p c r", c=4)[:, :, 0:r]
                    h_split.mark(nc.vector.tensor_tensor(dst, src, hi.bitcast(F32), ALU.subtract))

            def sum_z(t):
                r = rows(t)
                z_square.wait(dve, t)
                z_sum.mark(nc.vector.reduce_sum(qss[0:r, :], zz[0:r, :].rearrange("p (h d) -> p h d", d=HD), axis=AX))

            def var_z(t):
                r = rows(t)
                z_sum.wait(dve, t)
                z_rstd.wait(dve, t - 1)
                z_var.mark(nc.vector.tensor_scalar(qvar[0:r, :], qss[0:r, :], 1.0 / HD, EPS, ALU.mult, ALU.add))

            def scale_z(t):
                r = rows(t)
                z_rstd.wait(dve, t)
                qk_normed.wait(dve, t - 1)
                z_scaled.mark(nc.vector.tensor_tensor(
                    qu[0:r, :].rearrange("p (h d) -> p h d", d=HD),
                    z[0:r, t.p, 0:QW + KVW].rearrange("p (h d) -> p h d", d=HD),
                    qr[0:r, :].unsqueeze(2).broadcast_to([r, HQ + HKV, HD]), ALU.mult))

            def keep_k(t):
                qk_turned.wait(dve, t, 1)
                k_kept.mark(nc.vector.tensor_copy(kT[:, t.p, :], bank[3][:, 0:P]))

            def keep_p(t, first=False):
                for b in range(2, 4):
                    p_turned.wait(dve, t, b)
                    pv.wait(dve, t - 1)
                    parts = slice(1, 2) if first else slice(0, 2)
                    dst = pT[:, b * 512:(b + 1) * 512].rearrange("p (h a r) -> p h a r", h=2, a=2)[:, :, parts, :]
                    src = bank[4 + b][:, :].rearrange("p (h a r) -> p h a r", h=2, a=2)[:, :, parts, :]
                    p_kept_v.mark(nc.vector.tensor_copy(dst, src))

            def keep_o(t):
                pv.wait(dve, t)
                o_out.wait(dve, t - 2)
                s_den.wait(dve, t)
                o_ready.mark(nc.vector.tensor_tensor(
                    o[:, t.p, :].rearrange("p (h d) -> p h d", d=HD), bank[3][:, :].rearrange("p (h d) -> p h d", d=HD),
                    rden[:, :].unsqueeze(2).broadcast_to([P, HQ, HD]), ALU.mult))

            def softmax_stats(t, first=False):
                p_turned.wait(dve, t - 1)
                for b in range(4):
                    scored.wait(dve, t, b)
                    dst, src, msk = s[:, b * 512:(b + 1) * 512], bank[4 + b][:, :], C["mask"][:, :]
                    if first:
                        dst, src, msk = (a.rearrange("p (h a r) -> p h a r", h=2, a=2)[:, :, 1, :] for a in (dst, src, msk))
                    masked.mark(nc.vector.scalar_tensor_tensor(dst, src, ATT_SCALE, msk, ALU.mult, ALU.add))
                    if b % 2 == 0:
                        continue
                    if b == 1:
                        sum_z(t + 1)
                        var_z(t + 1)
                    else:
                        scale_z(t + 1)
                    hs = slice((b - 1) * 2, (b + 1) * 2)
                    masked.wait(dve, t, b)
                    s_stats.mark(nc.vector.reduce_max(
                        smax[:, hs], s[:, (b - 1) * 512:(b + 1) * 512].rearrange("p (h r) -> p h r", h=4), axis=AX))
                    s_stats.wait(dve, t, 2 * (b - 1))
                    s_stats.mark(nc.vector.tensor_tensor(m[:, hs], smax[:, hs], C["sinks"][:, hs], ALU.max))
                    s_stats.wait(dve, t, 2 * (b - 1) + 1)
                    s_stats.mark(nc.vector.tensor_tensor(sink_m[:, hs], C["sinks"][:, hs], m[:, hs], ALU.subtract))
                    s_stats.mark(nc.vector.tensor_scalar(neg_m[:, hs], m[:, hs], -1.0, None, ALU.mult))

            def denominators(t):
                s_exp.wait(dve, t)
                s_den.mark(nc.vector.tensor_tensor(den[:, :], ssum[:, :], esink[:, :], ALU.add))
                s_den.wait(dve, t, 0)
                s_den.mark(nc.vector.reciprocal(rden[:, :], den[:, :]))

            w.subtract(nc, dve)
            for t0 in range(2):
                var_x(Tile(0, t0))
                norm_x(Tile(0, t0))
            split_h(Tile(0, 0))
            split_h(Tile(0, 1))
            nc.vector.memset(s[:, :], NEG)
            sum_z(Tile(0, 0))
            var_z(Tile(0, 0))
            scale_z(Tile(0, 0))

            def period(t):
                static = isinstance(t.i, int)
                ahead = not (static and t.c + 2 > NT)
                if ahead:
                    var_x(t + 2)
                if ahead:
                    norm_x(t + 2)
                keep_k(t)
                if not (static and t.c == 0):
                    keep_p(t - 1, first=static and t.c == 1)
                if ahead:
                    split_h(t + 2)
                if not (static and t.c == 0):
                    keep_o(t - 1)
                softmax_stats(t, first=static and t.c == 0)
                denominators(t)

            tiles_loop(dve, period, 0, NT)
            last = Tile(0, NT - 1)
            keep_p(last)
            qk_turned.wait(dve, samp, 1)
            k_kept.mark(nc.vector.tensor_copy(ckT[:, :, WIN:WIN + ST], bank[3][:, 0:NS].rearrange("p (b t) -> p b t", t=ST)))
            keep_o(last)
            k_kept.wait(dve, samp)
            dve.wait_ge(s_act, 1)
            nc.vector.memset(stat[:, 0, :], 0.0).then_inc(s_keep, 1)
            nc.vector.memset(stat[:, 1, :], 0.0).then_inc(s_keep, 1)
            nc.vector.memset(stat[:, 6, :], 0.0).then_inc(s_keep, 1)
            for b in range(2):
                dve.wait_ge(sT_done, b + 1)
                nc.vector.tensor_copy(ckT[:, b * 4:(b + 1) * 4, 0:WIN], bank[b][:, :].rearrange("p (b s) -> p b s", b=4)).then_inc(s_keep, 1)
            dve.wait_ge(s_mask, 1)
            nc.vector.tensor_copy(mask_s[:, :], bank[7][:, 0:WIN + ST]).then_inc(s_keep, 1)
            nc.vector.tensor_copy(sink_s[:, :], bank[7][:, 256:256 + HKV]).then_inc(s_keep, 1)
            dve.wait_ge(s_score, 1)
            dve.wait_ge(s_keep, 7)
            for g in range(4):
                src = bank[4 + g // 2][:, (g % 2) * 256:(g % 2) * 256 + WIN + ST]
                ins_ = nc.vector.scalar_tensor_tensor(ss[:, g, :], src, ATT_SCALE, mask_s[:, :], ALU.mult, ALU.add)
            ins_.then_inc(s_dve, 1)
            dve.wait_ge(s_dve, 1)
            nc.vector.reduce_max(stat[:, 0, :], ss[:, :, :], axis=AX).then_inc(s_dve, 1)
            dve.wait_ge(s_dve, 2)
            sink_g = sink_s[:, :].unsqueeze(2).broadcast_to([P, HKV, 2])
            four = lambda a: a.rearrange("p (k b) -> p k b", k=HKV)
            nc.vector.tensor_tensor(four(stat[:, 1, :]), four(stat[:, 0, :]), sink_g, ALU.max).then_inc(s_dve, 1)
            dve.wait_ge(s_dve, 3)
            nc.vector.tensor_scalar(stat[:, 2, :], stat[:, 1, :], -1.0, None, ALU.mult).then_inc(s_dve, 1)
            nc.vector.tensor_tensor(four(stat[:, 3, :]), sink_g, four(stat[:, 1, :]), ALU.subtract).then_inc(s_dve, 1)
            dve.wait_ge(s_act, 6)
            nc.vector.tensor_tensor(stat[:, 6, :], stat[:, 4, :], stat[:, 5, :], ALU.add).then_inc(s_dve, 1)
            dve.wait_ge(s_dve, 6)
            nc.vector.reciprocal(stat[:, 7, :], stat[:, 6, :]).then_inc(s_dve, 1)
            dve.wait_ge(s_turn, 1)
            nc.vector.tensor_copy(psT[:, :, :], bank[6][:, :].rearrange("p (g r) -> p g r", g=4)).then_inc(s_dve, 1)
            nc.vector.tensor_copy(psnT[:, :, :], bank[7][0:ST, :].rearrange("p (g r) -> p g r", g=4)).then_inc(s_dve, 1)
            dve.wait_ge(s_pv, 1)
            dve.wait_ge(s_dve, 9)
            nc.vector.tensor_tensor(os_[:, :, :], bank[3][:, 0:4 * HD].rearrange("p (g d) -> p g d", g=4),
                                    stat[:, 7, :].unsqueeze(2).broadcast_to([P, 4, HD]), ALU.mult).then_inc(s_os, 1)

        @block.gpsimd
        def _(pool):
            def rstd_x(t):
                r = rows(t)
                x_normed.wait(pool, t - 1)
                x_var.wait(pool, t)
                x_rstd.mark(nc.gpsimd.tensor_tensor(xr[0:r, :], xvar[0:r, :], C["mhalf"][0:r, 0:1], ALU.pow))

            def keep_v(t):
                r = rows(t)
                z_ready.wait(pool, t, 1)
                pv.wait(pool, t - 1)
                v_kept.mark(nc.gpsimd.tensor_tensor(v[0:r, t.p, :], z[0:r, t.p, QW + KVW:ATT_W], C["ones"][0:r, 0:KVW], ALU.mult))

            def square_z(t):
                r = rows(t)
                z_ready.wait(pool, t, 1)
                z_sum.wait(pool, t - 1)
                zt = z[0:r, t.p, 0:QW + KVW]
                z_square.mark(nc.gpsimd.tensor_tensor(zz[0:r, :], zt, zt, ALU.mult))

            def rstd_z(t):
                r = rows(t)
                z_scaled.wait(pool, t - 1)
                z_var.wait(pool, t)
                z_rstd.mark(nc.gpsimd.tensor_tensor(qr[0:r, :], qvar[0:r, :], C["mhalf"][0:r, :], ALU.pow))

            def weigh_qk(t):
                r = rows(t)
                z_scaled.wait(pool, t)
                qk_turned.wait(pool, t - 1)
                qk_normed.mark(nc.gpsimd.tensor_tensor(
                    qn[0:r, :].rearrange("p (j k d) -> p k j d", k=HKV, d=HD),
                    qu[0:r, 0:QW].rearrange("p (k j d) -> p k j d", k=HKV, d=HD),
                    C["q_norm"][0:r, :].unsqueeze(1).unsqueeze(1).broadcast_to([r, HKV, GQ, HD]), ALU.mult))
                qk_normed.mark(nc.gpsimd.tensor_tensor(
                    kn[0:r, :].rearrange("p (h d) -> p h d", d=HD), qu[0:r, QW:QW + KVW].rearrange("p (h d) -> p h d", d=HD),
                    C["k_norm"][0:r, :].unsqueeze(1).broadcast_to([r, HKV, HD]), ALU.mult))

            rstd_x(Tile(0, 0))
            rstd_x(Tile(0, 1))
            square_z(Tile(0, 0))
            rstd_z(Tile(0, 0))
            weigh_qk(Tile(0, 0))

            def period(t):
                static = isinstance(t.i, int)
                if not (static and t.c + 2 > NT):
                    rstd_x(t + 2)
                square_z(t + 1)
                rstd_z(t + 1)
                if static and t.c == NT - 1:
                    qk_turned.wait(pool, t)
                    pool.dma_start(outs["k_prompt"][0, 0].rearrange("s k d -> s (k d)"), kn[:, :]).then_inc(k_out, 16)
                    pool.wait_ge(k_out, 16)
                weigh_qk(t + 1)
                keep_v(t)

            tiles_loop(pool, period, 0, NT)


def mlstm(nc, C, ins, outs, h_dram, o_dram, w):
    QM, KM, VM, OM = 2 * MH, 2 * MH + MLQ, 2 * MH + 2 * MLQ, 2 * MH + 2 * MLQ + MLV
    G = 4
    GW = ML_W // G
    slot = [(h % 2) * 2 + h // 2 for h in range(MH)]
    with ExitStack() as ctx:
        k = Stage(nc, ctx, "ml")
        w.use(k, "w")
        hh = k.sb("hh", [P, 2, 2, D], F32R)
        z = k.sb("z", [P, 2, ML_W])
        q_T = k.sb("q_T", [P, 2 * P])
        k_T = k.sb("k_T", [P, 2 * P])
        ig = k.sb("ig", [MH, P])
        fg = k.sb("fg", [MH, P])
        nab = k.sb("nab", [MH, P])
        ef = k.sb("ef", [MH, P])
        sp_ = k.sb("softplus", [MH, P])
        lf = k.sb("lf", [MH, P])
        b = k.sb("b", [MH, P])
        m = k.sb("m", [MH, 2, P])
        neg_M = k.sb("neg_M", [MH, P])
        R = k.sb("rows", [MH, 4, P])
        dsc = k.sb("dsc", [MH, MH])
        cols = k.sb("cols", [P, 20])
        e = k.sb("e", [P, MH * P])
        a = k.sb("a", [P, MH * P])
        vx = k.sb("vx", [P, MH, MVE])
        kw = k.sb("kw", [P, MLQ])
        num = k.sb("num", [P, MH * MVE])
        CT = k.sb("CT", [P, 2, 2 * MVE])
        dn = k.sb("dn", [P, MH])
        dn2 = k.sb("dn2", [P, MH])
        rd = k.sb("rd", [P, MH])
        h = k.sb("h", [P, MLV])
        hq = k.sb("hq", [P, MLV])
        hss = k.sb("hss", [P, MH])
        hvar = k.sb("hvar", [P, MH])
        hr = k.sb("hr", [P, MH])
        h1 = k.sb("h1", [P, MLV])
        eo = k.sb("eo", [P, MLV])
        sg = k.sb("sg", [P, MLV])
        o = k.sb("o", [P, 2, MLV])
        bank = k.banks()

        h_in = k.landed("h_in")
        proj = k.steps("proj", G)
        z_ready = k.steps("z_ready", G)
        turned = k.steps("turned", 2)
        qk_kept = k.steps("qk_kept", 2)
        rows_v = k.steps("rows_v", 9)
        rows_a = k.steps("rows_a", 5)
        mid = k.steps("mid", 3)
        cols_kept = k.steps("cols_kept")
        capped = k.steps("capped")
        e_done = k.steps("e_done")
        a_done = k.steps("a_done", 2)
        vx_kept = k.steps("vx_kept")
        kw_done = k.steps("kw_done")
        summed = k.steps("summed", 3)
        num_kept = k.steps("num_kept", 2)
        joined = k.steps("joined")
        state = k.steps("state")
        den_v = k.steps("den_v", 3)
        h_done = k.steps("h_done")
        h_square = k.steps("h_square")
        h_sum = k.steps("h_sum", 2)
        h_rstd = k.steps("h_rstd")
        h_scaled = k.steps("h_scaled")
        h_weighed = k.steps("h_weighed")
        o_exp = k.steps("o_exp")
        o_sig = k.steps("o_sig", 2)
        o_ready = k.steps("o_ready")
        o_out = k.landed("o_out")
        state_zero = k.sem("state_zero")
        prompt_turned, prompt_kept, prompt_out = k.sem("prompt_turned"), k.sem("prompt_kept"), k.sem("prompt_out")

        def rows(t):
            return NS if t.c == NT else P

        samp = Tile(0, NT)
        last = Tile(0, NT - 1)

        C0 = k.sb("C0", [P, SB * MH, MQK])
        n0 = k.sb("n0", [SB, MLQ])
        m0 = k.sb("m0", [MH, SB])
        C0T = k.sb("C0T", [P, SB, 2, MV])
        nT = k.sb("nT", [P, 2, SB])
        first_of = k.sb("first_of", [MH, NS])
        cols_s = k.sb("cols_s", [P, 16 + MH * SB + MH])
        iT = k.sb("iT", [P, MH, NS])
        tm = k.sb("tm", [MH, 2, NS])
        nq = k.sb("nq", [NS, MH, SB])
        nqs = k.sb("nqs", [NS, MH])
        kwx = k.sb("kwx", [NS, MH, SB, MQK])
        Cn = z[:, :, :].rearrange("p a n -> p (a n)")[:, 0:MH * SB * MQK].rearrange("p (h b d) -> p h b d", h=MH, b=SB)
        nn = k.sb("nn", [SB, MLQ])
        Cp = k.sb("Cp", [P, 2 * P])
        ev = {n: k.sem("ev_" + n) for n in (
            "state_in", "C0_turned", "C0_kept", "nT_turned", "nT_kept", "pattern", "bscan", "mscan", "tm", "tm_exp", "mid", "cols_kept",
            "qk", "interT", "iT", "inter", "nq_mult", "nq", "kwx", "delta", "Cscaled", "Cn", "n_delta", "nn", "joined", "out")}

        def sig(ins_, name):
            ins_.then_inc(ev[name], 1)

        def need(eng, name, n=1):
            eng.wait_ge(ev[name], n)

        block = ctx.enter_context(nc.Block())

        @block.sync
        def _(sp):
            def load_h(t):
                proj.wait(sp, t - 2)
                dst = hh[:, t.p, :, :].bitcast(F32)
                if t.c == NT:
                    cut = lambda x_: x_.rearrange("p a (c r) -> p (a c) r", r=P)[:, :, 0:NS]
                    h_in.mark(sp.dma_start(cut(dst), cut(h_dram[NT])), t)
                else:
                    h_in.mark(sp.dma_start(dst, h_dram[bass.ds(t.n, 1)].rearrange("a p b n -> (a p) b n")), t)

            def store_o(t):
                o_ready.wait(sp, t)
                r = rows(t)
                o_out.mark(sp.dma_start(o_dram[bass.ds(t.n * P, r), QW:QW + MLV], o[0:r, t.p, :]), t)

            load_h(Tile(0, 0))
            load_h(Tile(0, 1))
            sp.dma_start(C0[:, :, :], ins["state_mlstm_C"][0].rearrange("b h v d -> v (b h) d")).then_inc(ev["state_in"], 16)
            sp.dma_start(n0[:, :], ins["state_mlstm_n"][0].rearrange("b h d -> b (h d)")).then_inc(ev["state_in"], 16)
            with nc.allow_non_contiguous_dma(reason="32 stabilisers"):
                sp.dma_start(m0[:, :], ins["state_mlstm_m"][0].rearrange("b h -> h b")).then_inc(ev["state_in"], 16)

            def period(t):
                if not (isinstance(t.i, int) and t.c + 2 > NT):
                    load_h(t + 2)
                if not (isinstance(t.i, int) and t.c < 1):
                    store_o(t - 1)

            tiles_loop(sp, period, 0, NT)
            store_o(last)
            sp.wait_ge(prompt_kept, 1)
            state.wait(sp, last)
            for j in range(2):
                for hd in range(2):
                    sp.dma_start(outs["C_prompt"][0, 0, 2 * j + hd], Cp[:, j * P + hd * MQK:j * P + (hd + 1) * MQK]).then_inc(prompt_out, 16)
                    with nc.allow_non_contiguous_dma(reason="a normaliser of 64"):
                        sp.dma_start(outs["n_prompt"][0, 0, 2 * j + hd, :].rearrange("(d a) -> d a", a=1),
                                     CT[hd * MQK:(hd + 1) * MQK, j, hd * MVE + MV:hd * MVE + MVE]).then_inc(prompt_out, 16)
            with nc.allow_non_contiguous_dma(reason="four stabilisers"):
                sp.dma_start(outs["m_prompt"][0, 0, :].rearrange("(h a) -> h a", a=1), m[:, last.p, P - 1:P]).then_inc(prompt_out, 16)
            need(sp, "mscan", SB)
            with nc.allow_non_contiguous_dma(reason="32 stabilisers"):
                sp.dma_start(outs["m_sample"][0].rearrange("b h -> h b"),
                             m[:, 0, 0:NS].rearrange("h (b t) -> h b t", t=ST)[:, :, ST - 1]).then_inc(ev["out"], 16)
            need(sp, "nn", 2)
            sp.dma_start(outs["n_sample"][0].rearrange("b h d -> b (h d)"), nn[:, :]).then_inc(ev["out"], 16)
            for hd in range(MH):
                need(sp, "Cn", hd + 1)
                sp.dma_start(outs["C_sample"][0, :, hd].rearrange("b v d -> v b d"), Cn[:, hd]).then_inc(ev["out"], 16)
            need(sp, "joined")
            o_ready.wait(sp, samp)
            sp.dma_start(o_dram[SEQ:SEQ + NS, QW:QW + MLV], o[0:NS, 0, :]).then_inc(ev["out"], 16)
            sp.wait_ge(prompt_out, 16 * 9)
            need(sp, "out", 16 * 7)
            o_out.wait(sp, last)
            o_out.wait(sp, last - 1)

        @block.tensor
        def _(pe):
            def project(t, g):
                r = rows(t)
                if g == 0:
                    h_in.wait(pe, t)
                z_ready.wait(pe, t - 1 if g < 2 else t, (g - 2) % G)
                for c in range(KC):
                    if isinstance(t.i, int) and t.c == 0 and g == 0:
                        pe.wait_ge(w.split, c + 1)
                    at = slice(c * P, c * P + r)
                    ins_ = mm3(nc, bank[g % 2][0:r, 0:GW], hh[:, t.p, 0, at], hh[:, t.p, 1, at],
                               w.hi[:, c, g * GW:(g + 1) * GW], w.lo[:, c, g * GW:(g + 1) * GW], c == 0, c == KC - 1)
                proj.mark(ins_)

            def turn(t):
                r = rows(t)
                z_ready.wait(pe, t, 1)
                joined.wait(pe, t - 1)
                for n in range(4):
                    ins_ = nc.tensor.transpose(bank[2][:, n * P:n * P + r], z[0:r, t.p, QM + n * P:QM + (n + 1) * P], C["ident"][0:r, 0:r])
                turned.mark(ins_)
                for n in range(2):
                    ins_ = nc.tensor.transpose(bank[3][0:MH, n * P:n * P + r], z[0:r, t.p, n * MH:(n + 1) * MH], C["ident"][0:r, 0:r])
                turned.mark(ins_)

            def middle(t):
                qk_kept.wait(pe, t)
                rows_v.wait(pe, t, 1)
                for hd in range(MH):
                    part = slice((hd % 2) * MQK, (hd % 2 + 1) * MQK)
                    at = slice((hd // 2) * P, (hd // 2 + 1) * P)
                    ins_ = nc.tensor.matmul(bank[2 + hd % 2][:, at], k_T[part, at], q_T[part, at], start=True, stop=True)
                mid.mark(ins_)
                rows_v.wait(pe, t, 7)
                state.wait(pe, t - 1)
                for hd in range(MH):
                    ins_ = nc.tensor.matmul(bank[4][:, slot[hd] * P:(slot[hd] + 1) * P], C["sel_head"][:, hd * P:(hd + 1) * P],
                                            neg_M[:, :], start=True, stop=True)
                mid.mark(ins_)
                rows_a.wait(pe, t)
                rows_v.wait(pe, t)
                nc.tensor.matmul(bank[7][:, 16:20], C["ones"][0:MH, :], dsc[:, :], start=True, stop=True)
                for n in range(4):
                    ins_ = nc.tensor.transpose(bank[7][:, n * MH:(n + 1) * MH], R[:, n, :], C["ident"][0:MH, 0:MH])
                mid.mark(ins_)

            def sums(t):
                a_done.wait(pe, t)
                vx_kept.wait(pe, t)
                num_kept.wait(pe, t - 1)
                for hd in range(MH):
                    ins_ = nc.tensor.matmul(bank[5 + hd // 2][:, (hd % 2) * MVE:(hd % 2 + 1) * MVE],
                                            a[:, slot[hd] * P:(slot[hd] + 1) * P], vx[:, hd, :], start=True, stop=True)
                summed.mark(ins_)
                state.wait(pe, t - 1)
                pe.wait_ge(state_zero, 1)
                for j in range(2):
                    ins_ = nc.tensor.matmul(bank[2 + j][:, 0:2 * MVE], q_T[:, j * P:(j + 1) * P], CT[:, j, :], start=True, stop=True)
                summed.mark(ins_)
                kw_done.wait(pe, t)
                capped.wait(pe, t)
                for j in range(2):
                    ins_ = nc.tensor.matmul(bank[(4, 7)[j]][:, 0:2 * MVE], kw[:, j * P:(j + 1) * P],
                                            vx[:, 2 * j:2 * j + 2, :].rearrange("s h v -> s (h v)"), start=True, stop=True)
                summed.mark(ins_)

            for g in range(G):
                project(Tile(0, 0), g)

            def period(t):
                project(t + 1, 0)
                turn(t)
                project(t + 1, 1)
                project(t + 1, 2)
                middle(t)
                project(t + 1, 3)
                sums(t)

            tiles_loop(pe, period, 0, NT)
            state.wait(pe, last)
            for j in range(2):
                for hd in range(2):
                    nc.tensor.transpose(bank[4][:, (2 * j + hd) * P:(2 * j + hd + 1) * P], CT[:, j, hd * MVE:hd * MVE + MV], C["ident"][:, :])\
                        .then_inc(prompt_turned, 1)
            turn(samp)
            need(pe, "state_in", 48)
            z_ready.wait(pe, samp)
            for q in range(4):
                num_kept.wait(pe, last)
                for n in range(4):
                    b_, j = (4 * q + n) // 2, (4 * q + n) % 2
                    ins_ = nc.tensor.transpose(bank[(0, 1, 5, 6)[q]][:, n * P:(n + 1) * P],
                                               C0[:, b_ * MH + 2 * j:b_ * MH + 2 * j + 2, :].rearrange("v h d -> v (h d)"), C["ident"][:, :])
                sig(ins_, "C0_turned")
            for j in range(2):
                ins_ = nc.tensor.transpose(bank[7][:, j * SB:(j + 1) * SB], n0[:, j * P:(j + 1) * P], C["ident"][0:SB, 0:SB])
            sig(ins_, "nT_turned")
            qk_kept.wait(pe, samp)
            need(pe, "bscan")
            for hd in range(MH):
                part = slice((hd % 2) * MQK, (hd % 2 + 1) * MQK)
                at = (hd // 2) * P
                ins_ = nc.tensor.matmul(bank[2 + hd % 2][0:NS, at:at + NS], k_T[part, at:at + NS], q_T[part, at:at + NS], start=True, stop=True)
            sig(ins_, "qk")
            rows_v.wait(pe, samp, 7)
            pe.wait_ge(prompt_kept, 1)
            for hd in range(MH):
                nc.tensor.matmul(bank[4][0:NS, slot[hd] * NS:(slot[hd] + 1) * NS], C["sel_head"][:, hd * P:hd * P + NS],
                                 neg_M[:, 0:NS], start=True, stop=True)
            rows_a.wait(pe, samp)
            need(pe, "nT_kept")
            for n in range(4):
                nc.tensor.transpose(bank[7][0:NS, n * MH:(n + 1) * MH], R[:, n, 0:NS], C["ident"][0:MH, 0:MH])
            sc = R[:, 1, 0:NS].rearrange("h (b t) -> h b t", t=ST)[:, :, ST - 1]
            for hd in range(MH):
                nc.tensor.matmul(bank[7][:, 16 + hd * SB:16 + (hd + 1) * SB], C["sel_head"][:, hd * P:(hd + 1) * P], sc, start=True, stop=True)
            sig(nc.tensor.transpose(bank[7][0:SB, 16 + MH * SB:16 + MH * SB + MH], sc, C["ident"][0:MH, 0:MH]), "mid")
            need(pe, "C0_kept", 4)
            for hd in range(MH):
                part = slice((hd % 2) * MQK, (hd % 2 + 1) * MQK)
                for b_ in range(SB):
                    at = (hd // 2) * P + b_ * ST
                    ins_ = nc.tensor.matmul(bank[5 + hd % 2][:, (hd // 2) * NS + b_ * ST:(hd // 2) * NS + (b_ + 1) * ST],
                                            C0T[part, b_, hd // 2, :], q_T[part, at:at + ST], start=True, stop=True)
            for hd in range(MH):
                part = slice((hd % 2) * MQK, (hd % 2 + 1) * MQK)
                at = (hd // 2) * P
                ins_ = nc.tensor.matmul(bank[hd % 2][0:NS, (hd // 2) * SB:(hd // 2 + 1) * SB], q_T[part, at:at + NS],
                                        nT[part, hd // 2, :], start=True, stop=True)
            sig(ins_, "interT")
            a_done.wait(pe, samp)
            vx_kept.wait(pe, samp)
            for hd in range(MH):
                ins_ = nc.tensor.matmul(bank[2 + hd // 2][0:NS, (hd % 2) * MVE:(hd % 2 + 1) * MVE],
                                        a[0:NS, slot[hd] * NS:(slot[hd] + 1) * NS], vx[0:NS, hd, :], start=True, stop=True)
            summed.mark(ins_)
            need(pe, "iT", 2)
            for hd in range(MH):
                ins_ = nc.tensor.transpose(bank[5][0:NS, hd * P:(hd + 1) * P], iT[:, hd, :], C["ident"][:, :])
            sig(ins_, "inter")
            need(pe, "kwx")
            need(pe, "nq_mult", 4)
            capped.wait(pe, samp)
            for hd in range(MH):
                sig(nc.tensor.matmul(bank[(0, 1, 4, 6)[hd]][:, :], vx[0:NS, hd, 0:MV],
                                     kwx[:, hd, :, :].rearrange("s b d -> s (b d)"), start=True, stop=True), "delta")
            sig(nc.tensor.matmul(bank[7][0:SB, 0:MLQ], C["blk"][:, :], kw[0:NS, :], start=True, stop=True), "n_delta")

        @block.scalar
        def _(act):
            def keep_z(t, g):
                r = rows(t)
                proj.wait(act, t, g)
                if g == 0:
                    turned.wait(act, t - 2)
                    vx_kept.wait(act, t - 2)
                    kw_done.wait(act, t - 2)
                    o_exp.wait(act, t - 2)
                z_ready.mark(nc.scalar.activation(z[0:r, t.p, g * GW:(g + 1) * GW], bank[g % 2][0:r, 0:GW], ACT.Copy))

            def keep_qk(t):
                r = rows(t)
                turned.wait(act, t, 0)
                summed.wait(act, t - 1, 1)
                src = bank[2][:, :].rearrange("p (n r) -> p n r", r=P)
                cut = lambda x_: x_[:, :].rearrange("p (n r) -> p n r", r=P)[:, :, 0:r]
                qk_kept.mark(nc.scalar.activation(cut(q_T), src[:, 0:2, 0:r], ACT.Copy, scale=ML_SCALE))
                qk_kept.mark(nc.scalar.activation(cut(k_T), src[:, 2:4, 0:r], ACT.Copy))

            def forget(t):
                r = rows(t)
                rows_v.wait(act, t, 2)
                rows_a.mark(nc.scalar.activation(ef[:, 0:r], nab[:, 0:r], ACT.Exp))
                rows_a.wait(act, t, 0)
                rows_a.mark(nc.scalar.activation(sp_[:, 0:r], ef[:, 0:r], ACT.Ln, bias=1.0))

            def weights(t):
                rows_v.wait(act, t, 7)
                mid.wait(act, t - 1)
                rows_a.mark(nc.scalar.activation(R[:, 1, :], neg_M[:, :], ACT.Exp, bias=m[:, 1 - t.p, P - 1:P]))
                rows_a.mark(nc.scalar.activation(R[:, 2, :], m[:, t.p, :], ACT.Exp, scale=-1.0))
                rows_a.mark(nc.scalar.activation(R[:, 3, :], R[:, 0, :], ACT.Exp, bias=neg_M[:, P - 1:P]))

            def exp_e(t):
                capped.wait(act, t)
                r, w = (NS, MH * NS) if t.c == NT else (P, MH * P)
                e_done.mark(nc.scalar.activation(e[0:r, 0:w], e[0:r, 0:w], ACT.Exp))

            def exp_o(t):
                r = rows(t)
                z_ready.wait(act, t)
                o_sig.wait(act, t - 1, 0)
                o_exp.mark(nc.scalar.activation(eo[0:r, :], z[0:r, t.p, OM:ML_W], ACT.Exp, scale=-1.0))

            def keep_num(t):
                summed.wait(act, t, 0)
                h_done.wait(act, t - 1)
                for j in range(2):
                    num_kept.mark(nc.scalar.activation(num[:, j * 2 * MVE:(j + 1) * 2 * MVE], bank[5 + j][:, 0:2 * MVE], ACT.Copy))

            w.round(nc, act)
            for g in range(G):
                keep_z(Tile(0, 0), g)

            def period(t):
                keep_z(t + 1, 0)
                keep_qk(t)
                forget(t)
                keep_z(t + 1, 1)
                weights(t)
                exp_o(t)
                keep_z(t + 1, 2)
                exp_e(t)
                keep_z(t + 1, 3)
                keep_num(t)

            act.wait_ge(state_zero, 1)
            tiles_loop(act, period, 0, NT)
            act.wait_ge(prompt_turned, 4)
            src = bank[4][:, :].rearrange("p (n r) -> p n r", r=P)
            for j in range(2):
                nc.scalar.activation(Cp[:, j * P:j * P + MQK], src[:, 2 * j, 0:MQK], ACT.Copy)
                ins_ = nc.scalar.activation(Cp[:, j * P + MQK:(j + 1) * P], src[:, 2 * j + 1, MQK:2 * MQK], ACT.Copy)
            ins_.then_inc(prompt_kept, 1)
            keep_qk(samp)
            forget(samp)
            exp_o(samp)
            for q in range(4):
                need(act, "C0_turned", q + 1)
                sig(nc.scalar.activation(C0T[:, 2 * q:2 * q + 2, :, :].rearrange("p b j v -> p (b j v)"),
                                         bank[(0, 1, 5, 6)[q]][:, :], ACT.Copy), "C0_kept")
            need(act, "tm", 2)
            mid.wait(act, last)
            rows_a.mark(nc.scalar.activation(R[:, 1, 0:NS], tm[:, 0, :], ACT.Exp))
            rows_a.mark(nc.scalar.activation(R[:, 2, 0:NS], m[:, 0, 0:NS], ACT.Exp, scale=-1.0))
            rows_a.mark(nc.scalar.activation(R[:, 3, 0:NS], tm[:, 1, :], ACT.Exp))
            exp_e(samp)
            need(act, "interT")
            for n in range(2):
                sig(nc.scalar.activation(iT[:, n:MH:2, :], bank[5 + n][:, 0:2 * NS].rearrange("p (a r) -> p a r", a=2), ACT.Copy), "iT")
            h_done.wait(act, last)
            summed.wait(act, samp, 0)
            for j in range(2):
                num_kept.mark(nc.scalar.activation(num[0:NS, j * 2 * MVE:(j + 1) * 2 * MVE], bank[2 + j][0:NS, 0:2 * MVE], ACT.Copy))

        @block.vector
        def _(dve):
            def gates(t):
                r = rows(t)
                turned.wait(dve, t)
                rows_a.wait(dve, t - 1)
                rows_v.mark(nc.vector.tensor_scalar(ig[:, 0:r], bank[3][0:MH, 0:r], C["bias_i"][:, 0:1], None, ALU.add))
                rows_v.mark(nc.vector.tensor_scalar(fg[:, 0:r], bank[3][0:MH, P:P + r], C["bias_f"][:, 0:1], None, ALU.add))
                rows_v.wait(dve, t, 1)
                rows_v.mark(nc.vector.scalar_tensor_tensor(nab[:, 0:r], fg[:, 0:r], -1.0, fg[:, 0:r], ALU.mult, ALU.min))

            def log_forget(t):
                r = rows(t)
                rows_a.wait(dve, t, 1)
                rows_v.mark(nc.vector.scalar_tensor_tensor(lf[:, 0:r], fg[:, 0:r], 0.0, sp_[:, 0:r], ALU.min, ALU.subtract))
                rows_v.wait(dve, t, 3)

            def scans(t):
                log_forget(t)
                mid.wait(dve, t - 1)
                rows_v.mark(nc.vector.tensor_tensor_scan(b[:, :], C["ones"][0:MH, :], lf[:, :], 0.0, ALU.mult, ALU.add))
                rows_v.mark(nc.vector.tensor_tensor_scan(m[:, t.p, :], lf[:, :], ig[:, :], m[:, 1 - t.p, P - 1:P], ALU.add, ALU.max))
                rows_v.wait(dve, t, 5)
                rows_v.mark(nc.vector.tensor_tensor(R[:, 0, :], ig[:, :], b[:, :], ALU.subtract))
                rows_v.mark(nc.vector.tensor_tensor(neg_M[:, :], b[:, :], m[:, t.p, :], ALU.subtract))

            def decay(t):
                rows_a.wait(dve, t, 2)
                rows_v.mark(nc.vector.tensor_scalar(dsc[:, :], C["ident"][0:MH, 0:MH], R[:, 1, P - 1:P], None, ALU.mult))

            def cap_e(t):
                mid.wait(dve, t)
                joined.wait(dve, t - 1)
                state.wait(dve, t - 1)
                cols_kept.mark(nc.vector.tensor_copy(cols[:, :], bank[7][:, 0:20]))
                cols_kept.wait(dve, t)
                a_done.wait(dve, t - 1)
                for hd in range(MH):
                    at = slice(slot[hd] * P, (slot[hd] + 1) * P)
                    ins_ = nc.vector.scalar_tensor_tensor(e[:, at], bank[4][:, at], cols[:, hd:hd + 1], C["cap"][:, :], ALU.add, ALU.min)
                capped.mark(ins_)

            def make_a(t):
                e_done.wait(dve, t)
                summed.wait(dve, t - 1, 0)
                for n in range(2):
                    a_done.mark(nc.vector.tensor_tensor(a[:, n * 2 * P:(n + 1) * 2 * P], bank[2 + n][:, 0:2 * P],
                                                        e[:, n * 2 * P:(n + 1) * 2 * P], ALU.mult))

            def join(t):
                num_kept.wait(dve, t)
                summed.wait(dve, t, 1)
                for hd in range(MH):
                    at = slice(hd * MVE, (hd + 1) * MVE)
                    ins_ = nc.vector.scalar_tensor_tensor(num[:, at], bank[2 + hd // 2][:, (hd % 2) * MVE:(hd % 2 + 1) * MVE],
                                                          cols[:, MH + hd:MH + hd + 1], num[:, at], ALU.mult, ALU.add)
                joined.mark(ins_)

            def update_state(t):
                summed.wait(dve, t)
                for hd in range(MH):
                    part = slice((hd % 2) * MQK, (hd % 2 + 1) * MQK)
                    blk = CT[part, hd // 2, (hd % 2) * MVE:(hd % 2 + 1) * MVE]
                    ins_ = nc.vector.scalar_tensor_tensor(blk, blk, cols[part, 16 + hd:17 + hd],
                                                          bank[(4, 7)[hd // 2]][part, (hd % 2) * MVE:(hd % 2 + 1) * MVE], ALU.mult, ALU.add)
                state.mark(ins_)

            def divide(t):
                r = rows(t)
                joined.wait(dve, t)
                nv = num[0:r, :].rearrange("p (h v) -> p h v", h=MH)
                cc = cols_s if t.c == NT else cols
                den_v.mark(nc.vector.scalar_tensor_tensor(dn[0:r, :], nv[:, :, MV], -1.0, nv[:, :, MV], ALU.mult, ALU.max))
                den_v.wait(dve, t, 0)
                den_v.mark(nc.vector.tensor_tensor(dn2[0:r, :], dn[0:r, :], cc[0:r, 8:12], ALU.max))
                den_v.wait(dve, t, 1)
                den_v.mark(nc.vector.reciprocal(rd[0:r, :], dn2[0:r, :]))
                den_v.wait(dve, t, 2)
                h_square.wait(dve, t - 1)
                h_done.mark(nc.vector.tensor_tensor(h[0:r, :].rearrange("p (h v) -> p h v", h=MH), nv[:, :, 0:MV],
                                                    rd[0:r, :].unsqueeze(2).broadcast_to([r, MH, MV]), ALU.mult))

            def gate_out(t):
                r = rows(t)
                o_exp.wait(dve, t)
                o_sig.mark(nc.vector.tensor_scalar(sg[0:r, :], eo[0:r, :], 1.0, None, ALU.add))
                o_sig.wait(dve, t, 0)
                o_sig.mark(nc.vector.reciprocal(sg[0:r, :], sg[0:r, :]))

            def norm_out(t):
                r = rows(t)
                h_square.wait(dve, t)
                h_sum.mark(nc.vector.reduce_sum(hss[0:r, :], hq[0:r, :].rearrange("p (h v) -> p h v", h=MH), axis=AX))
                h_sum.wait(dve, t, 0)
                h_rstd.wait(dve, t - 1)
                h_sum.mark(nc.vector.tensor_scalar(hvar[0:r, :], hss[0:r, :], 1.0 / MV, EPS, ALU.mult, ALU.add))

            def scale_out(t):
                r = rows(t)
                h_rstd.wait(dve, t)
                h_weighed.wait(dve, t - 1)
                h_scaled.mark(nc.vector.tensor_tensor(h1[0:r, :].rearrange("p (h v) -> p h v", h=MH),
                                                      h[0:r, :].rearrange("p (h v) -> p h v", h=MH),
                                                      hr[0:r, :].unsqueeze(2).broadcast_to([r, MH, MV]), ALU.mult))

            def finish_out(t):
                r = rows(t)
                h_weighed.wait(dve, t)
                o_sig.wait(dve, t)
                o_out.wait(dve, t - 2)
                o_ready.mark(nc.vector.tensor_tensor(o[0:r, t.p, :], hq[0:r, :], sg[0:r, :], ALU.mult))

            w.subtract(nc, dve)
            nc.vector.memset(CT[:, :, :], 0.0)
            nc.vector.memset(m[:, :, :], 0.0)
            nc.vector.memset(vx[:, :, MV:MVE], 1.0).then_inc(state_zero, 1)
            dve.wait_ge(state_zero, 1)

            def period(t):
                before = not (isinstance(t.i, int) and t.c == 0)
                if before:
                    norm_out(t - 1)
                gates(t)
                if before:
                    scale_out(t - 1)
                scans(t)
                if before:
                    finish_out(t - 1)
                decay(t)
                cap_e(t)
                make_a(t)
                join(t)
                update_state(t)
                divide(t)
                gate_out(t)

            tiles_loop(dve, period, 0, NT)
            norm_out(last)
            scale_out(last)
            finish_out(last)
            nc.vector.memset(first_of[:, :], 1.0).then_inc(ev["pattern"], 1)
            need(dve, "pattern")
            nc.vector.memset(first_of[:, :].rearrange("h (b t) -> h b t", t=ST)[:, :, 0], 0.0).then_inc(ev["pattern"], 1)
            gates(samp)
            need(dve, "nT_turned")
            sig(nc.vector.tensor_copy(nT[:, :, :], bank[7][:, 0:2 * SB].rearrange("p (j b) -> p j b", j=2)), "nT_kept")
            log_forget(samp)
            need(dve, "pattern", 2)
            mid.wait(dve, last)
            rows_v.mark(nc.vector.tensor_tensor_scan(b[:, 0:NS], first_of[:, :], lf[:, 0:NS], 0.0, ALU.mult, ALU.add))
            sig(nc.vector.memset(dsc[:, :], 0.0), "bscan")
            need(dve, "state_in", 48)
            for b_ in range(SB):
                at = slice(b_ * ST, (b_ + 1) * ST)
                sig(nc.vector.tensor_tensor_scan(m[:, 0, at], lf[:, at], ig[:, at], m0[:, b_:b_ + 1], ALU.add, ALU.max), "mscan")
            rows_v.wait(dve, samp, 4)
            need(dve, "mscan", SB)
            rows_v.mark(nc.vector.tensor_tensor(R[:, 0, 0:NS], ig[:, 0:NS], b[:, 0:NS], ALU.subtract))
            rows_v.mark(nc.vector.tensor_tensor(neg_M[:, 0:NS], b[:, 0:NS], m[:, 0, 0:NS], ALU.subtract))
            rows_v.mark(nc.vector.memset(tm[:, :, :], 0.0))
            rows_v.wait(dve, samp, 7)
            bt = lambda x_: x_.rearrange("h (b t) -> h b t", t=ST)
            sig(nc.vector.tensor_tensor(bt(tm[:, 0, :]), bt(neg_M[:, 0:NS]), m0[:, :].unsqueeze(2).broadcast_to([MH, SB, ST]), ALU.add), "tm")
            sig(nc.vector.tensor_tensor(bt(tm[:, 1, :]), bt(R[:, 0, 0:NS]),
                                        bt(neg_M[:, 0:NS])[:, :, ST - 1:ST].broadcast_to([MH, SB, ST]), ALU.add), "tm")
            need(dve, "mid")
            nc.vector.tensor_copy(cols_s[0:NS, 0:16], bank[7][0:NS, 0:16])
            nc.vector.tensor_copy(cols_s[:, 16:16 + MH * SB], bank[7][:, 16:16 + MH * SB])
            cols_kept.mark(nc.vector.tensor_copy(cols_s[0:SB, 16 + MH * SB:16 + MH * SB + MH], bank[7][0:SB, 16 + MH * SB:16 + MH * SB + MH]))
            cols_kept.wait(dve, samp)
            for hd in range(MH):
                at = slice(slot[hd] * NS, (slot[hd] + 1) * NS)
                ins_ = nc.vector.scalar_tensor_tensor(e[0:NS, at], bank[4][0:NS, at], cols_s[0:NS, hd:hd + 1], C["cap64"][:, :], ALU.add, ALU.min)
            capped.mark(ins_)
            e_done.wait(dve, samp)
            for n in range(2):
                a_done.mark(nc.vector.tensor_tensor(
                    a[0:NS, n * 2 * NS:(n + 1) * 2 * NS].rearrange("p (a r) -> p a r", a=2),
                    bank[2 + n][0:NS, 0:2 * P].rearrange("p (a r) -> p a r", a=2)[:, :, 0:NS],
                    e[0:NS, n * 2 * NS:(n + 1) * 2 * NS].rearrange("p (a r) -> p a r", a=2), ALU.mult))
            kw_done.wait(dve, samp)
            for hd in range(MH):
                ins_ = nc.vector.tensor_tensor(kwx[:, hd, :, :], kw[0:NS, hd * MQK:(hd + 1) * MQK].unsqueeze(1).broadcast_to([NS, SB, MQK]),
                                               C["blk"][:, :].unsqueeze(2).broadcast_to([NS, SB, MQK]), ALU.mult)
            sig(ins_, "kwx")
            turned.wait(dve, samp)
            vx_kept.wait(dve, samp)
            o_exp.wait(dve, samp)
            c0 = C0[:, :, :].rearrange("v (b h) d -> v b h d", h=MH)
            for hd in range(MH):
                sig(nc.vector.tensor_tensor(Cn[:, hd], c0[:, :, hd, :],
                                            cols_s[:, 16 + hd * SB:16 + (hd + 1) * SB].unsqueeze(2).broadcast_to([P, SB, MQK]), ALU.mult), "Cscaled")
            gate_out(samp)
            need(dve, "interT")
            for hd in range(MH):
                sig(nc.vector.tensor_tensor(nq[:, hd, :], bank[hd % 2][0:NS, (hd // 2) * SB:(hd // 2 + 1) * SB], C["blk"][:, :], ALU.mult), "nq_mult")
            need(dve, "nq_mult", 4)
            sig(nc.vector.reduce_sum(nqs[:, :], nq[:, :, :], axis=AX), "nq")
            for hd in range(MH):
                need(dve, "delta", hd + 1)
                need(dve, "Cscaled", hd + 1)
                sig(nc.vector.tensor_tensor(Cn[:, hd], Cn[:, hd], bank[(0, 1, 4, 6)[hd]][:, :].rearrange("p (b d) -> p b d", b=SB), ALU.add), "Cn")
            need(dve, "n_delta")
            hv = lambda x_: x_.rearrange("b (h d) -> b h d", h=MH)
            sig(nc.vector.tensor_tensor(hv(nn[:, :]), hv(n0[:, :]),
                                        cols_s[0:SB, 16 + MH * SB:16 + MH * SB + MH].unsqueeze(2).broadcast_to([SB, MH, MQK]), ALU.mult), "nn")
            need(dve, "nn")
            sig(nc.vector.tensor_tensor(nn[:, :], nn[:, :], bank[7][0:SB, 0:MLQ], ALU.add), "nn")
            need(dve, "inter")
            need(dve, "nq")
            num_kept.wait(dve, samp)
            for hd in range(MH):
                at = slice(hd * MVE, hd * MVE + MV)
                nc.vector.scalar_tensor_tensor(num[0:NS, at], bank[5][0:NS, hd * P:(hd + 1) * P], cols_s[0:NS, MH + hd:MH + hd + 1],
                                               num[0:NS, at], ALU.mult, ALU.add)
                d_ = num[0:NS, hd * MVE + MV:(hd + 1) * MVE]
                ins_ = nc.vector.scalar_tensor_tensor(d_, nqs[:, hd:hd + 1], cols_s[0:NS, MH + hd:MH + hd + 1], d_, ALU.mult, ALU.add)
            joined.mark(ins_)
            divide(samp)
            norm_out(samp)
            scale_out(samp)
            finish_out(samp)
            sig(nc.vector.memset(dsc[:, :], 0.0), "joined")

        @block.gpsimd
        def _(pool):
            def keep_v(t):
                r = rows(t)
                z_ready.wait(pool, t, 3)
                summed.wait(pool, t - 1)
                vx_kept.mark(nc.gpsimd.tensor_tensor(vx[0:r, :, 0:MV], z[0:r, t.p, VM:VM + MLV].rearrange("p (h v) -> p h v", h=MH),
                                                     C["ones"][0:r, :].unsqueeze(1).broadcast_to([r, MH, MV]), ALU.mult))

            def weigh_k(t):
                r = rows(t)
                cols_kept.wait(pool, t)
                cc = cols_s if t.c == NT else cols
                kw_done.mark(nc.gpsimd.tensor_tensor(kw[0:r, :].rearrange("p (h d) -> p h d", h=MH),
                                                     z[0:r, t.p, KM:KM + MLQ].rearrange("p (h d) -> p h d", h=MH),
                                                     cc[0:r, 12:16].unsqueeze(2).broadcast_to([r, MH, MQK]), ALU.mult))

            def square_h(t):
                r = rows(t)
                o_ready.wait(pool, t - 1)
                h_done.wait(pool, t)
                h_square.mark(nc.gpsimd.tensor_tensor(hq[0:r, :], h[0:r, :], h[0:r, :], ALU.mult))

            def rstd_h(t):
                r = rows(t)
                h_scaled.wait(pool, t - 1)
                h_sum.wait(pool, t)
                h_rstd.mark(nc.gpsimd.tensor_tensor(hr[0:r, :], hvar[0:r, :], C["mhalf"][0:r, 0:MH], ALU.pow))

            def weigh_h(t):
                r = rows(t)
                h_scaled.wait(pool, t)
                h_weighed.mark(nc.gpsimd.tensor_tensor(hq[0:r, :], h1[0:r, :], C["ml_norm"][0:r, :], ALU.mult))

            def period(t):
                keep_v(t)
                weigh_k(t)
                square_h(t)
                rstd_h(t)
                weigh_h(t)

            pool.wait_ge(state_zero, 1)
            tiles_loop(pool, period, 0, NT)
            period(samp)


def output(nc, ident, mhalf, ins, o_dram, x1_dram, h2_dram, conv_cols, load_ahead):
    with ExitStack() as ctx:
        k = Stage(nc, ctx, "out")
        w = Weight(k, "w", D)
        w.use(k, "w")
        norm_w = k.sb("norm_w", [P, D])
        o = k.sb("o", [P, 2, D])
        o_hi = k.sb("o_hi", [P, 2, D], F32R)
        o_lo = k.sb("o_lo", [P, 2, D], F32R)
        x1 = k.sb("x1", [P, 2, D])
        square = k.sb("square", [P, D])
        xss = k.sb("xss", [P, 1])
        xvar = k.sb("xvar", [P, 1])
        xr = k.sb("xr", [P, 1])
        hn = k.sb("hn", [P, D])
        conv_rows = nc.alloc_sbuf_tensor_at("out_conv_rows", [SB * (CW - 1) + CW + 1, FF], F32, offset=(nc.sbuf_base + 31) // 32 * 32)
        h_hi = k.sb("h_hi", [P, 2, D], F32R)
        h_lo = k.sb("h_lo", [P, 2, D], F32R)
        bank = k.banks()

        rows_in, rows_turned, rows_kept = k.sem("rows_in"), k.sem("rows_turned"), k.sem("rows_kept")
        norm_in = k.sem("norm_in")
        o_in, x_in = k.landed("o_in"), k.landed("x_in")
        o_turned = k.steps("o_turned", 2)
        o_rounded = k.steps("o_rounded", 2)
        o_split = k.steps("o_split", 2)
        proj = k.steps("proj", 2)
        added = k.steps("added", 2)
        x_square = k.steps("x_square")
        x_var = k.steps("x_var")
        x_rstd = k.steps("x_rstd")
        x_normed = k.steps("x_normed")
        h_turned = k.steps("h_turned", 2)
        h_rounded = k.steps("h_rounded", 2)
        h_split = k.steps("h_split", 2)
        x1_out, h_out = k.landed("x1_out"), k.landed("h_out", 2)

        samp = Tile(0, NT)

        def rows(t):
            return NS if t.c == NT else P

        def cut(a, r):
            return a.rearrange("p (c r) -> p c r", r=P)[:, :, 0:r]

        block = ctx.enter_context(nc.Block())

        @block.sync
        def _(sp):
            def load_o(t):
                o_turned.wait(sp, t - 2)
                r = rows(t)
                o_in.mark(sp.dma_start(o[0:r, t.p, :], o_dram[bass.ds(t.n * P, r), :]), t)

            def load_x(t):
                x1_out.wait(sp, t - 2)
                src = ins["x_sample"].rearrange("b t d -> (b t) d") if t.c == NT else ins["x_prompt"][0, bass.ds(t.n * P, P), :]
                x_in.mark(sp.dma_start(x1[0:rows(t), t.p, :], src), t)

            def store_x1(t):
                x_normed.wait(sp, t)
                r = rows(t)
                x1_out.mark(sp.dma_start(x1_dram[bass.ds(t.n, 1), 0:r].rearrange("a p n -> (a p) n"), x1[0:r, t.p, :]), t)

            def store_h(t):
                h_split.wait(sp, t)
                r = rows(t)
                for part, src in ((0, h_hi), (1, h_lo)):
                    h_out.mark(sp.dma_start(h2_dram[:, part, :, bass.ds(t.n * P, r)], cut(src[:, t.p, :].bitcast(F32), r)), t)

            load_o(Tile(0, 0))
            load_x(Tile(0, 0))
            w.load(sp, [ins["w_out"][0]])
            sp.dma_start(norm_w[:, :], ins["norm_ffn_w"][0:1, :].partition_broadcast(P)).then_inc(norm_in, 16)
            rows_of = conv_rows[:, :]
            sp.dma_start(rows_of[0:SB * (CW - 1), :], ins["cache_ffn_conv"][0].rearrange("b c f -> (b c) f")).then_inc(rows_in, 16)
            sp.dma_start(rows_of[SB * (CW - 1):SB * (CW - 1) + CW, :], ins["conv_w"][0]).then_inc(rows_in, 16)
            sp.dma_start(rows_of[SB * (CW - 1) + CW:SB * (CW - 1) + CW + 1, :], ins["conv_b"][0:1, :]).then_inc(rows_in, 16)
            load_o(Tile(0, 1))
            load_x(Tile(0, 1))

            def period(t):
                static = isinstance(t.i, int)
                if not (static and t.c < 1):
                    store_x1(t - 1)
                    if not (static and t.c + 1 > NT):
                        load_x(t + 1)
                if not (static and t.c + 2 > NT):
                    load_o(t + 2)
                if not (static and t.c < 2):
                    store_h(t - 2)
                if static and NT - 6 <= t.c < NT - 2:
                    h_out.wait(sp, Tile(0, NT // 2 - 2))
                    h_out.wait(sp, Tile(0, NT // 2 - 1))
                    load_ahead(sp, *divmod(t.c - (NT - 6), 2))

            tiles_loop(sp, period, 0, NT + 1, peel=NT - 6)
            store_x1(samp)
            store_h(samp - 1)
            store_h(samp)
            for t in (samp - 1, samp):
                x1_out.wait(sp, t)
                h_out.wait(sp, t)

        @block.tensor
        def _(pe):
            def turn(t, src, ready, turned, free, at):
                r = rows(t)
                ready.wait(pe, t)
                for b in range(2):
                    free.wait(pe, t - 1, b)
                    for c in range(4):
                        ins_ = nc.tensor.transpose(bank[at + b][:, c * P:c * P + r], src(t)[0:r, (b * 4 + c) * P:(b * 4 + c + 1) * P], ident[0:r, 0:r])
                    turned.mark(ins_)

            def turn_o(t):
                turn(t, lambda t: o[:, t.p, :], o_in, o_turned, o_split, 2)

            def turn_h(t):
                turn(t, lambda t: hn[:, :], x_normed, h_turned, h_split, 4)

            def project(t, g):
                r = rows(t)
                o_split.wait(pe, t)
                added.wait(pe, t - 1, g)
                for c in range(KC):
                    if isinstance(t.i, int) and t.c == 0 and g == 0:
                        pe.wait_ge(w.split, c + 1)
                    at = slice(c * P, c * P + r)
                    ins_ = mm3(nc, bank[g][0:r, :], o_hi[:, t.p, at], o_lo[:, t.p, at],
                               w.hi[:, c, g * 512:(g + 1) * 512], w.lo[:, c, g * 512:(g + 1) * 512], c == 0, c == KC - 1)
                proj.mark(ins_)

            turn_o(Tile(0, 0))

            def turn_rows():
                pe.wait_ge(rows_in, 48)
                n = SB * (CW - 1) + CW + 1
                for f in range(FC):
                    ins_ = nc.tensor.transpose(bank[6][:, f * n:(f + 1) * n], conv_rows[:, f * P:(f + 1) * P], ident[0:n, 0:n])
                ins_.then_inc(rows_turned, 1)

            def period(t):
                project(t, 0)
                if isinstance(t.i, int) and t.c == 0:
                    turn_rows()
                if not (isinstance(t.i, int) and t.c + 1 > NT):
                    turn_o(t + 1)
                project(t, 1)
                if not (isinstance(t.i, int) and t.c < 1):
                    turn_h(t - 1)

            tiles_loop(pe, period, 0, NT + 1)
            turn_h(samp)

        def round_(act, t, dst, turned, rounded, free, at):
            r = rows(t)
            free(t - 2)
            for b in range(2):
                turned.wait(act, t, b)
                rounded.mark(nc.scalar.activation(cut(dst[:, t.p, b * 512:(b + 1) * 512], r), cut(bank[at + b][:, :], r), ACT.Copy))

        def split_(dve, t, hi, lo, rounded, split, at):
            r = rows(t)
            for b in range(2):
                rounded.wait(dve, t, b)
                sl = slice(b * 512, (b + 1) * 512)
                split.mark(nc.vector.tensor_tensor(cut(lo[:, t.p, sl], r), cut(bank[at + b][:, :], r), cut(hi[:, t.p, sl], r).bitcast(F32), ALU.subtract))

        @block.scalar
        def _(act):
            def round_o(t):
                round_(act, t, o_hi, o_turned, o_rounded, lambda u: proj.wait(act, u), 2)

            def round_h(t):
                round_(act, t, h_hi, h_turned, h_rounded, lambda u: h_out.wait(act, u), 4)

            def square_x(t):
                r = rows(t)
                added.wait(act, t)
                x_var.wait(act, t - 1)
                x_square.wait(act, t - 1)
                x_square.mark(nc.scalar.activation(square[0:r, :], x1[0:r, t.p, :], ACT.Square, accum_out=xss[0:r, :]))

            round_o(Tile(0, 0))
            w.round(nc, act)

            def period(t):
                if not (isinstance(t.i, int) and t.c + 1 > NT):
                    round_o(t + 1)
                if not (isinstance(t.i, int) and t.c < 1):
                    round_h(t - 1)
                square_x(t)

            tiles_loop(act, period, 0, NT + 1)
            round_h(samp)

        @block.vector
        def _(dve):
            def split_o(t):
                split_(dve, t, o_hi, o_lo, o_rounded, o_split, 2)

            def split_h(t):
                split_(dve, t, h_hi, h_lo, h_rounded, h_split, 4)

            def add_x(t, g):
                r = rows(t)
                proj.wait(dve, t, g)
                if g == 0:
                    x_in.wait(dve, t)
                at = slice(g * 512, (g + 1) * 512)
                added.mark(nc.vector.tensor_tensor(x1[0:r, t.p, at], bank[g][0:r, :], x1[0:r, t.p, at], ALU.add))

            def norm_x(t):
                r = rows(t)
                x_square.wait(dve, t)
                x_rstd.wait(dve, t - 1)
                x_var.mark(nc.vector.tensor_scalar(xvar[0:r, :], xss[0:r, :], 1.0 / D, EPS, ALU.mult, ALU.add))
                x_rstd.wait(dve, t)
                h_turned.wait(dve, t - 1)
                x_normed.mark(nc.vector.scalar_tensor_tensor(hn[0:r, :], x1[0:r, t.p, :], xr[0:r, 0:1], norm_w[0:r, :],
                                                             ALU.mult, ALU.mult))

            split_o(Tile(0, 0))
            w.subtract(nc, dve)
            dve.wait_ge(norm_in, 16)

            def period(t):
                add_x(t, 0)
                if isinstance(t.i, int) and t.c == 0:
                    dve.wait_ge(rows_turned, 1)
                    nc.vector.tensor_copy(conv_cols[:, :], bank[6][:, 0:FC * (SB * (CW - 1) + CW + 1)]).then_inc(rows_kept, 1)
                if not (isinstance(t.i, int) and t.c + 1 > NT):
                    split_o(t + 1)
                add_x(t, 1)
                if not (isinstance(t.i, int) and t.c < 1):
                    split_h(t - 1)
                norm_x(t)

            tiles_loop(dve, period, 0, NT + 1)
            split_h(samp)

        @block.gpsimd
        def _(pool):
            def period(t):
                r = rows(t)
                x_normed.wait(pool, t - 1)
                x_var.wait(pool, t)
                x_rstd.mark(nc.gpsimd.tensor_tensor(xr[0:r, :], xvar[0:r, :], mhalf[0:r, 0:1], ALU.pow))

            tiles_loop(pool, period, 0, NT + 1)


def load_h2(sp, h2, h_in, h2_dram, G, b, part):
    off, n = G.blocks[b]
    sp.dma_start(h2[:, part, :, off:off + n].bitcast(F32),
                 h2_dram[:, part, :, G.base + off:G.base + off + n]).then_inc(h_in[G.index][b], 16)


class Group:

    def __init__(self, index, base, blocks, sample):
        self.index, self.base, self.blocks, self.sample = index, base, blocks, sample
        self.nb, self.B2 = len(blocks), 2 * len(blocks)
        self.TG = blocks[-1][0] + blocks[-1][1]
        self.ntile = (self.TG + P - 1) // P
        self.items = [(j, g) for j in range(self.ntile) for g in range(2)]
        self.NI = len(self.items)
        self.ring = 4 if self.NI % 4 == 0 else 3

    def round(self, i):
        return i + self.index * (FC // 2)

    def final(self, i):
        return self.sample and isinstance(i, int) and i == FC // 2 - 1


GROUPS = (Group(0, 0, [(0, 512), (512, 512)], False), Group(1, SEQ // 2, [(0, 384), (384, 384), (768, 320)], True))


def ffn(nc, ident, ins, outs, x1_dram, h2_dram, h2, h_in, conv_cols, halo, conv_out):
    NP = FC // 2
    CC = SB * (CW - 1) + CW + 1
    half = SEQ // 2
    groups = GROUPS
    TG = max(G.TG for G in groups)
    ntile = max(G.ntile for G in groups)
    with ExitStack() as ctx:
        k = Stage(nc, ctx, "ffn")
        acc = k.sb("acc", [P, ntile, D])
        act_hi = k.sb("act_hi", [P, 2, TG], F32R)
        act_lo = k.sb("act_lo", [P, 2, TG], F32R)
        raw = k.sb("raw", [P, TG])
        w_hi = k.sb("w_hi", [P, 2, 2, KC * P], F32R)
        w_lo = k.sb("w_lo", [P, 2, 2, KC * P], F32R)
        d_hi = k.sb("d_hi", [P, 2, D], F32R)
        d_lo = k.sb("d_lo", [P, 2, D], F32R)
        stage = k.sb("stage", [P, 2, D])
        gp = k.sb("gp", [P, half + CW - 1])
        gs = k.sb("gs", [P, SB, ST + CW - 1])
        t = k.sb("t", [P, 2, 512])
        cc = k.sb("cc", [P, 2, CC])
        bank = k.banks()

        acc_in, y_out = k.sem("acc_in"), k.sem("y_out")
        st_in = [k.sem("stage_in0"), k.sem("stage_in1")]
        w_rounded, w_split = k.sem("w_rounded"), k.sem("w_split")
        up = k.sem("up")
        down = k.sem("down")
        g_kept, t_made, silu = k.sem("g_kept"), k.sem("t_made"), k.sem("silu")
        taps, prod = k.sem("taps"), k.sem("prod")
        a_rounded, a_split = k.sem("a_rounded"), k.sem("a_split")
        added, cols_kept, kept_tail = k.sem("added"), k.sem("cols_kept"), k.sem("kept_tail")
        head_kept = k.sem("head_kept")
        rows_turned, rows_kept, rows_out = k.sem("rows_turned"), k.sem("rows_kept"), k.sem("rows_out")

        def at(sem, per):
            return lambda eng, G, i, s: wait(eng, sem, sum(NP * per(g) for g in groups[:G.index]) + per(G) * i + s + 1)

        w_up = at(up, lambda G: 2 * G.B2)
        w_down = at(down, lambda G: G.NI)
        w_g, w_t, w_silu, w_prod, w_aspl, w_arnd = (at(s, lambda G: G.B2) for s in (g_kept, t_made, silu, prod, a_split, a_rounded))
        w_taps = at(taps, lambda G: 2 * G.B2)
        w_added = at(added, lambda G: G.NI)
        w_cols = at(cols_kept, lambda G: 2)
        w_tail = at(kept_tail, lambda G: 2)

        PIECES = 6

        def pieces(i, last):
            out = [(0, "w", 1, 0), (1, "w", 1, 1)]
            if not last:
                out += [(2, "w", 0, 0), (3, "w", 0, 1)]
            n = len(out)
            return out + [(n, "d", 0, 0), (n + 1, "d", 1, 0)]

        def rounds(eng, step, first=0):
            for i in range(first, 2):
                step(i)
            with eng.Fori(2, NP - 1) as i:
                step(i)
            step(NP - 1)

        block = ctx.enter_context(nc.Block())

        @block.sync
        def _(sp):
            def store_y(G):
                for n, (j, g) in enumerate(G.items):
                    if g == 0:
                        continue
                    w_added(sp, G, NP - 1, n)
                    if j * P < half:
                        dst = outs["y_prompt"][0, G.base + j * P:G.base + (j + 1) * P, :]
                        sp.dma_start(dst, acc[:, j, :]).then_inc(y_out, 16)
                    else:
                        sp.dma_start(outs["y_sample"].rearrange("b t d -> (b t) d"), acc[0:NS, j, :]).then_inc(y_out, 16)

            def group(G):
                def piece(i, pos, kind, x, part):
                    n = PIECES * G.round(i) + pos + 2
                    wait(sp, w_split, n - 1)
                    if kind == "w":
                        chunk = 0 if x == 0 and isinstance(i, int) and i == NP - 1 else 2 * (i + (1 - x)) + x
                        src = ins["w_ffn_in"][0].rearrange("(c p) n -> p c n", p=P)[:, :, bass.ds(chunk * P + part * FF, P)]
                        dst = stage[:, pos % 2, :].rearrange("p (c n) -> p c n", c=KC)
                    else:
                        src = ins["w_down"][0][bass.ds((2 * i + x) * P, P), :]
                        dst = stage[:, pos % 2, :]
                    sp.dma_start(dst, src).then_inc(st_in[pos % 2], 16)

                def load_acc():
                    for j in range(G.ntile):
                        r = min(P, G.TG - j * P)
                        sp.dma_start(acc[0:r, j, :], x1_dram[G.base // P + j, 0:r, :]).then_inc(acc_in, 16)

                if G.index == 0:
                    piece(-1, 4, "w", 0, 0)
                    piece(-1, 5, "w", 0, 1)
                    load_acc()
                else:
                    w_up(sp, groups[0], NP - 1, 2 * groups[0].B2 - 1)
                    for b in range(G.nb):
                        for part in range(2):
                            load_h2(sp, h2, h_in, h2_dram, G, b, part)
                    store_y(groups[0])

                def step(i):
                    for p_ in pieces(i, G.final(i)):
                        piece(i, *p_)

                step(0)
                if G.index == 1:
                    sp.wait_ge(y_out, 16 * groups[0].ntile)
                    load_acc()
                rounds(sp, step, 1)
                if G.sample:
                    store_y(G)
                    for q in range(3):
                        sp.wait_ge(rows_kept, q + 1)
                        w_ = min(8, FC - 8 * q) * P
                        sl = slice(8 * q * P, 8 * q * P + w_)
                        sp.dma_start(outs["conv_prompt"][0, 0, :, sl], stage[0:CW - 1, q % 2, 0:w_]).then_inc(rows_out, 16)
                        sp.dma_start(outs["conv_sample"][0].rearrange("b c f -> (b c) f")[:, sl], stage[CW - 1:CC - 2, q % 2, 0:w_]).then_inc(rows_out, 16)
                        if q == 0:
                            sp.wait_ge(rows_out, 32)
                    sp.wait_ge(rows_out, 96)
                    sp.wait_ge(y_out, 16 * sum(g.ntile for g in groups))

            for G in groups:
                group(G)

        @block.tensor
        def _(pe):
            def group(G):
                def gate_up(i, x):
                    for b, (off, n) in enumerate(G.blocks):
                        kk = x * G.nb + b
                        if isinstance(i, int) and i == 0 and x == 0:
                            pe.wait_ge(h_in[G.index][b], 16 * 2)
                        for part in range(2):
                            if part == 0:
                                w_t(pe, G, i - (kk < 2), (kk - 2) % G.B2)
                            else:
                                w_prod(pe, G, i - (kk < 2), (kk - 2) % G.B2)
                            out = bank[2 * part + kk % 2][:, 0:n]
                            for c in range(KC):
                                sl = slice(c * P, (c + 1) * P)
                                ins_ = mm3(nc, out, w_hi[:, x, part, sl], w_lo[:, x, part, sl],
                                           h2[:, 0, c, off:off + n], h2[:, 1, c, off:off + n], c == 0, c == KC - 1)
                            ins_.then_inc(up, 1)

                def project_down(i):
                    w_aspl(pe, G, i, G.B2 - 1)
                    for n, (j, g) in enumerate(G.items):
                        r = min(P, G.TG - j * P)
                        bk = bank[4 + n % G.ring]
                        w_added(pe, G, i - (n < G.ring), (n - G.ring) % G.NI)
                        for x in range(2):
                            cs = slice(g * 512, (g + 1) * 512)
                            ins_ = mm3(nc, bk[0:r, :], act_hi[:, x, j * P:j * P + r], act_lo[:, x, j * P:j * P + r],
                                       d_hi[:, x, cs], d_lo[:, x, cs], x == 0, x == 1)
                        ins_.then_inc(down, 1)

                def step(i):
                    wait(pe, w_split, 2 if isinstance(i, int) and G.round(i) == 0 else PIECES * G.round(i))
                    gate_up(i, 0)
                    if not (isinstance(i, int) and i == 0):
                        wait(pe, w_split, PIECES * G.round(i) + 2)
                        project_down(i - 1)
                    wait(pe, w_split, PIECES * G.round(i) + 4)
                    gate_up(i, 1)

                rounds(pe, step)
                wait(pe, w_split, PIECES * G.round(NP) + (0 if G.sample else 2))
                project_down(NP - 1)
                if G.sample:
                    w_tail(pe, G, NP - 1, 1)
                    for f in range(FC):
                        q = f // 8
                        bk = bank[(f % 8) // 4]
                        if f % 8 == 0:
                            wait(pe, rows_kept, q)
                        ins_ = nc.tensor.transpose(bk[0:CC - 2, (f % 4) * P:(f % 4 + 1) * P], conv_out[:, f * (CC - 2):(f + 1) * (CC - 2)], ident[:, :])
                        if f % 8 == 7 or f == FC - 1:
                            ins_.then_inc(rows_turned, 1)

            for G in groups:
                group(G)

        @block.scalar
        def _(act):
            def group(G):
                def round_piece(i, pos, kind, x, part):
                    n = PIECES * G.round(i) + pos + 2
                    act.wait_ge(st_in[pos % 2], 16 * (3 * G.round(i) + 1 + pos // 2 + 1))
                    if kind == "w" and x == 1:
                        w_up(act, G, i - 1, 2 * G.B2 - 1)
                    elif kind == "w":
                        w_up(act, G, i, G.B2 - 1)
                    else:
                        w_down(act, G, i - 1, G.NI - 1)
                    dst = w_hi[:, x, part, :] if kind == "w" else d_hi[:, x, :]
                    nc.scalar.activation(dst, stage[:, pos % 2, :], ACT.Copy).then_inc(w_rounded, 1)

                def post(i, x, b):
                    off, n = G.blocks[b]
                    kk = x * G.nb + b
                    w_up(act, G, i, 2 * kk)
                    w_cols(act, G, i, x)
                    if b == 0:
                        w_taps(act, G, i - (x == 0), (2 * (kk - 1) + 1) % (2 * G.B2))
                        w_tail(act, G, i - (x == 0), (x - 1) % 2)
                    src = bank[kk % 2]
                    pn = min(n, half - off)
                    ins_ = nc.scalar.activation(gp[:, CW - 1 + off:CW - 1 + off + pn], src[:, 0:pn], ACT.Copy)
                    if pn < n:
                        ins_ = nc.scalar.activation(gs[:, :, CW - 1:], src[:, pn:n].rearrange("p (b t) -> p b t", t=ST), ACT.Copy)
                    ins_.then_inc(g_kept, 1)
                    w_prod(act, G, i - (kk < 2), (kk - 2) % G.B2)
                    w_aspl_if(act, i, kk)
                    nc.scalar.activation(t[:, kk % 2, 0:n], src[:, 0:n], ACT.Identity, scale=cc[:, x, CC - 2:CC - 1],
                                         bias=cc[:, x, CC - 1:CC]).then_inc(t_made, 1)
                    w_taps(act, G, i, 2 * kk + 1)
                    nc.scalar.activation(t[:, kk % 2, 0:n], t[:, kk % 2, 0:n], ACT.Silu).then_inc(silu, 1)

                def w_aspl_if(eng, i, kk):
                    prev, step = i - (kk < 2), (kk - 2) % G.B2
                    if step >= G.nb:
                        w_aspl(eng, G, prev, step)

                def round_a(i, x, b):
                    off, n = G.blocks[b]
                    w_prod(act, G, i, x * G.nb + b)
                    w_down(act, G, i - 1, G.NI - 1)
                    src = raw[:, off:off + n] if x == 0 else t[:, (G.nb + b) % 2, 0:n]
                    nc.scalar.activation(act_hi[:, x, off:off + n], src, ACT.Copy).then_inc(a_rounded, 1)

                def first(pos, part):
                    act.wait_ge(st_in[pos % 2], 16)
                    nc.scalar.activation(w_hi[:, 0, part, :], stage[:, pos % 2, :], ACT.Copy).then_inc(w_rounded, 1)

                if G.index == 0:
                    first(0, 0)
                    first(1, 1)

                def step(i):
                    ps = pieces(i, G.final(i))
                    for b in range(G.nb):
                        post(i, 0, b)
                        if b < 2:
                            round_piece(i, *ps[b])
                    if len(ps) == PIECES:
                        round_piece(i, *ps[2])
                        round_piece(i, *ps[3])
                    for b in range(G.nb):
                        round_a(i, 0, b)
                    round_piece(i, *ps[-2])
                    post(i, 1, 0)
                    round_a(i, 1, 0)
                    round_piece(i, *ps[-1])
                    for b in range(1, G.nb):
                        post(i, 1, b)
                        round_a(i, 1, b)

                rounds(act, step)

            for G in groups:
                group(G)

        @block.vector
        def _(dve):
            def group(G):
                def split_piece(i, pos, kind, x, part):
                    n = PIECES * G.round(i) + pos + 2
                    dve.wait_ge(w_rounded, n + 1)
                    hi, lo = (w_hi[:, x, part, :], w_lo[:, x, part, :]) if kind == "w" else (d_hi[:, x, :], d_lo[:, x, :])
                    nc.vector.tensor_tensor(lo, stage[:, pos % 2, :], hi.bitcast(F32), ALU.subtract).then_inc(w_split, 1)

                def columns(i, x):
                    w_t(dve, G, i - 1, x * G.nb + G.nb - 1)
                    w_taps(dve, G, i - 1, 2 * (x * G.nb + G.nb - 1) + 1)
                    nc.vector.tensor_copy(cc[:, x, :], conv_cols[:, bass.ds((2 * i + x) * CC, CC)]).then_inc(cols_kept, 1)

                def heads(i, x):
                    if G.sample:
                        w_cols(dve, G, i, x)
                        nc.vector.tensor_copy(gp[:, 0:CW - 1], halo[:, bass.ds((2 * i + x) * (CW - 1), CW - 1)])
                        ins_ = nc.vector.tensor_copy(gs[:, :, 0:CW - 1], cc[:, x, 0:SB * (CW - 1)].rearrange("p (b c) -> p b c", b=SB))
                        ins_.then_inc(head_kept, 1)
                        wait(dve, head_kept, 2 * i + x + 2)

                def tails(i, x):
                    w_g(dve, G, i, x * G.nb + G.nb - 1)
                    f = 2 * i + x
                    if G.sample:
                        nc.vector.tensor_copy(conv_out[:, bass.ds(f * (CC - 2), CW - 1)], gp[:, half:half + CW - 1])
                        nc.vector.tensor_copy(conv_out[:, bass.ds(f * (CC - 2) + CW - 1, SB * (CW - 1))].rearrange("p (b c) -> p b c", b=SB),
                                              gs[:, :, ST:ST + CW - 1]).then_inc(kept_tail, 1)
                    else:
                        nc.vector.tensor_copy(halo[:, bass.ds(f * (CW - 1), CW - 1)], gp[:, half:half + CW - 1]).then_inc(kept_tail, 1)

                def post(i, x, b):
                    off, n = G.blocks[b]
                    kk = x * G.nb + b
                    if b == 0:
                        heads(i, x)
                    pn = min(n, half - off)
                    tb = t[:, kk % 2, 0:n]
                    w_t(dve, G, i, kk)
                    for s in (1, 2):
                        col = cc[:, x, CC - 2 - s:CC - 1 - s]
                        ins_ = nc.vector.scalar_tensor_tensor(tb[:, 0:pn], gp[:, CW - 1 + off - s:CW - 1 + off - s + pn], col, tb[:, 0:pn], ALU.mult, ALU.add)
                        if pn < n:
                            ts = tb[:, pn:n].rearrange("p (b t) -> p b t", t=ST)
                            ins_ = nc.vector.scalar_tensor_tensor(ts, gs[:, :, CW - 1 - s:CW - 1 - s + ST], col, ts, ALU.mult, ALU.add)
                        ins_.then_inc(taps, 1)
                        w_taps(dve, G, i, 2 * kk + s - 1)
                    if b == G.nb - 1:
                        tails(i, x)
                    w_silu(dve, G, i, kk)
                    w_up(dve, G, i, 2 * kk + 1)
                    dst = raw[:, off:off + n] if x == 0 else tb
                    nc.vector.tensor_tensor(dst, tb, bank[2 + kk % 2][:, 0:n], ALU.mult).then_inc(prod, 1)

                def split_a(i, x, b):
                    off, n = G.blocks[b]
                    w_arnd(dve, G, i, x * G.nb + b)
                    src = raw[:, off:off + n] if x == 0 else t[:, (G.nb + b) % 2, 0:n]
                    nc.vector.tensor_tensor(act_lo[:, x, off:off + n], src, act_hi[:, x, off:off + n].bitcast(F32), ALU.subtract).then_inc(a_split, 1)

                def add(i, n):
                    j, g = G.items[n]
                    r = min(P, G.TG - j * P)
                    if n == 0 and isinstance(i, int) and i == 0:
                        dve.wait_ge(acc_in, 16 * sum(g.ntile for g in groups[:G.index + 1]))
                    w_down(dve, G, i, n)
                    sl = acc[0:r, j, g * 512:(g + 1) * 512]
                    nc.vector.tensor_tensor(sl, bank[4 + n % G.ring][0:r, :], sl, ALU.add).then_inc(added, 1)

                if not G.sample:
                    nc.vector.memset(gp[:, 0:CW - 1], 0.0).then_inc(head_kept, 1)
                    dve.wait_ge(head_kept, 1)

                def first(pos, part):
                    dve.wait_ge(w_rounded, pos + 1)
                    nc.vector.tensor_tensor(w_lo[:, 0, part, :], stage[:, pos % 2, :], w_hi[:, 0, part, :].bitcast(F32), ALU.subtract).then_inc(w_split, 1)

                if G.index == 0:
                    first(0, 0)
                    first(1, 1)
                else:
                    w_tail(dve, groups[0], NP - 1, 1)

                def step(i):
                    ps = pieces(i, G.final(i))
                    columns(i, 0)
                    columns(i, 1)
                    for b in range(G.nb):
                        post(i, 0, b)
                        if b < 2:
                            split_piece(i, *ps[b])
                    if not (isinstance(i, int) and i == 0):
                        for n in range(G.NI):
                            if n in (6, 12) and len(ps) == PIECES:
                                split_piece(i, *ps[n // 6 + 1])
                            add(i - 1, n)
                    elif len(ps) == PIECES:
                        split_piece(i, *ps[2])
                        split_piece(i, *ps[3])
                    for b in range(G.nb):
                        split_a(i, 0, b)
                    split_piece(i, *ps[-2])
                    post(i, 1, 0)
                    split_a(i, 1, 0)
                    split_piece(i, *ps[-1])
                    for b in range(1, G.nb):
                        post(i, 1, b)
                        split_a(i, 1, b)

                rounds(dve, step)
                for n in range(G.NI):
                    add(NP - 1, n)
                if G.sample:
                    for q in range(3):
                        dve.wait_ge(rows_turned, q + 1)
                        if q == 2:
                            dve.wait_ge(rows_out, 32)
                        left = min(8, FC - 8 * q) * P
                        for bk in range((left + 511) // 512):
                            w_ = min(512, left - bk * 512)
                            ins_ = nc.vector.tensor_copy(stage[0:CC - 2, q % 2, bk * 512:bk * 512 + w_], bank[bk][0:CC - 2, 0:w_])
                        ins_.then_inc(rows_kept, 1)

            for G in groups:
                group(G)


def constant_buffers(nc, ctx):
    def sb(name, shape):
        return ctx.enter_context(nc.sbuf_tensor(name, shape, F32))

    names = {
        "mask": [P, 4 * P], "cap": [P, P], "cap64": [NS, NS], "sel_head": [MH, MH * P], "sel_t": [ST, P],
        "sel_j": [GQ, P], "mask_s8": [ST, WIN + ST], "blk": [NS, SB], "ones": [P, P],
        "norm_mix": [P, D], "ml_norm": [P, MLV], "q_norm": [P, HD], "k_norm": [P, HD],
        "sinks": [P, HQ], "bias_i": [MH, 1], "bias_f": [MH, 1], "sink_rows": [GQ, HKV],
    }
    return {n: sb(n, shape) for n, shape in names.items()}


def trunk_step(nc, ins, outs, h_dram, o_dram, x1_dram, h2_dram):
    rows = SB * (CW - 1)
    with ExitStack() as outer:
        def kept(name, shape):
            return outer.enter_context(nc.sbuf_tensor(name, shape, F32))

        ident = kept("ident", [P, P])
        mhalf = kept("mhalf", [P, HQ + HKV])
        with ExitStack() as inner:
            C = constant_buffers(nc, inner)
            C["ident"], C["mhalf"] = ident, mhalf
            ahead = Stage(nc, inner, "ahead")
            ml_w = Weight(ahead, "ml_w", ML_W)
            w_in = ins["w_in"][0]

            def load_ml_w(sp):
                ml_w.load(sp, [w_in[:, IN_W - 2 * MH:IN_W], w_in[:, ATT_W:IN_W - 2 * MH]])

            with ExitStack() as first_ctx:
                att_w = Weight(Stage(nc, first_ctx, "first"), "att_w", ATT_W)
                constants(nc, C, ins, lambda sp: att_w.load(sp, [ins["w_in"][0][:, 0:ATT_W]]))
                attention(nc, C, ins, outs, h_dram, o_dram, att_w, load_ml_w)
            mlstm(nc, C, ins, outs, h_dram, o_dram, ml_w)
        conv_cols = kept("conv_cols", [P, FC * (rows + CW + 1)])
        halo = kept("halo", [P, FC * (CW - 1)])
        conv_out = kept("conv_out", [P, FC * (CW - 1 + rows)])
        late = Stage(nc, outer, "late")
        h2 = late.sb("h2", [P, 2, KC, max(G.TG for G in GROUPS)], F32R)
        h_in = [[late.sem(f"h2_in{G.index}{b}") for b in range(G.nb)] for G in GROUPS]
        output(nc, ident, mhalf, ins, o_dram, x1_dram, h2_dram, conv_cols,
               lambda sp, b, part: load_h2(sp, h2, h_in, h2_dram, GROUPS[0], b, part))
        ffn(nc, ident, ins, outs, x1_dram, h2_dram, h2, h_in, conv_cols, halo, conv_out)


_INS = ["x_prompt", "x_sample", "cache_attn_k", "cache_attn_v", "state_mlstm_C", "state_mlstm_n", "state_mlstm_m",
        "cache_ffn_conv", "norm_mix_w", "w_in", "b_gates", "q_norm_w", "k_norm_w", "sinks", "ml_norm_w", "w_out",
        "norm_ffn_w", "w_ffn_in", "conv_w", "conv_b", "w_down"]
_OUTS = [("y_prompt", (1, SEQ, D)), ("y_sample", (SB, ST, D)),
         ("k_prompt", (1, 1, WIN, HKV, HD)), ("v_prompt", (1, 1, WIN, HKV, HD)),
         ("C_prompt", (1, 1, MH, MV, MQK)), ("n_prompt", (1, 1, MH, MQK)), ("m_prompt", (1, 1, MH)),
         ("conv_prompt", (1, 1, CW - 1, FF)),
         ("k_sample", (1, SB, WIN, HKV, HD)), ("v_sample", (1, SB, WIN, HKV, HD)),
         ("C_sample", (1, SB, MH, MV, MQK)), ("n_sample", (1, SB, MH, MQK)), ("m_sample", (1, SB, MH)),
         ("conv_sample", (1, SB, CW - 1, FF))]


def kernel(**inputs):
    import numpy as _np
    import concourse.bacc as _bacc
    from concourse import mybir as _mybir
    from concourse.bass_utils import run_bass_kernel_spmd as _run

    nc = _bacc.Bacc("TRN2", target_bir_lowering=False, num_devices=1)
    arrays, args, results = {}, [], []
    for name in _INS:
        a = _np.ascontiguousarray(inputs[name])
        arrays[f"in_{name}_dram"] = a
        args.append(nc.dram_tensor(f"in_{name}_dram", a.shape, _mybir.dt.from_np(a.dtype), kind="ExternalInput").ap())
    for name, shape in _OUTS:
        results.append(nc.dram_tensor(f"out_{name}_dram", shape, F32, kind="ExternalOutput").ap())
    h_dram = nc.dram_tensor("h_parts", (NT + 1, P, 2, D), F32, kind="Internal").ap()
    o_dram = nc.dram_tensor("mixed", (SEQ + NS, D), F32, kind="Internal").ap()
    x1_dram = nc.dram_tensor("x1", (NT + 1, P, D), F32, kind="Internal").ap()
    h2_dram = nc.dram_tensor("h2_parts", (P, 2, KC, SEQ + NS), F32, kind="Internal").ap()
    trunk_step(nc, dict(zip(_INS, args)), {n: r for (n, _), r in zip(_OUTS, results)}, h_dram, o_dram, x1_dram, h2_dram)
    r = _run(nc, [arrays], core_ids=[0])
    return tuple(r.results[0][f"out_{name}_dram"] for name, _ in _OUTS)
```
